# Optimizing a Trainium2 kernel written in Bass

```python
import jax, jax.numpy as jnp
from jax import lax
import numpy as np
import math

D_MODEL = 1024
BATCH = 1
SEQ = 256
DEPTH = 1

POOL_GROUPS = 4
POOL_WINDOWS = (2, 4, 8, 16)
POOL_GROUP_W = 128
POOL_W = POOL_GROUPS * POOL_GROUP_W
POOL_OUT_GROUP_W = D_MODEL // POOL_GROUPS
ATTN_HEADS = 16
HEAD_DIM = 64
ATTN_W = ATTN_HEADS * HEAD_DIM
Q_BLOCK = 128
N_BRANCH = 2
IN_W = POOL_W + 3 * ATTN_W + ATTN_HEADS + N_BRANCH * D_MODEL
PEER_HEADS = 8
N_KEYS = 128
N_EXPERTS = N_KEYS * N_KEYS
PEER_HALF = 128
PEER_KEY_DIM = 2 * PEER_HALF
PEER_TOPK = 16
TOK_CHUNK = 128
N_MOD = 6
EPS = 1e-6
NEG_INF = -1e30


def rmsnorm(x, g):
    xf = x.astype(jnp.float32)
    y = xf * lax.rsqrt(jnp.mean(xf * xf, axis=-1, keepdims=True) + EPS)
    return (y * g.astype(jnp.float32)).astype(x.dtype)

def modulate(h, shift, scale):
    return h * (1.0 + scale[:, None, :]) + shift[:, None, :]

def causal_pool_mixer(u, w_pool, pool_scale):
    B, S, _ = u.shape
    ug = u.reshape(B, S, POOL_GROUPS, POOL_GROUP_W)
    cs = jnp.cumsum(ug.astype(jnp.float32), axis=1)
    pos = jnp.arange(S)
    means = []
    for g, w in enumerate(POOL_WINDOWS):
        csg = cs[:, :, g]
        lag = jnp.pad(csg, ((0, 0), (w, 0), (0, 0)))[:, :S]
        cnt = jnp.minimum(pos + 1, w).astype(jnp.float32)[None, :, None]
        means.append((csg - lag) / cnt)
    pooled = jnp.stack(means, axis=2).astype(u.dtype) - ug
    y = jnp.einsum('bsgc,gcd->bsgd', pooled, w_pool).reshape(B, S, D_MODEL)
    return y * pool_scale

def forgetting_attention(q, k, v, log_f):
    B, S, H, Dh = q.shape
    F = jnp.transpose(jnp.cumsum(log_f.astype(jnp.float32), axis=1), (0, 2, 1))
    scale = Dh ** -0.5
    outs = []
    for i in range(S // Q_BLOCK):
        q0 = i * Q_BLOCK
        L = q0 + Q_BLOCK
        s = jnp.einsum('bqhd,bkhd->bhqk', q[:, q0:L], k[:, :L],
                       preferred_element_type=jnp.float32) * scale
        s = s + F[:, :, q0:L, None] - F[:, :, None, :L]
        qpos = q0 + jnp.arange(Q_BLOCK)
        kpos = jnp.arange(L)
        s = jnp.where(kpos[None, :] <= qpos[:, None], s, NEG_INF)
        p = jax.nn.softmax(s, axis=-1).astype(v.dtype)
        outs.append(jnp.einsum('bhqk,bkhd->bqhd', p, v[:, :L]))
    return jnp.concatenate(outs, axis=1).reshape(B, S, H * Dh)

def peer_ffn(h, w_query, sub_keys, expert_u, expert_v):
    B, S, D = h.shape
    q = jnp.einsum('bsd,dk->bsk', h, w_query).reshape(B, S, PEER_HEADS, 2, PEER_HALF)
    sc = jnp.einsum('bshpc,hpnc->bshpn', q, sub_keys,
                    preferred_element_type=jnp.float32)
    s1, i1 = lax.top_k(sc[..., 0, :], PEER_TOPK)
    s2, i2 = lax.top_k(sc[..., 1, :], PEER_TOPK)
    cand_s = (s1[..., :, None] + s2[..., None, :]).reshape(B, S, PEER_HEADS, PEER_TOPK * PEER_TOPK)
    cand_i = (i1[..., :, None] * N_KEYS + i2[..., None, :]).reshape(B, S, PEER_HEADS, PEER_TOPK * PEER_TOPK)
    top_s, sel = lax.top_k(cand_s, PEER_TOPK)
    idx = jnp.take_along_axis(cand_i, sel, axis=-1)
    gates = jax.nn.softmax(top_s, axis=-1).astype(h.dtype)
    T = B * S
    n_chunks = T // TOK_CHUNK
    hc = h.reshape(n_chunks, TOK_CHUNK, D)
    ic = idx.reshape(n_chunks, TOK_CHUNK, PEER_HEADS, PEER_TOPK)
    gc = gates.reshape(n_chunks, TOK_CHUNK, PEER_HEADS, PEER_TOPK)

    def chunk(args):
        xc, ec, wc = args
        u = expert_u[ec]
        a = jax.nn.gelu(jnp.einsum('cd,chkd->chk', xc, u), approximate=False) * wc
        return jnp.einsum('chk,chkd->cd', a, expert_v[ec])

    out = lax.map(chunk, (hc, ic, gc))
    return out.reshape(B, S, D)

def first_inputs(seed: int = 0) -> dict:
    key = jax.random.key(seed)
    ks = jax.random.split(key, 20)
    nrm = jax.random.normal
    d = D_MODEL
    x = nrm(ks[0], (BATCH, SEQ, d), jnp.float32)
    c = nrm(ks[1], (BATCH, d), jnp.float32)
    w_mod = nrm(ks[2], (DEPTH, d, N_MOD * d), jnp.float32) * (0.5 * d ** -0.5)
    b_mod = nrm(ks[3], (DEPTH, N_MOD * d), jnp.float32) * 0.02
    norm1_g = 1.0 + 0.02 * nrm(ks[4], (DEPTH, d), jnp.float32)
    w_in = nrm(ks[5], (DEPTH, d, IN_W), jnp.float32) * d ** -0.5
    b_f = jax.random.uniform(ks[6], (DEPTH, ATTN_HEADS), jnp.float32, 1.0, 4.0)
    w_pool = nrm(ks[7], (DEPTH, POOL_GROUPS, POOL_GROUP_W, POOL_OUT_GROUP_W), jnp.float32) * POOL_GROUP_W ** -0.5
    pool_scale = 1.0 + 0.02 * nrm(ks[8], (DEPTH, d), jnp.float32)
    w_out = nrm(ks[9], (DEPTH, d, d), jnp.float32) * d ** -0.5
    norm2_g = 1.0 + 0.02 * nrm(ks[10], (DEPTH, d), jnp.float32)
    peer_w_query = nrm(ks[11], (DEPTH, d, PEER_HEADS * PEER_KEY_DIM), jnp.float32) * d ** -0.5
    peer_sub_keys = nrm(ks[12], (DEPTH, PEER_HEADS, 2, N_KEYS, PEER_HALF), jnp.float32) * PEER_HALF ** -0.5
    peer_u = nrm(ks[13], (DEPTH, N_EXPERTS, d), jnp.float32) * d ** -0.5
    peer_v = nrm(ks[14], (DEPTH, N_EXPERTS, d), jnp.float32) * PEER_HEADS ** -0.5
    final_g = 1.0 + 0.02 * nrm(ks[15], (d,), jnp.float32)
    return {"x": x, "c": c, "w_mod": w_mod, "b_mod": b_mod, "norm1_g": norm1_g,
            "w_in": w_in, "b_f": b_f, "w_pool": w_pool, "pool_scale": pool_scale,
            "w_out": w_out, "norm2_g": norm2_g, "peer_w_query": peer_w_query,
            "peer_sub_keys": peer_sub_keys, "peer_u": peer_u, "peer_v": peer_v,
            "final_g": final_g}

def first_block(x, c, w_mod, b_mod, norm1_g, w_in, b_f, w_pool, pool_scale, w_out,
              norm2_g, peer_w_query, peer_sub_keys, peer_u, peer_v, final_g):
    B, S, D = x.shape
    for l in range(DEPTH):
        mod = jnp.einsum('bd,de->be', c, w_mod[l]) + b_mod[l]
        sh1, sc1, gt1, sh2, sc2, gt2 = jnp.split(mod, N_MOD, axis=-1)

        h = modulate(rmsnorm(x, norm1_g[l]), sh1, sc1)
        z = jnp.einsum('bsd,de->bse', h, w_in[l])
        o = 0
        u_pool = z[..., o:o + POOL_W]; o += POOL_W
        q = z[..., o:o + ATTN_W].reshape(B, S, ATTN_HEADS, HEAD_DIM); o += ATTN_W
        k = z[..., o:o + ATTN_W].reshape(B, S, ATTN_HEADS, HEAD_DIM); o += ATTN_W
        v = z[..., o:o + ATTN_W].reshape(B, S, ATTN_HEADS, HEAD_DIM); o += ATTN_W
        f_logit = z[..., o:o + ATTN_HEADS]; o += ATTN_HEADS
        g_a = jax.nn.sigmoid(z[..., o:o + D]); o += D
        g_b = jax.nn.sigmoid(z[..., o:o + D])

        y_a = causal_pool_mixer(u_pool, w_pool[l], pool_scale[l])
        log_f = jax.nn.log_sigmoid((f_logit + b_f[l]).astype(jnp.float32))
        y_b = forgetting_attention(q, k, v, log_f)
        y = g_a * y_a + g_b * y_b
        x = x + gt1[:, None, :] * jnp.einsum('bsd,de->bse', y, w_out[l])

        h2 = modulate(rmsnorm(x, norm2_g[l]), sh2, sc2)
        x = x + gt2[:, None, :] * peer_ffn(h2, peer_w_query[l], peer_sub_keys[l], peer_u[l], peer_v[l])
    return rmsnorm(x, final_g)


DEPTH_2 = 2

N_A_LAYERS = DEPTH_2 // 2
N_B_LAYERS = DEPTH_2 - N_A_LAYERS
D_FF = 2816
RWKV_HEAD = 64
RWKV_HEADS = D_MODEL // RWKV_HEAD
LORA_DECAY = 64
LORA_AAA = 64
LORA_GATE = 160
RWKV_LN_EPS = 64e-5
N_SHIFT_MIX = 6
DIFF_HEAD = 64
DIFF_HEADS = D_MODEL // (2 * DIFF_HEAD)
DIFF_V_HEAD = 2 * DIFF_HEAD
NORM_EPS = 1e-6
SUBLN_EPS = 1e-5


def rms_norm(x, g, eps=NORM_EPS):
    xf = x.astype(jnp.float32)
    y = xf * lax.rsqrt(jnp.mean(xf * xf, axis=-1, keepdims=True) + eps)
    return (y * g.astype(jnp.float32)).astype(x.dtype)

def swiglu(h, w_in, w_out):
    gate, up = jnp.split(h @ w_in, 2, axis=-1)
    return (jax.nn.silu(gate) * up) @ w_out

def lambda_init(layer_idx):
    return 0.8 - 0.6 * math.exp(-0.3 * layer_idx)

def alibi_slopes(n_heads):
    return 2.0 ** (-8.0 * jnp.arange(1, n_heads + 1, dtype=jnp.float32) / n_heads)

def wkv7_scan(r, decay, k, v, a, b):
    B, T, H, N = r.shape

    def step(S, inp):
        r_t, w_t, k_t, v_t, a_t, b_t = inp
        sa = jnp.einsum('bhij,bhj->bhi', S, a_t)
        S = S * w_t[:, :, None, :] + sa[..., None] * b_t[:, :, None, :] + v_t[..., None] * k_t[:, :, None, :]
        return S, jnp.einsum('bhij,bhj->bhi', S, r_t)

    xs = [jnp.moveaxis(t.astype(jnp.float32), 1, 0) for t in (r, decay, k, v, a, b)]
    S0 = jnp.zeros((B, H, N, N), jnp.float32)
    _, y = lax.scan(step, S0, xs)
    return jnp.moveaxis(y, 0, 1)

def rwkv7_time_mix(h, mu, w_rkv, w0, w1, w2, a0, a1, a2, g1, g2, k_k, k_a, r_k, ln_g, ln_b, w_o):
    B, T, C = h.shape
    H, N = RWKV_HEADS, RWKV_HEAD
    h_prev = jnp.pad(h, ((0, 0), (1, 0), (0, 0)))[:, :-1]
    dx = h_prev - h
    r, k, v = jnp.einsum('sbtc,scd->sbtd', h[None] + dx[None] * mu[:3, None, None, :], w_rkv)
    xw = h + dx * mu[3]
    xa = h + dx * mu[4]
    xg = h + dx * mu[5]
    w_log = -jax.nn.softplus(-(w0 + jnp.tanh(xw @ w1) @ w2)) - 0.5
    decay = jnp.exp(-jnp.exp(w_log.astype(jnp.float32)))
    a = jax.nn.sigmoid(a0 + (xa @ a1) @ a2)
    g = jax.nn.sigmoid(xg @ g1) @ g2
    kk = (k * k_k).reshape(B, T, H, N).astype(jnp.float32)
    kk = kk * lax.rsqrt(jnp.maximum(jnp.sum(kk * kk, axis=-1, keepdims=True), 1e-24))
    k = k * (1 + (a - 1) * k_a)
    heads = lambda t: t.reshape(B, T, H, N)
    a_h = heads(a).astype(jnp.float32)
    y = wkv7_scan(heads(r), heads(decay), heads(k), heads(v), -kk, kk * a_h)
    mean = jnp.mean(y, axis=-1, keepdims=True)
    var = jnp.mean(jnp.square(y - mean), axis=-1, keepdims=True)
    y = ((y - mean) * lax.rsqrt(var + RWKV_LN_EPS)).reshape(B, T, C) * ln_g + ln_b
    bonus = jnp.sum(heads(r).astype(jnp.float32) * heads(k).astype(jnp.float32) * r_k, axis=-1, keepdims=True)
    y = y + (bonus * heads(v).astype(jnp.float32)).reshape(B, T, C)
    return (y.astype(h.dtype) * g) @ w_o

def shared_kv(x, kv_norm, w_kv, k_norm):
    B, T, _ = x.shape
    kv = rms_norm(x, kv_norm) @ w_kv
    k = rms_norm(kv[..., :D_MODEL].reshape(B, T, DIFF_HEADS, 2, DIFF_HEAD), k_norm).transpose(0, 2, 3, 1, 4)
    v = kv[..., D_MODEL:].reshape(B, T, DIFF_HEADS, DIFF_V_HEAD).transpose(0, 2, 1, 3)
    return k, v

def diff_attention(h, k_sh, v_sh, w_q, q_norm, lam, subln, w_o, lam_init):
    B, T, _ = h.shape
    H, d = DIFF_HEADS, DIFF_HEAD
    n_blk = T // Q_BLOCK
    q = rms_norm((h @ w_q).reshape(B, T, H, 2, d), q_norm)
    q = q.reshape(B, n_blk, Q_BLOCK, H, 2, d).transpose(1, 0, 3, 4, 2, 5)
    lamf = lam.astype(jnp.float32)
    lam_full = jnp.exp(jnp.sum(lamf[0] * lamf[1])) - jnp.exp(jnp.sum(lamf[2] * lamf[3])) + lam_init
    slopes = alibi_slopes(H)
    k_pos = jnp.arange(T, dtype=jnp.int32)
    scale = d ** -0.5

    def block(args):
        qb, start = args
        s = jnp.einsum('bhcqd,bhckd->bhcqk', qb, k_sh).astype(jnp.float32) * scale
        dist = (start + jnp.arange(Q_BLOCK, dtype=jnp.int32))[:, None] - k_pos[None, :]
        bias = -slopes[:, None, None] * dist.astype(jnp.float32)
        s = jnp.where(dist >= 0, s + bias[None, :, None], -jnp.inf)
        p = jax.nn.softmax(s, axis=-1)
        attn = p[:, :, 0] - lam_full * p[:, :, 1]
        return jnp.einsum('bhqk,bhkd->bhqd', attn.astype(v_sh.dtype), v_sh)

    starts = jnp.arange(n_blk, dtype=jnp.int32) * Q_BLOCK
    o = lax.map(block, (q, starts))
    o = rms_norm(o, subln, SUBLN_EPS) * (1.0 - lam_init)
    o = o.transpose(1, 0, 3, 2, 4).reshape(B, T, H * DIFF_V_HEAD)
    return o @ w_o

def second_inputs(seed: int = 0) -> dict:
    key = jax.random.key(seed)
    ks = jax.random.split(key, 29)
    C, F = D_MODEL, D_FF
    nA, nB = N_A_LAYERS, N_B_LAYERS
    nrm = lambda k, shape, s: jax.random.normal(k, shape, jnp.float32) * s
    gain = lambda k, shape: 1.0 + nrm(k, shape, 0.02)
    return {
        "x": nrm(ks[0], (BATCH, SEQ, C), 1.0),
        "ffn_norm": gain(ks[1], (DEPTH_2, 2, C)),
        "ffn_w_in": nrm(ks[2], (DEPTH_2, 2, C, 2 * F), C ** -0.5),
        "ffn_w_out": nrm(ks[3], (DEPTH_2, 2, F, C), F ** -0.5),
        "mix_norm": gain(ks[4], (DEPTH_2, C)),
        "rwkv_mu": jax.random.uniform(ks[5], (nA, N_SHIFT_MIX, C), jnp.float32),
        "rwkv_w_rkv": nrm(ks[6], (nA, 3, C, C), C ** -0.5),
        "rwkv_w0": jax.random.uniform(ks[7], (nA, C), jnp.float32, -6.0, -1.0),
        "rwkv_w1": nrm(ks[8], (nA, C, LORA_DECAY), C ** -0.5),
        "rwkv_w2": nrm(ks[9], (nA, LORA_DECAY, C), 0.5 * LORA_DECAY ** -0.5),
        "rwkv_a0": nrm(ks[10], (nA, C), 0.1),
        "rwkv_a1": nrm(ks[11], (nA, C, LORA_AAA), C ** -0.5),
        "rwkv_a2": nrm(ks[12], (nA, LORA_AAA, C), 0.5 * LORA_AAA ** -0.5),
        "rwkv_g1": nrm(ks[13], (nA, C, LORA_GATE), C ** -0.5),
        "rwkv_g2": nrm(ks[14], (nA, LORA_GATE, C), LORA_GATE ** -0.5),
        "rwkv_k_k": 0.85 + nrm(ks[15], (nA, C), 0.02),
        "rwkv_k_a": gain(ks[16], (nA, C)),
        "rwkv_r_k": nrm(ks[17], (nA, RWKV_HEADS, RWKV_HEAD), 0.1),
        "rwkv_ln_g": gain(ks[18], (nA, C)),
        "rwkv_ln_b": nrm(ks[19], (nA, C), 0.02),
        "rwkv_w_o": nrm(ks[20], (nA, C, C), 0.5 * C ** -0.5),
        "kv_norm": gain(ks[21], (C,)),
        "w_kv": nrm(ks[22], (C, 2 * C), C ** -0.5),
        "k_norm": gain(ks[23], (DIFF_HEAD,)),
        "diff_w_q": nrm(ks[24], (nB, C, C), C ** -0.5),
        "diff_q_norm": gain(ks[25], (nB, DIFF_HEAD)),
        "diff_lambda": nrm(ks[26], (nB, 4, DIFF_HEAD), 0.1),
        "diff_subln": gain(ks[27], (nB, DIFF_V_HEAD)),
        "diff_w_o": nrm(ks[28], (nB, C, C), 0.5 * C ** -0.5),
    }

def second_block(x, ffn_norm, ffn_w_in, ffn_w_out, mix_norm, rwkv_mu, rwkv_w_rkv, rwkv_w0, rwkv_w1, rwkv_w2,
              rwkv_a0, rwkv_a1, rwkv_a2, rwkv_g1, rwkv_g2, rwkv_k_k, rwkv_k_a, rwkv_r_k, rwkv_ln_g, rwkv_ln_b,
              rwkv_w_o, kv_norm, w_kv, k_norm, diff_w_q, diff_q_norm, diff_lambda, diff_subln, diff_w_o):
    k_sh = None
    v_sh = None
    for l in range(DEPTH_2):
        x = x + 0.5 * swiglu(rms_norm(x, ffn_norm[l, 0]), ffn_w_in[l, 0], ffn_w_out[l, 0])
        h = rms_norm(x, mix_norm[l])
        if l < N_A_LAYERS:
            i = l
            x = x + rwkv7_time_mix(h, rwkv_mu[i], rwkv_w_rkv[i], rwkv_w0[i], rwkv_w1[i], rwkv_w2[i],
                                   rwkv_a0[i], rwkv_a1[i], rwkv_a2[i], rwkv_g1[i], rwkv_g2[i],
                                   rwkv_k_k[i], rwkv_k_a[i], rwkv_r_k[i], rwkv_ln_g[i], rwkv_ln_b[i], rwkv_w_o[i])
        else:
            j = l - N_A_LAYERS
            x = x + diff_attention(h, k_sh, v_sh, diff_w_q[j], diff_q_norm[j], diff_lambda[j],
                                   diff_subln[j], diff_w_o[j], lambda_init(l))
        x = x + 0.5 * swiglu(rms_norm(x, ffn_norm[l, 1]), ffn_w_in[l, 1], ffn_w_out[l, 1])
        if l == N_A_LAYERS - 1:
            k_sh, v_sh = shared_kv(x, kv_norm, w_kv, k_norm)
    return x


def setup_inputs(seed=0):
    out = dict(first_inputs(seed))
    for name, value in second_inputs(seed + 1).items():
        if name != "x":
            out[name + "_2"] = value
    return out


def reference(
    x, c, w_mod, b_mod, norm1_g, w_in, b_f, w_pool, pool_scale, w_out, norm2_g, peer_w_query,
    peer_sub_keys, peer_u, peer_v, final_g, ffn_norm_2, ffn_w_in_2, ffn_w_out_2, mix_norm_2,
    rwkv_mu_2, rwkv_w_rkv_2, rwkv_w0_2, rwkv_w1_2, rwkv_w2_2, rwkv_a0_2, rwkv_a1_2, rwkv_a2_2,
    rwkv_g1_2, rwkv_g2_2, rwkv_k_k_2, rwkv_k_a_2, rwkv_r_k_2, rwkv_ln_g_2, rwkv_ln_b_2,
    rwkv_w_o_2, kv_norm_2, w_kv_2, k_norm_2, diff_w_q_2, diff_q_norm_2, diff_lambda_2,
    diff_subln_2, diff_w_o_2,
):
    x = first_block(
        x, c, w_mod, b_mod, norm1_g, w_in, b_f, w_pool, pool_scale, w_out, norm2_g,
        peer_w_query, peer_sub_keys, peer_u, peer_v, final_g,
    )
    return second_block(
        x, ffn_norm_2, ffn_w_in_2, ffn_w_out_2, mix_norm_2, rwkv_mu_2, rwkv_w_rkv_2, rwkv_w0_2,
        rwkv_w1_2, rwkv_w2_2, rwkv_a0_2, rwkv_a1_2, rwkv_a2_2, rwkv_g1_2, rwkv_g2_2, rwkv_k_k_2,
        rwkv_k_a_2, rwkv_r_k_2, rwkv_ln_g_2, rwkv_ln_b_2, rwkv_w_o_2, kv_norm_2, w_kv_2,
        k_norm_2, diff_w_q_2, diff_q_norm_2, diff_lambda_2, diff_subln_2, diff_w_o_2,
    )


_drawn_inputs = setup_inputs


def setup_inputs(seed=0):
    import zlib

    import numpy as np

    out = dict(_drawn_inputs(seed))
    spreads = {}
    factors = {'norm1_g': 3.675,
     'pool_scale': 4.824,
     'norm2_g': 8.656,
     'ffn_norm_2': 3.25,
     'mix_norm_2': 4.357,
     'rwkv_w1_2': 7.176,
     'rwkv_w2_2': 6.918,
     'rwkv_a0_2': 4.648,
     'rwkv_k_k_2': 64.0,
     'rwkv_k_a_2': 8.0,
     'rwkv_ln_g_2': 64.0,
     'rwkv_ln_b_2': 64.0,
     'kv_norm_2': 44.414,
     'k_norm_2': 52.389,
     'diff_q_norm_2': 64.0,
     'diff_subln_2': 64.0,
     'diff_lambda_2': 3.587}
    for name, (base, spread) in spreads.items():
        noise = np.random.default_rng([zlib.crc32(name.encode()), seed]).standard_normal(out[name].shape)
        drawn = base * np.exp(spread * noise) if base else spread * noise
        out[name] = __import__('jax').numpy.asarray(drawn.astype(out[name].dtype))
    for name, factor in factors.items():
        out[name] = (out[name] * factor).astype(out[name].dtype)
    return out
```

```python
import math
from contextlib import ExitStack

import concourse.bass as bass
from concourse import mybir

F32 = mybir.dt.float32
F32R = mybir.dt.float32r
U32 = mybir.dt.uint32
I32 = mybir.dt.int32
ALU = mybir.AluOpType
ACT = mybir.ActivationFunctionType
AXX = mybir.AxisListType.X

P = 128
D = 1024
T = 256
KT = D // P
TT = T // P
WRING = 3
SLOTW = 2048
CW = SLOTW // KT
EPS = 1e-6
NEG = -1e30
HEADS, DH = 16, 64
PEER_HEADS, TOPK, NKEYS = 8, 16, 128
POOL_WINDOWS = (2, 4, 8, 16)
FF = 2816
FTILES = FF // CW
LORA, LORA_G = 64, 160
RWKV_EPS, SUBLN_EPS = 64e-5, 1e-5
DECAY = math.exp(-0.5)
LAM_INIT = 0.8 - 0.6 * math.exp(-0.3 * 1)
DIFF_HEADS = 8
RROWS = 8

PHASES = [("mod", 24), ("w_in", 22), ("w_out", 4), ("query", 8), ("ffn0", 33), ("rkv", 12), ("rwkv_o", 4),
          ("ffn1", 33), ("kv", 8), ("ffn2", 33), ("diff_q", 4), ("diff_o", 4), ("ffn3", 33)]
BASE, NSLOTS = {}, 0
for _name, _count in PHASES:
    BASE[_name] = NSLOTS
    NSLOTS += _count


def projection_number(n):
    return n - 33 * sum(n >= BASE[f"ffn{f}"] + 33 for f in range(4))


VEC_A = ["mu0", "mu1", "mu2", "mu3", "mu4", "mu5", "ffn0", "ffn1", "ffn2", "ffn3", "mix0", "mix1",
         "norm1_g", "norm2_g", "pool_scale", "w0"]
VEC_B = ["a0", "k_k", "k_a", "r_k", "ln_g", "ln_b", "kv_norm"]
COL = {name: KT * i for i, name in enumerate(VEC_A + VEC_B)}
COL["k_norm"], COL["q_norm"], COL["subln"] = (KT * (len(VEC_A) + len(VEC_B)) + i for i in range(3))
NVEC_B = KT * len(VEC_B) + 3
NVEC = P + NVEC_B


class Order:

    def __init__(self, engine, done):
        self.engine, self.done, self.count = engine, done, 0

    def __call__(self, instruction):
        instruction.then_inc(self.done, 1)
        self.count += 1

    def wait(self):
        if self.count:
            self.engine.wait_ge(self.done, self.count)


def build_program(nc, A, out):
    ctx = ExitStack()
    with ctx:
        def sb(name, shape, dt=F32):
            return ctx.enter_context(nc.sbuf_tensor(name, shape, dt))

        sems = {}

        def S(name):
            if name not in sems:
                sems[name] = ctx.enter_context(nc.semaphore(name))
            return sems[name]

        w_raw = [sb(f"w_raw{i}", [P, SLOTW]) for i in range(WRING)]
        w_hi = [sb(f"w_hi{i}", [P, SLOTW], F32R) for i in range(WRING)]
        w_lo = [sb(f"w_lo{i}", [P, SLOTW], F32R) for i in range(WRING)]
        x = sb("x", [P, TT, D])
        hf = sb("hf", [P, KT, T])
        hh = sb("hh", [P, KT, T], F32R)
        hl = sb("hl", [P, KT, T], F32R)
        act_hi = sb("act_hi", [P, 512], F32R)
        act_lo = sb("act_lo", [P, 512], F32R)
        big = sb("big", [P, 8 * SLOTW])
        aux = sb("aux", [P, 6400])
        ident = sb("ident", [P, P])
        ones = sb("ones", [P, T])
        amask = sb("amask", [P, 384])
        wkv_masks = sb("wkv_masks", [P, 5, P])
        head_ones = sb("head_ones", [P, P])
        half_ones = sb("half_ones", [P, 2])
        vec = sb("vec", [P, NVEC])
        modc = sb("modc", [P, 6 * KT])
        small = sb("small", [P, 256])
        stat = sb("stat", [P, 16])
        w_f = sb("w_f", [P, KT, HEADS])
        bank = [ctx.enter_context(nc.psum_tensor(f"bank{i}", [P, 512], F32)) for i in range(8)]

        def bigs(i, count=1):
            return big[:, i * SLOTW:(i + count) * SLOTW]

        def fm(flat):
            return flat.rearrange("p (k t) -> p k t", t=T)

        def tm(flat):
            return flat.rearrange("p (a d) -> p a d", a=TT)

        def col(name, k):
            return vec[:, COL[name] + k:COL[name] + k + 1]

        xn = tm(bigs(7))
        low16, low_far, up16, up_strict, up_incl = (wkv_masks[:, i, :] for i in range(5))
        silu_g = big[:, 6 * SLOTW:6 * SLOTW + 512]
        act_f = big[:, 6 * SLOTW + 512:6 * SLOTW + 1024]

        vec_rows = bigs(5)
        c_rows = vec_rows[0:KT, 512:640]
        b_mod_row = big[0:1, 0:6 * D]
        gt1, gt2 = aux[:, 0:D], aux[:, D:2 * D]
        h2tok = aux[:, 2 * D:4 * D].rearrange("p (a d) -> p a d", a=TT)
        mod_tmp = big[:, 3 * SLOTW:5 * SLOTW]

        def mod_place(j):
            part, c0 = j // 4, (j % 4) * CW
            if part in (2, 5):
                return (gt1 if part == 2 else gt2)[:, c0:c0 + CW]
            q = {0: 0, 1: 1, 3: 2, 4: 3}[part]
            return mod_tmp[:, q * D + c0:q * D + c0 + CW]

        qT, kT, vtok = fm(bigs(0)), fm(bigs(1)), tm(bigs(2))
        upool, ga, gb = bigs(3)[:, 0:4 * T].rearrange("p (g t) -> p g t", t=T), fm(bigs(4)), fm(bigs(5))
        pool_win = bigs(3)[:, 4 * T:8 * T].rearrange("p (a t) -> p a t", t=T)
        w_pool = bigs(6)[:, 0:4 * T].rearrange("p (g d) -> p g d", g=4)
        pooled = bigs(6)[:, 4 * T:8 * T].rearrange("p (g t) -> p g t", g=4)
        inv_count = small[:, 0:64].rearrange("p (g t) -> p g t", g=4)
        logf, cumf, negf, ftmp = (aux[0:HEADS, 4096 + i * T:4096 + (i + 1) * T] for i in range(4))
        att_s = big[:, 7 * SLOTW:7 * SLOTW + 2 * 384].rearrange("p (b n) -> p b n", b=2)
        att_pT = big[:, 7 * SLOTW + 768:7 * SLOTW + 2 * 768].rearrange("p (b n) -> p b n", b=2)
        b_f = small[0:HEADS, 64:65]
        att_stat = small[:, 96:96 + 8 * 2].rearrange("p (b n) -> p b n", b=2)

        def slot_source(n):
            for name, count in PHASES:
                if BASE[name] <= n < BASE[name] + count:
                    j = n - BASE[name]
                    break
            def columns(w, c0):
                return w.rearrange("(k p) c -> p k c", p=P)[:, :, c0:c0 + CW]
            if name == "mod":
                return columns(A["w_mod"][0], j * CW)
            if name == "w_in":
                starts = [512 + CW * i for i in range(12)] + [0, 256] + [3600 + CW * i for i in range(8)]
                return columns(A["w_in"][0], starts[j])
            if name == "w_out":
                return columns(A["w_out"][0], j * CW)
            if name == "query":
                return columns(A["peer_w_query"][0], j * CW)
            if name == "rkv":
                return columns(A["rwkv_w_rkv_2"][0, j // 4], (j % 4) * CW)
            if name == "rwkv_o":
                return columns(A["rwkv_w_o_2"][0], j * CW)
            if name == "kv":
                return columns(A["w_kv_2"], j * CW)
            if name == "diff_q":
                return columns(A["diff_w_q_2"][0], j * CW)
            return columns(A["diff_w_o_2"][0], j * CW)

        def slot_view(tile):
            return tile[:, :].rearrange("p (k c) -> p k c", k=KT)

        def load_slot(sp, n, i, src):
            if not (isinstance(n, int) and n < WRING):
                sp.wait_ge(S("w_lo"), n - (WRING - 1))
            k = src.shape[1]
            sp.dma_start(w_raw[i][:, :].rearrange("p (k c) -> p k c", k=k), src).then_inc(S(f"w_loaded{i}"), 16)

        def ffn_sp(sp, f):
            base = BASE[f"ffn{f}"]
            w_in = A["ffn_w_in_2"][f // 2, f % 2].rearrange("(k p) c -> p k c", p=P)
            w_out = A["ffn_w_out_2"][f // 2, f % 2].rearrange("(a p) d -> p a d", p=P)

            def g(n, i, r):
                load_slot(sp, n, r, w_in[:, :, bass.ds(i * CW, CW)])

            def u(n, i, r):
                load_slot(sp, n, r, w_in[:, :, bass.ds(i * CW + FF, CW)])

            def o(n, i, r):
                load_slot(sp, n, r, w_out[:, bass.ds(i * 2, 2), :])
            g(base, 0, base % WRING)
            u(base + 1, 0, (base + 1) % WRING)
            with sp.Fori(0, FTILES - 1) as i:
                n = i * 3 + (base + 2)
                g(n, i + 1, (base + 2) % WRING)
                u(n + 1, i + 1, (base + 3) % WRING)
                o(n + 2, i, (base + 4) % WRING)
            o(base + 32, FTILES - 1, (base + 32) % WRING)

        def split_hi(act, n, i, loaded):
            act.wait_ge(S(f"w_loaded{i}"), loaded)
            if not (isinstance(n, int) and n < WRING):
                act.wait_ge(S("slot_done"), n - (WRING - 1))
            act.activation(w_hi[i][:, :], w_raw[i][:, :], ACT.Copy).then_inc(S("w_hi"), 1)

        def split_lo(dve, n, i):
            dve.wait_ge(S("w_hi"), n + 1)
            dve.tensor_tensor(w_lo[i][:, :], w_raw[i][:, :], w_hi[i][:, :].bitcast(F32), ALU.subtract)\
               .then_inc(S("w_lo"), 1)

        class HiStream:
            def __init__(self, act):
                self.act, self.next = act, 0

            def upto(self, n):
                while self.next <= min(n, NSLOTS - 1):
                    m = self.next
                    split_hi(self.act, m, m % WRING, 16 * (m // WRING + 1))
                    self.next += 1

        class LoStream:
            def __init__(self, dve):
                self.dve, self.next = dve, 0

            def upto(self, n):
                while self.next <= min(n, NSLOTS - 1):
                    split_lo(self.dve, self.next, self.next % WRING)
                    self.next += 1

        def project(pe, n, hi, lo, mode):
            number = projection_number(n)
            b = bank[number % 2]
            wh, wl = slot_view(w_hi[n % WRING]), slot_view(w_lo[n % WRING])
            pe.wait_ge(S("w_lo"), n + 1)
            if number >= 2:
                pe.wait_ge(S(f"proj_free{number % 2}"), number // 2)
            for part in range(1 if mode == "M" else 2):
                for k in range(KT):
                    for m, (wp, ap) in enumerate(((wh, hi), (wh, lo), (wl, hi))):
                        if mode == "F":
                            lhs, rhs = wp[:, k, part * P:(part + 1) * P], ap[:, k, :]
                        else:
                            lhs, rhs = ap[:, k, part * P:(part + 1) * P], wp[:, k, :]
                        mm = pe.matmul(b[:, part * CW:(part + 1) * CW], lhs, rhs, start=(k == 0 and m == 0),
                                       stop=(mode != "M" and k == KT - 1 and m == 2))
            if mode == "M":
                j = n - BASE["mod"]
                mm = pe.matmul(b[:, 0:CW], ones[0:1, 0:P], b_mod_row[:, j * CW:(j + 1) * CW], start=False, stop=True)
            mm.then_inc(S("slot_done"), 1)

        def evac_ready(eng, n):
            eng.wait_ge(S("slot_done"), n + 1)
            return bank[projection_number(n) % 2], S(f"proj_free{projection_number(n) % 2}")

        def norm_act(act, n, hi):
            if n > 0:
                act.wait_ge(S("x_ready"), XREADY[n])
            for tt in range(TT):
                act.activation(xn[:, tt, :], x[:, tt, :], ACT.Square, accum_out=stat[:, tt:tt + 1])\
                   .then_inc(S("norm_ss"), 1)
            act.wait_ge(S("norm_rstd"), n + 1)
            for tt in range(TT):
                act.activation(xn[:, tt, :], x[:, tt, :], ACT.Copy, scale=stat[:, 4 + tt:5 + tt])\
                   .then_inc(S("norm_xn"), 1)
            if n in SPLIT:
                for kp in range(4):
                    act.wait_ge(S("norm_hf"), 4 * n + kp + 1)
                    act.activation(hh[:, 2 * kp:2 * kp + 2, :], hf[:, 2 * kp:2 * kp + 2, :], ACT.Copy)\
                       .then_inc(S("norm_hh"), 1)

        def norm_pool(pool, n):
            pool.wait_ge(S("norm_ss"), TT * (n + 1))
            pool.tensor_scalar(stat[:, 2:4], stat[:, 0:2], 1.0 / D, EPS, ALU.mult, ALU.add).then_inc(S("norm_ms"), 1)
            pool.wait_ge(S("norm_ms"), n + 1)
            pool.tensor_tensor(stat[:, 4:6], stat[:, 2:4], stat[:, 6:8], ALU.pow).then_inc(S("norm_rstd"), 1)

        def norm_pe(pe, n):
            for kp in range(4):
                b = bank[4 + kp]
                for k in (2 * kp, 2 * kp + 1):
                    for tt in range(TT):
                        pe.wait_ge(S("norm_xn"), TT * n + tt + 1)
                        mm = pe.transpose(b[:, (k % 2) * T + tt * P:(k % 2) * T + (tt + 1) * P],
                                          xn[:, tt, k * P:(k + 1) * P], ident[:, :])
                mm.then_inc(S("norm_tr"), 1)

        def norm_dve(dve, n, scale, bias=None):
            for kp in range(4):
                dve.wait_ge(S("norm_tr"), 4 * n + kp + 1)
                for k in (2 * kp, 2 * kp + 1):
                    src = bank[4 + kp][:, (k % 2) * T:(k % 2 + 1) * T]
                    if bias is None:
                        v = dve.tensor_scalar(hf[:, k, :], src, scale(k), None, ALU.mult)
                    else:
                        v = dve.tensor_scalar(hf[:, k, :], src, scale(k), bias(k), ALU.mult, ALU.add)
                v.then_inc(S("norm_hf"), 1)
            if n in SPLIT:
                for half in range(2):
                    dve.wait_ge(S("norm_hh"), 4 * SPLIT.index(n) + 2 * half + 2)
                    k0 = 4 * half
                    dve.tensor_tensor(hl[:, k0:k0 + 4, :], hf[:, k0:k0 + 4, :], hh[:, k0:k0 + 4, :].bitcast(F32),
                                      ALU.subtract).then_inc(S("act_split"), 1)

        SPLIT = [0, 1, 2, 4, 5, 6, 7, 8]
        XREADY = {1: 4, 2: 6, 3: 10, 4: 14, 5: 18, 6: 18, 7: 22, 8: 26}
        SPLITS = {}
        _total = 0
        for _step, _n in [("norm0", 2), ("y1", 1), ("norm1", 2), ("norm2", 2), ("mix_r", 1), ("mix_k", 1),
                          ("mix_v", 1), ("rwkv_y", 1), ("norm4", 2), ("norm5", 2), ("norm6", 2), ("norm7", 2),
                          ("diff_y", 1), ("norm8", 2)]:
            _total += _n
            SPLITS[_step] = _total

        def ffn_pe(pe, f):
            base = BASE[f"ffn{f}"]
            norm = {0: 2, 1: 4, 2: 6, 3: 8}[f]
            norm_pe(pe, norm)
            pe.wait_ge(S("act_split"), SPLITS[f"norm{norm}"])

            def up(n, i, r, b, freed):
                pe.wait_ge(S("w_lo"), n + 1)
                if not (isinstance(i, int) and i + f == 0):
                    pe.wait_ge(S(freed), i + FTILES * f)
                wh, wl = slot_view(w_hi[r]), slot_view(w_lo[r])
                for part in range(2):
                    for k in range(KT):
                        for m, (wp, ap) in enumerate(((wh, hh), (wh, hl), (wl, hh))):
                            mm = pe.matmul(b[:, part * T:(part + 1) * T], wp[:, k, part * P:(part + 1) * P],
                                           ap[:, k, :], start=(k == 0 and m == 0), stop=(k == KT - 1 and m == 2))
                mm.then_inc(S("slot_done"), 1)

            def down(n, i, r, first, last):
                pe.wait_ge(S("w_lo"), n + 1)
                pe.wait_ge(S("ffn_act"), i + (FTILES * f + 1))
                wh = w_hi[r][:, :].rearrange("p (a d) -> p a d", a=2)
                wl = w_lo[r][:, :].rearrange("p (a d) -> p a d", a=2)
                for tt in range(TT):
                    for half in range(2):
                        for a in range(2):
                            rows = slice(a * T + tt * P, a * T + (tt + 1) * P)
                            for m, (ap, wp) in enumerate(((act_hi, wh), (act_lo, wh), (act_hi, wl))):
                                mm = pe.matmul(bank[4 + 2 * tt + half][:, :], ap[:, rows],
                                               wp[:, a, half * 512:(half + 1) * 512],
                                               start=(first and a == 0 and m == 0), stop=(last and a == 1 and m == 2))
                mm.then_inc(S("slot_done"), 1)

            def step(i, first):
                n = i * 3 + (base + 2)
                up(n, i + 1, (base + 2) % WRING, bank[2], "ffn_silu")
                up(n + 1, i + 1, (base + 3) % WRING, bank[3], "ffn_mult")
                down(n + 2, i, (base + 4) % WRING, first, False)
            up(base, 0, base % WRING, bank[2], "ffn_silu")
            up(base + 1, 0, (base + 1) % WRING, bank[3], "ffn_mult")
            step(0, True)
            with pe.Fori(1, FTILES - 1) as i:
                step(i, False)
            down(base + 32, FTILES - 1, (base + 32) % WRING, False, True)

        def ffn_act(act, f, hi):
            base = BASE[f"ffn{f}"]
            norm_act(act, {0: 2, 1: 4, 2: 6, 3: 8}[f], hi)
            hi.upto(base + 1)

            def silu(i, n):
                act.wait_ge(S("slot_done"), n + 1)
                if not (isinstance(i, int) and i + f == 0):
                    act.wait_ge(S("ffn_mult"), i + FTILES * f)
                act.activation(silu_g, bank[2][:, :], ACT.Silu).then_inc(S("ffn_silu"), 1)

            def act_round(i, n):
                act.wait_ge(S("ffn_mult"), i + (FTILES * f + 1))
                act.wait_ge(S("slot_done"), n)
                act.activation(act_hi[:, :], act_f, ACT.Copy).then_inc(S("ffn_act_hi"), 1)

            def step(i, split):
                n = i * 3 + (base + 2)
                split(n + 2, 2, i)
                silu(i + 1, n)
                split(n + 3, 3, i)
                split(n + 4, 4, i)
                act_round(i + 1, n + 3)

            def split_static(n, j, i):
                hi.upto(n)

            def split_loop(n, j, i):
                slot0 = base + 2 + j
                split_hi(act, n, slot0 % WRING, i * 16 + 16 * (slot0 // WRING + 1))
            hi.upto(base + 2)
            silu(0, base)
            hi.upto(base + 3)
            act_round(0, base)
            step(0, split_static)
            with act.Fori(1, FTILES - 2) as i:
                step(i, split_loop)
            hi.next = base + 2 + 3 * (FTILES - 2) + 2
            step(FTILES - 2, split_static)
            hi.upto(base + 34)

        def ffn_dve(dve, f, lo):
            base = BASE[f"ffn{f}"]
            n_norm = {0: 2, 1: 4, 2: 6, 3: 8}[f]
            norm_dve(dve, n_norm, lambda k: col(f"ffn{f}", k))
            lo.upto(base + 1)

            def mult(i, n):
                dve.wait_ge(S("ffn_silu"), i + (FTILES * f + 1))
                dve.wait_ge(S("slot_done"), n + 1)
                if not (isinstance(i, int) and i + f == 0):
                    dve.wait_ge(S("ffn_act"), i + FTILES * f)
                dve.tensor_tensor(act_f, silu_g, bank[3][:, :], ALU.mult).then_inc(S("ffn_mult"), 1)

            def act_rest(i):
                dve.wait_ge(S("ffn_act_hi"), i + (FTILES * f + 1))
                dve.tensor_tensor(act_lo[:, :], act_f, act_hi[:, :].bitcast(F32), ALU.subtract)\
                   .then_inc(S("ffn_act"), 1)

            def step(i, split):
                n = i * 3 + (base + 2)
                split(n + 2, 2)
                split(n + 3, 3)
                mult(i + 1, n + 1)
                split(n + 4, 4)
                act_rest(i + 1)

            def split_static(n, j):
                lo.upto(n)

            def split_loop(n, j):
                split_lo(dve, n, (base + 2 + j) % WRING)
            lo.upto(base + 2)
            mult(0, base + 1)
            lo.upto(base + 3)
            act_rest(0)
            step(0, split_static)
            with dve.Fori(1, FTILES - 2) as i:
                step(i, split_loop)
            lo.next = base + 2 + 3 * (FTILES - 2) + 2
            step(FTILES - 2, split_static)
            lo.upto(base + 34)
            dve.wait_ge(S("slot_done"), base + 33)
            for tt in range(TT):
                for half in range(2):
                    part = x[:, tt, half * 512:(half + 1) * 512]
                    dve.scalar_tensor_tensor(out=part, in0=bank[4 + 2 * tt + half][:, :], scalar=0.5, in1=part,
                                             op0=ALU.mult, op1=ALU.add).then_inc(S("x_ready"), 1)

        cT = small[:, 72:80]

        def rows(v):
            return v.rearrange("(k p) -> k p", p=P)

        SETUP_LOADS = 20

        def setup_act(act):
            def load(dst, src):
                act.dma_start(dst, src).then_inc(S("params"), 16)
            load(c_rows, rows(A["c"][0]))
            load(b_mod_row, A["b_mod"])
            load(x[:, :, :], A["x"][0].rearrange("(a p) d -> p a d", p=P))
            r = 0
            for src in ([A["rwkv_mu_2"].rearrange("a m (k p) -> (a m k) p", p=P),
                         A["ffn_norm_2"].rearrange("a m (k p) -> (a m k) p", p=P),
                         A["mix_norm_2"].rearrange("a (k p) -> (a k) p", p=P)]
                        + [rows(A[n][0]) for n in ("norm1_g", "norm2_g", "pool_scale", "rwkv_w0_2")]):
                load(vec_rows[r:r + src.shape[0], 0:P], src)
                r += src.shape[0]
            r = 0
            for src in ([rows(A[n][0]) for n in ("rwkv_a0_2", "rwkv_k_k_2", "rwkv_k_a_2")]
                        + [A["rwkv_r_k_2"][0].rearrange("(k a) d -> k (a d)", a=2)]
                        + [rows(A[n][0]) for n in ("rwkv_ln_g_2", "rwkv_ln_b_2")] + [rows(A["kv_norm_2"])]):
                load(vec_rows[r:r + KT, P:2 * P], src)
                r += KT
            head_gains = [A["k_norm_2"], A["diff_q_norm_2"][0]]
            for src in head_gains:
                act.dma_start(vec_rows[r:r + 1, P:P + DH], src.rearrange("(a d) -> a d", a=1)).then_inc(S("params"), 16)
                act.dma_start(vec_rows[r:r + 1, P + DH:2 * P], src.rearrange("(a d) -> a d", a=1))\
                   .then_inc(S("params"), 16)
                r += 1
            load(vec_rows[r:r + 1, P:2 * P], A["diff_subln_2"])
            load(w_f[:, :, :], A["w_in"][0].rearrange("(k p) c -> p k c", p=P)[:, :, 3584:3600])
            load(b_f, A["b_f"].rearrange("a h -> h a"))
            load(w_pool, A["w_pool"][0].rearrange("g c d -> c g d"))
            act.wait_ge(S("cT"), 1)
            act.activation(hh[:, :, 0:P], cT.unsqueeze(2).to_broadcast([P, KT, P]), ACT.Copy).then_inc(S("c_hi"), 1)

        N_PARAMS = 16 * (3 + 7 + 7 + 4 + 1 + 3)

        pool_order = []

        def setup_pool(pool):
            o = Order(pool, S("pool_order"))
            pool_order.append(o)
            o(pool.memset(ident[:, :], 0.0))
            o(pool.memset(stat[:, 6:8], -0.5))
            pool.memset(ones[:, :], 1.0).then_inc(S("ones"), 1)
            o.wait()
            pool.affine_select(out=ident[:, :], in_=ident[:, :], compare_op=ALU.not_equal, fill=1.0, base=0,
                               pattern=[[-1, P]], channel_multiplier=1).then_inc(S("ident"), 1)
            o(pool.memset(amask[:, :], 0.0))
            o.wait()
            for c0 in (0, 256):
                pool.affine_select(out=amask[:, c0:c0 + P], in_=amask[:, c0:c0 + P], compare_op=ALU.is_ge, fill=NEG,
                                   base=0, pattern=[[-1, P]], channel_multiplier=1).then_inc(S("causal"), 1)
            pool.iota(small[:, 80:96], pattern=[[1, 16]], base=1, channel_multiplier=0,
                      allow_small_or_imprecise_dtypes=True).then_inc(S("token_count"), 1)

        def setup_pe(pe):
            pe.wait_ge(S("ident"), 1)
            pe.wait_ge(S("ones"), 1)
            pe.wait_ge(S("params"), N_PARAMS)
            pe.transpose(bank[4][:, 0:KT], c_rows, ident[0:KT, 0:KT]).then_inc(S("setup_tr"), 1)
            pe.transpose(bank[5][:, 0:P], vec_rows[:, 0:P], ident[:, :])
            pe.transpose(bank[5][:, P:NVEC], vec_rows[0:NVEC_B, P:2 * P], ident[0:NVEC_B, 0:NVEC_B])\
              .then_inc(S("setup_tr"), 1)
            pe.wait_ge(S("act_split_c"), 1)
            for n in range(24):
                project(pe, n, hh, hl, "M")
            for b in range(2):
                pe.wait_ge(S(f"proj_free{b}"), 10)
            for j in range(4 * KT):
                mm = pe.matmul(bank[4][:, j:j + 1], mod_tmp[0:1, j * P:(j + 1) * P], ones[0:1, 0:1],
                               start=True, stop=True)
            mm.then_inc(S("mod_tr"), 1)

        def setup_dve(dve, lo):
            o = Order(dve, S("dve_order"))
            dve.wait_ge(S("setup_tr"), 1)
            dve.tensor_copy(cT, bank[4][:, 0:KT]).then_inc(S("cT"), 1)
            dve.wait_ge(S("setup_tr"), 2)
            dve.tensor_copy(vec[:, :], bank[5][:, 0:NVEC]).then_inc(S("vec"), 1)
            dve.wait_ge(S("c_hi"), 1)
            dve.tensor_tensor(hl[:, :, 0:P], cT.unsqueeze(2).to_broadcast([P, KT, P]), hh[:, :, 0:P].bitcast(F32),
                              ALU.subtract).then_inc(S("act_split_c"), 1)
            dve.wait_ge(S("token_count"), 1)
            for g, w in enumerate(POOL_WINDOWS):
                o(dve.tensor_scalar(inv_count[:, g, :], small[:, 80:96], float(w), None, ALU.min))
            o.wait()
            o(dve.reciprocal(inv_count, inv_count))
            for n in range(24):
                lo.upto(n + 2)
                b, free = evac_ready(dve, n)
                dve.tensor_copy(mod_place(n), b[:, 0:CW]).then_inc(free, 1)
            dve.wait_ge(S("mod_tr"), 1)
            dve.tensor_copy(modc[:, 0:32], bank[4][:, 0:32]).then_inc(S("modc"), 1)
            dve.wait_ge(S("modc"), 1)
            dve.wait_ge(S("vec"), 1)
            for i, g in enumerate(("norm1_g", "norm2_g")):
                o(dve.scalar_tensor_tensor(out=modc[:, 32 + KT * i:32 + KT * (i + 1)],
                                           in0=modc[:, 16 * i + KT:16 * i + 2 * KT], scalar=1.0,
                                           in1=vec[:, COL[g]:COL[g] + KT], op0=ALU.add, op1=ALU.mult))
            o.wait()
            return o

        def mod_gain(i):
            return lambda k: modc[:, 32 + KT * i + k:33 + KT * i + k]

        def mod_shift(i):
            return lambda k: modc[:, 16 * i + k:16 * i + k + 1]

        WIN = BASE["w_in"]
        Q0, K0, V0, U0, GA0, GB0 = WIN, WIN + 4, WIN + 8, WIN + 12, WIN + 14, WIN + 18

        def block1_pe(pe):
            pe.wait_ge(S("modc"), 1)
            norm_pe(pe, 0)
            pe.wait_ge(S("act_split"), SPLITS["norm0"])
            for k in range(KT):
                mm = pe.matmul(bank[2][0:HEADS, 0:T], w_f[:, k, :], hf[:, k, :], start=(k == 0), stop=(k == KT - 1))
            mm.then_inc(S("forget_logits"), 1)
            for n in range(WIN, WIN + 22):
                project(pe, n, hh, hl, "T" if V0 <= n < U0 else "F")
            pe.wait_ge(S("pooled"), 4)
            for g in range(4):
                for half in range(2):
                    mm = pe.matmul(bank[4 + g][:, half * T:(half + 1) * T], w_pool[:, g, half * P:(half + 1) * P],
                                   pooled[:, g, :], start=True, stop=True)
                mm.then_inc(S("pool_out"), 1)
            pe.wait_ge(S("pool_mixed"), 4)
            pe.wait_ge(S("cumf"), 2)
            for b in range(2):
                pe.wait_ge(S(f"proj_free{b}"), projection_number(U0) // 2)

            def scores(h):
                po, k = DH * (h % 2), h // 2
                if h >= 2:
                    pe.wait_ge(S("att_masked"), h - 1)
                for qt in range(TT):
                    n_keys = P * (qt + 1)
                    o_ = bank[2 + h % 2][:, P * qt:P * qt + n_keys]
                    pick = ident[0:HEADS, h:h + 1]
                    pe.matmul(o_, qT[po:po + DH, k, qt * P:(qt + 1) * P], kT[po:po + DH, k, 0:n_keys],
                              start=True, stop=False)
                    pe.matmul(o_, cumf[:, qt * P:(qt + 1) * P], pick.to_broadcast([HEADS, n_keys]),
                              start=False, stop=False)
                    mm = pe.matmul(o_, pick.to_broadcast([HEADS, P]), negf[:, 0:n_keys], start=False, stop=True)
                mm.then_inc(S("att_scores"), 1)

            def turn(h):
                pe.wait_ge(S("att_p"), h + 1)
                if h >= 2:
                    pe.wait_ge(S("att_pT"), h - 1)
                for j in range(3):
                    mm = pe.transpose(bank[4 + h % 2][:, j * P:(j + 1) * P], att_s[:, h % 2, j * P:(j + 1) * P],
                                      ident[:, :])
                mm.then_inc(S("att_turned"), 1)

            def values(h):
                po = DH * (h % 2)
                pe.wait_ge(S("att_pT"), h + 1)
                if h % 2 == 0 and h >= 4:
                    pe.wait_ge(S("att_out"), h // 2 - 1)
                o_ = bank[6 + (h // 2) % 2][po:po + DH, :]
                for qt, j, kt in ((0, 0, 0), (1, 1, 0), (1, 2, 1)):
                    mm = pe.matmul(o_[:, qt * P:(qt + 1) * P], vtok[:, kt, h * DH:(h + 1) * DH],
                                   att_pT[:, h % 2, j * P:(j + 1) * P], start=(kt == 0), stop=(kt == qt))
                mm.then_inc(S("att_pv"), 1)
            for h in range(HEADS + 2):
                if h < HEADS:
                    scores(h)
                if 1 <= h <= HEADS:
                    turn(h - 1)
                if h >= 2:
                    values(h - 2)
            pe.wait_ge(S("act_split"), SPLITS["y1"])
            for n in range(BASE["w_out"], BASE["w_out"] + 4):
                project(pe, n, hh, hl, "T")

        def block1_act(act, hi):
            act.wait_ge(S("params"), N_PARAMS)
            norm_act(act, 0, hi)
            o = Order(act, S("act_order"))
            act.wait_ge(S("forget_z"), 1)
            o(act.activation(ftmp, logf, ACT.Abs))
            o.wait()
            o(act.activation(ftmp, ftmp, ACT.Exp, scale=-1.0))
            o.wait()
            act.activation(ftmp, ftmp, ACT.Ln, bias=1.0).then_inc(S("softplus"), 1)
            for n in range(WIN, WIN + 22):
                hi.upto(n + 2)
                j = n - WIN
                if Q0 <= n < K0:
                    b, free = evac_ready(act, n)
                    act.activation(qT[:, 2 * j:2 * j + 2, :], b[:, :], ACT.Copy, scale=DH ** -0.5).then_inc(free, 1)
                if GA0 <= n:
                    b, free = evac_ready(act, n)
                    g, j = (ga, n - GA0) if n < GB0 else (gb, n - GB0)
                    act.activation(g[:, 2 * j:2 * j + 2, :], b[:, :], ACT.Sigmoid).then_inc(free, 1)

            def exps(h):
                act.wait_ge(S("att_max"), h + 1)
                for qt in range(TT):
                    s = att_s[:, h % 2, P * qt:P * qt + P * (qt + 1)]
                    a = act.activation(s, s, ACT.Exp, bias=att_stat[:, h % 2, qt:qt + 1],
                                       accum_out=att_stat[:, h % 2, 2 + qt:3 + qt])
                a.then_inc(S("att_exp"), 1)

            def copy_out(h):
                act.wait_ge(S("att_turned"), h + 1)
                if h >= 2:
                    act.wait_ge(S("att_pv"), h - 1)
                act.activation(att_pT[:, h % 2, :], bank[4 + h % 2][:, 0:384], ACT.Copy).then_inc(S("att_pT"), 1)
            for h in range(HEADS + 1):
                if h < HEADS:
                    exps(h)
                if h >= 1:
                    copy_out(h - 1)
            act.wait_ge(S("att_out"), HEADS // 2)
            act.dma_start(keys_rows, A["peer_sub_keys"][0].rearrange("h i n c -> n (h i) c")).then_inc(S("keys"), 16)
            act.activation(hh[:, :, :], hf[:, :, :], ACT.Copy).then_inc(S("y1_hi"), 1)
            hi.upto(BASE["w_out"] + 5)

        def block1_dve(dve, lo, o):
            norm_dve(dve, 0, mod_gain(0), mod_shift(0))
            dve.wait_ge(S("forget_logits"), 1)
            dve.tensor_scalar(logf, bank[2][0:HEADS, 0:T], b_f, None, ALU.add).then_inc(S("forget_z"), 1)
            dve.wait_ge(S("softplus"), 1)
            o(dve.tensor_scalar(logf, logf, 0.0, None, ALU.min))
            o.wait()
            o(dve.tensor_tensor(logf, logf, ftmp, ALU.subtract))
            o.wait()
            dve.tensor_tensor_scan(cumf, ones[0:HEADS, :], logf, 0.0, ALU.mult, ALU.add).then_inc(S("cumf"), 1)
            dve.wait_ge(S("cumf"), 1)
            dve.tensor_scalar(negf, cumf, -1.0, None, ALU.mult).then_inc(S("cumf"), 1)
            for n in range(WIN, WIN + 22):
                lo.upto(n + 2)
                if K0 <= n < GA0:
                    b, free = evac_ready(dve, n)
                    two = b[:, :].rearrange("p (a t) -> p a t", a=2)
                    if n < V0:
                        v = dve.tensor_copy(kT[:, 2 * (n - K0):2 * (n - K0) + 2, :], two)
                    elif n < U0:
                        v = dve.tensor_copy(vtok[:, :, CW * (n - V0):CW * (n - V0 + 1)], two)
                    else:
                        v = dve.tensor_copy(upool[:, 2 * (n - U0):2 * (n - U0) + 2, :], two)
                    v.then_inc(free, 1)
                if n == GA0:
                    pool_windows(dve, o)
            dve.wait_ge(S(f"proj_free{projection_number(GB0 - 1) % 2}"), projection_number(GB0 - 1) // 2 + 1)
            dve.wait_ge(S(f"proj_free{projection_number(GB0 - 2) % 2}"), projection_number(GB0 - 2) // 2 + 1)
            for g in range(4):
                dve.wait_ge(S("pool_out"), g + 1)
                for half in range(2):
                    k = 2 * g + half
                    v = dve.scalar_tensor_tensor(out=ga[:, k, :], in0=bank[4 + g][:, half * T:(half + 1) * T],
                                                 scalar=col("pool_scale", k), in1=ga[:, k, :],
                                                 op0=ALU.mult, op1=ALU.mult)
                v.then_inc(S("pool_mixed"), 1)
            dve.wait_ge(S("causal"), 2)

            def mask_max(h):
                dve.wait_ge(S("att_scores"), h + 1)
                if h >= 2:
                    dve.wait_ge(S("att_turned"), h - 1)
                dve.tensor_tensor(att_s[:, h % 2, :], bank[2 + h % 2][:, 0:384], amask[:, :], ALU.add)\
                   .then_inc(S("att_masked"), 1)
                dve.wait_ge(S("att_masked"), h + 1)
                for qt in range(TT):
                    v = dve.tensor_reduce(att_stat[:, h % 2, qt:qt + 1], att_s[:, h % 2, P * qt:P * qt + P * (qt + 1)],
                                          AXX, ALU.max, negate=True)
                v.then_inc(S("att_max"), 1)

            def normalise(h):
                dve.wait_ge(S("att_exp"), h + 1)
                o(dve.reciprocal(att_stat[:, h % 2, 4:6], att_stat[:, h % 2, 2:4]))
                o.wait()
                for qt in range(TT):
                    s = att_s[:, h % 2, P * qt:P * qt + P * (qt + 1)]
                    v = dve.tensor_scalar(s, s, att_stat[:, h % 2, 4 + qt:5 + qt], None, ALU.mult)
                v.then_inc(S("att_p"), 1)

            def gate(k):
                dve.wait_ge(S("att_pv"), 2 * k + 2)
                dve.tensor_tensor(hf[:, k, :], bank[6 + k % 2][:, 0:T], gb[:, k, :], ALU.mult).then_inc(S("att_gated"), 1)
                dve.wait_ge(S("att_gated"), k + 1)
                dve.tensor_tensor(hf[:, k, :], hf[:, k, :], ga[:, k, :], ALU.add).then_inc(S("att_out"), 1)
            for h in range(HEADS + 3):
                if h < HEADS:
                    mask_max(h)
                if 1 <= h <= HEADS:
                    normalise(h - 1)
                if h >= 3 and h % 2 == 1:
                    gate((h - 3) // 2)
            dve.wait_ge(S("y1_hi"), 1)
            dve.tensor_tensor(hl[:, :, :], hf[:, :, :], hh[:, :, :].bitcast(F32), ALU.subtract)\
               .then_inc(S("act_split"), 1)
            residual(dve, lo, BASE["w_out"], gt1)

        def pool_windows(dve, o):
            win = big[:, 7 * SLOTW:8 * SLOTW].rearrange("p (b g t) -> p b g t", b=2, g=4)
            src = upool
            for b, free in ((projection_number(U0) % 2, projection_number(U0) // 2 + 1),
                            (projection_number(U0 + 1) % 2, projection_number(U0 + 1) // 2 + 1)):
                dve.wait_ge(S(f"proj_free{b}"), free)
            for level in range(4):
                shift, dst = 1 << level, win[:, level % 2, :, :]
                o(dve.tensor_tensor(dst[:, level:4, shift:T], src[:, level:4, shift:T], src[:, level:4, 0:T - shift],
                                    ALU.add))
                o(dve.tensor_copy(dst[:, level:4, 0:shift], src[:, level:4, 0:shift]))
                o.wait()
                src = dst
            for g, w in enumerate(POOL_WINDOWS):
                s = win[:, g % 2, g, :]
                dve.scalar_tensor_tensor(out=pooled[:, g, 16:T], in0=s[:, 16:T], scalar=1.0 / w, in1=upool[:, g, 16:T],
                                         op0=ALU.mult, op1=ALU.subtract)
                o(dve.tensor_tensor(s[:, 0:16], s[:, 0:16], inv_count[:, g, :], ALU.mult))
            o.wait()
            for g in range(4):
                dve.tensor_tensor(pooled[:, g, 0:16], win[:, g % 2, g, 0:16], upool[:, g, 0:16], ALU.subtract)\
                   .then_inc(S("pooled"), 1)

        res_count = [0]

        def residual(dve, lo, base, gate_bc=None):
            tmp = big[:, 0:2 * 512].rearrange("p (b a c) -> p b a c", b=2, a=TT)
            for j in range(4):
                lo.upto(base + j + 2)
                b, free = evac_ready(dve, base + j)
                two = b[:, :].rearrange("p (a t) -> p a t", a=TT)
                part = x[:, :, j * CW:(j + 1) * CW]
                if gate_bc is not None:
                    dve.tensor_tensor(tmp[:, j % 2], two, gate_bc[:, j * CW:(j + 1) * CW].unsqueeze(1)
                                      .to_broadcast([P, TT, CW]), ALU.mult).then_inc(free, 1)
                    dve.wait_ge(free, projection_number(base + j) // 2 + 1)
                    dve.tensor_tensor(part, part, tmp[:, j % 2], ALU.add).then_inc(S("x_ready"), 1)
                else:
                    dve.tensor_tensor(part, part, two, ALU.add).then_inc(free, 1)
                    dve.wait_ge(free, projection_number(base + j) // 2 + 1)
                    dve.sem_inc(S("x_ready"), 1)
        QRY = BASE["query"]
        NPICK = PEER_HEADS * TOPK
        ring_rows = [big[:, s * D:(s + 1) * D] for s in range(RROWS)]
        keys_rows = big[:, 4 * SLOTW:5 * SLOTW].rearrange("p (j c) -> p j c", c=P)
        keysT = big[:, 6 * SLOTW:7 * SLOTW].rearrange("p (j n) -> p j n", n=NKEYS)
        scores_tok = big[:, 4 * SLOTW:6 * SLOTW].rearrange("p (a n) -> p a n", a=TT)
        query = big[:, 7 * SLOTW:7 * SLOTW + 1024].rearrange("p (b i t) -> p b i t", b=2, i=2)
        one_hot = big[:, 7 * SLOTW:7 * SLOTW + 1024].rearrange("p (h k i) -> p h k i", h=4, k=TOPK)
        diag = big[:, 7 * SLOTW + 1024:8 * SLOTW].rearrange("p (s n) -> p s n", n=P)
        v_acc = big[:, 6 * SLOTW:7 * SLOTW].rearrange("p (a d) -> p a d", a=TT)
        final_gain = big[:, 5 * SLOTW:5 * SLOTW + D]
        cand = hf[:, :, :].rearrange("p k t -> p (k t)").rearrange("p (h n) -> p h n", h=PEER_HEADS)
        half_s = aux[:, 4096:4608].rearrange("p (a h i k) -> p a h i k", a=TT, h=PEER_HEADS, i=2)
        half_i = aux[:, 4608:5120].bitcast(U32).rearrange("p (a h i k) -> p a h i k", a=TT, h=PEER_HEADS, i=2)
        half_if = aux[:, 5120:5632].rearrange("p (a h i k) -> p a h i k", a=TT, h=PEER_HEADS, i=2)
        sel = aux[:, 5632:5888].bitcast(U32).rearrange("p (a n) -> p a n", a=TT)
        top_s = aux[:, 5888:6144].rearrange("p (a n) -> p a n", a=TT)
        expert = aux[:, 6144:6400].bitcast(I32)
        sel_part = [aux[:, P * i:P * (i + 1)] for i in range(2)]
        sel_key = [aux[:, 256 + P * i:256 + P * (i + 1)] for i in range(2)]
        gates = aux[:, 512:768].rearrange("p (a n) -> p a n", a=TT)
        dots = aux[:, 768:1024]
        gate_sum = small[:, 112:128].rearrange("p (a h) -> p a h", a=TT)
        stage = ctx.enter_context(nc.sbuf_tensor("stage", [P, 2 * RROWS], I32))
        PER = NPICK // RROWS
        V_SHARES = {0: [(0, PER // 2, ()), (PER // 2, PER, (0, 2, 4, 6))], 1: [(0, PER, (0, 4))]}

        def diag_before(tt, step0):
            total = 0
            for a in range(TT):
                for s0, s1, mine in V_SHARES[a]:
                    if (a, s0) < (tt, step0):
                        total += (s1 - s0) * (RROWS - len(mine))
            return total

        def peer_pe(pe):
            pe.wait_ge(S("keys"), 16)
            for g in range(4):
                for j in range(4):
                    mm = pe.transpose(bank[4 + g][:, j * P:(j + 1) * P], keys_rows[:, 4 * g + j, :], ident[:, :])
                mm.then_inc(S("keys_tr"), 1)
            pe.wait_ge(S("keysT"), 4)
            norm_pe(pe, 1)
            pe.wait_ge(S("norm_hf"), 8)
            for tt in range(TT):
                for half in range(2):
                    for j in range(4):
                        k = 4 * half + j
                        mm = pe.transpose(bank[4 + 2 * tt + half][:, j * P:(j + 1) * P],
                                          hf[:, k, tt * P:(tt + 1) * P], ident[:, :])
                    mm.then_inc(S("h2tok_tr"), 1)
            pe.wait_ge(S("act_split"), SPLITS["norm1"])

            def key_scores(h):
                pe.wait_ge(S("query"), h + 1)
                if h >= 2:
                    pe.wait_ge(S("key_scores_read"), h - 1)
                for tt in range(TT):
                    for i in range(2):
                        c = (tt * 2 + i) * P
                        mm = pe.matmul(bank[2 + h % 2][:, c:c + P], query[:, h % 2, i, tt * P:(tt + 1) * P],
                                       keysT[:, 2 * h + i, :], start=True, stop=True)
                mm.then_inc(S("key_scores"), 1)
            for h in range(PEER_HEADS + 1):
                if h < PEER_HEADS:
                    project(pe, QRY + h, hh, hl, "F")
                if h >= 1:
                    key_scores(h - 1)
            for tt in range(TT):
                pe.wait_ge(S("v_zero"), TT)
                if tt == 0:
                    pe.wait_ge(S("h2tok"), 4)
                for half in range(2):
                    mm = pe.matmul(bank[4 + 2 * tt + half][:, :], v_acc[:, tt, 0:P],
                                   h2tok[:, tt, half * 512:(half + 1) * 512], start=True, stop=True)
            mm.then_inc(S("v_open"), 1)
            for tt in range(TT):
                for s0, s1, mine in V_SHARES[tt]:
                    own = [s for s in range(RROWS) if s not in mine]
                    with pe.Fori(s0, s1) as it:
                        use = it + PER * (2 * tt + 1)
                        for i, s in enumerate(own):
                            pe.wait_ge(S(f"row{s}"), use * 16 + 16)
                            pe.wait_ge(S("diag"), (it - s0) * len(own) + (diag_before(tt, s0) + i + 1))
                            for half in range(2):
                                mm = pe.matmul(bank[4 + 2 * tt + half][:, :], diag[:, s, :],
                                               ring_rows[s][:, half * 512:(half + 1) * 512],
                                               start=False, stop=True, skip_group_check=True)
                            mm.then_inc(S(f"row_used{s}"), 1)

        def peer_act(act, hi):
            norm_n = 1
            for g in range(4):
                act.wait_ge(S("keys_tr"), g + 1)
                act.activation(keysT[:, 4 * g:4 * g + 4, :], bank[4 + g][:, :], ACT.Copy).then_inc(S("keysT"), 1)
            norm_act(act, norm_n, hi)
            for tt in range(TT):
                for half in range(2):
                    act.wait_ge(S("h2tok_tr"), 2 * tt + half + 1)
                    act.activation(h2tok[:, tt, half * 512:(half + 1) * 512], bank[4 + 2 * tt + half][:, :], ACT.Copy)\
                       .then_inc(S("h2tok"), 1)

            def key_scores_out(h):
                act.wait_ge(S("key_scores"), h + 1)
                act.activation(scores_tok[:, :, h * 256:(h + 1) * 256], bank[2 + h % 2][:, :], ACT.Copy)\
                   .then_inc(S("key_scores_read"), 1)
            for h in range(PEER_HEADS + 1):
                if h < PEER_HEADS:
                    hi.upto(QRY + h + 2)
                    b, free = evac_ready(act, QRY + h)
                    if h >= 2:
                        act.wait_ge(S("key_scores"), h - 1)
                    act.activation(query[:, h % 2], b[:, :], ACT.Copy).then_inc(S("query"), 1)
                    act.wait_ge(S("query"), h + 1)
                    act.sem_inc(free, 1)
                if h >= 1:
                    key_scores_out(h - 1)
            hi.upto(QRY + 9)
            for tt in range(TT):
                if tt == 0:
                    gate_exp(act, 0)
                act.wait_ge(S(f"row_used{RROWS - 1}"), PER * (2 * tt + 1))
                act.activation(dots[:, tt * P:(tt + 1) * P], dots[:, tt * P:(tt + 1) * P], ACT.Gelu)\
                   .then_inc(S("gelu"), 1)
                act.wait_ge(S("v_coef"), tt + 1)
                for s0, s1, mine in V_SHARES[tt]:
                    own = [s for s in range(RROWS) if s not in mine]
                    with act.Fori(s0, s1) as it:
                        use = it + PER * (2 * tt + 1)
                        for s in own:
                            act.wait_ge(S(f"row_used{s}"), use)
                            act.activation(diag[:, s, :], ident[:, :], ACT.Copy,
                                           scale=dots[:, bass.ds(it * RROWS + (tt * P + s), 1)]).then_inc(S("diag"), 1)
                    if tt == 0 and s0 == 0:
                        gate_exp(act, 1)
            act.wait_ge(S("experts"), 2)
            act.dma_start(final_gain, A["final_g"].partition_broadcast(P)).then_inc(S("final_gain"), 16)
            for tt in range(TT):
                act.wait_ge(S("peer_x"), tt + 1)
                act.activation(v_acc[:, tt, :], x[:, tt, :], ACT.Square, accum_out=stat[:, 8 + tt:9 + tt])\
                   .then_inc(S("final_ss"), 1)

        def gate_exp(act, tt):
            act.wait_ge(S("gate_shifted"), tt + 1)
            act.activation(gates[:, tt, :], gates[:, tt, :], ACT.Exp).then_inc(S("gate_exp"), 1)

        def peer_pool(pool):
            norm_pool(pool, 1)
            ring = [s for s in range(RROWS)]

            def gather(table, tt, ph, it, half):
                use = it * 2 + (PER * ph + half)
                if not (isinstance(use, int) and use < 2):
                    for s in ring:
                        pool.wait_ge(S(f"row{s}"), use * 16 - 16)
                staged = stage[:, half * RROWS:(half + 1) * RROWS]
                pool.tensor_copy(staged, expert[:, bass.ds(it * 2 * RROWS + (tt * P + half * RROWS), RROWS)])\
                    .then_inc(S("staged"), 1)
                copies = pool.to_reg(use + 1)
                for s in ring:
                    pool.wait_ge(S("experts"), tt + 1)
                    if s == 0:
                        pool.wait_ge(S("staged"), copies)
                    if not (isinstance(use, int) and use < 1):
                        pool.wait_ge(S(f"row_used{s}"), use)
                    pool.indirect_dma_start(ring_rows[s], None, table,
                                            bass.IndirectOffsetOnAxis(ap=staged[:, s:s + 1], axis=0))\
                        .then_inc(S(f"row{s}"), 16)
            for tt in range(TT):
                pool.wait_ge(S("experts"), tt + 1)
                for q, table in enumerate((A["peer_u"][0], A["peer_v"][0])):
                    ph, first = 2 * tt + q, 0
                    if ph == 0:
                        for half in range(2):
                            gather(table, tt, ph, 0, half)
                        first = 1
                    with pool.Fori(first, PER // 2) as it:
                        for half in range(2):
                            gather(table, tt, ph, it, half)
            pool.wait_ge(S("final_ss"), TT)
            pool.tensor_scalar(stat[:, 10:12], stat[:, 8:10], 1.0 / D, EPS, ALU.mult, ALU.add).then_inc(S("final_ms"), 1)
            pool.wait_ge(S("final_ms"), 1)
            pool.tensor_tensor(stat[:, 12:14], stat[:, 10:12], stat[:, 6:8], ALU.pow).then_inc(S("final_rstd"), 1)

        def top_experts(dve, o, tt):
            def top16(values, tops, indices):
                n = range(len(values))
                for b in range(2):
                    part = slice(8 * b, 8 * b + 8)
                    for i in n:
                        o(dve.max(tops[i][:, part], values[i]))
                    o.wait()
                    for i in n:
                        o(dve.max_index(indices[i][:, part], tops[i][:, part], values[i]))
                    o.wait()
                    if b == 0:
                        for i in n:
                            o(dve.match_replace(values[i], tops[i][:, part], values[i], -3e38))
                        o.wait()
            pairs = [(h, i) for h in range(PEER_HEADS) for i in range(2)]
            top16([scores_tok[:, tt, (2 * h + i) * NKEYS:(2 * h + i + 1) * NKEYS] for h, i in pairs],
                  [half_s[:, tt, h, i, :] for h, i in pairs], [half_i[:, tt, h, i, :] for h, i in pairs])
            o(dve.tensor_copy(half_if[:, tt], half_i[:, tt]))
            o(dve.tensor_tensor(cand.rearrange("p h (i j) -> p h i j", j=TOPK),
                                half_s[:, tt, :, 0, :].unsqueeze(3).to_broadcast([P, PEER_HEADS, TOPK, TOPK]),
                                half_s[:, tt, :, 1, :].unsqueeze(2).to_broadcast([P, PEER_HEADS, TOPK, TOPK]), ALU.add))
            o.wait()
            heads = range(PEER_HEADS)
            top16([cand[:, h, :] for h in heads], [top_s[:, tt, h * TOPK:(h + 1) * TOPK] for h in heads],
                  [sel[:, tt, h * TOPK:(h + 1) * TOPK] for h in heads])
            best = top_s[:, tt, :].rearrange("p (h k) -> p h k", k=TOPK)
            dve.tensor_tensor(gates[:, tt, :].rearrange("p (h k) -> p h k", k=TOPK), best,
                              best[:, :, 0:1].to_broadcast([P, PEER_HEADS, TOPK]), ALU.subtract)\
               .then_inc(S("gate_shifted"), 1)
            su = [p.bitcast(U32) for p in sel_part]
            o(dve.tensor_scalar(su[0], sel[:, tt, :], 4, None, ALU.logical_shift_right))
            o(dve.tensor_scalar(su[1], sel[:, tt, :], 15, None, ALU.bitwise_and))
            o.wait()
            for i in range(2):
                o(dve.tensor_scalar(sel_key[i], su[i], 1.0, None, ALU.add))
            o.wait()
            for i in range(2):
                o(dve.tensor_copy(sel_part[i], sel_key[i]))
            o.wait()
            rank = small[:, 80:96].unsqueeze(1).unsqueeze(1).to_broadcast([P, 4, TOPK, TOPK])
            for i in range(2):
                for q in range(2):
                    picked = sel_part[i].rearrange("p (h k) -> p h k", k=TOPK)[:, 4 * q:4 * q + 4, :]
                    o(dve.tensor_tensor(one_hot, picked.unsqueeze(3).to_broadcast([P, 4, TOPK, TOPK]), rank, ALU.is_equal))
                    o.wait()
                    o(dve.tensor_tensor(one_hot, one_hot, half_if[:, tt, 4 * q:4 * q + 4, i, :].unsqueeze(2)
                                        .to_broadcast([P, 4, TOPK, TOPK]), ALU.mult))
                    o.wait()
                    o(dve.tensor_reduce(sel_key[i].rearrange("p (h k) -> p h k", k=TOPK)[:, 4 * q:4 * q + 4, :], one_hot,
                                        AXX, ALU.add))
                    o.wait()
            dve.scalar_tensor_tensor(out=expert[:, tt * P:(tt + 1) * P], in0=sel_key[0], scalar=float(NKEYS),
                                     in1=sel_key[1], op0=ALU.mult, op1=ALU.add).then_inc(S("experts"), 1)
            dve.wait_ge(S("gate_exp"), tt + 1)
            g3 = gates[:, tt, :].rearrange("p (h k) -> p h k", k=TOPK)
            o(dve.tensor_reduce(gate_sum[:, tt, :], g3, AXX, ALU.add))
            o.wait()
            o(dve.reciprocal(gate_sum[:, tt, :], gate_sum[:, tt, :]))
            o.wait()
            o(dve.tensor_tensor(g3, g3, gate_sum[:, tt, :].unsqueeze(2).to_broadcast([P, PEER_HEADS, TOPK]), ALU.mult))
            o.wait()

        def peer_dve(dve, lo, o):
            norm_dve(dve, 1, mod_gain(1), mod_shift(1))
            lo.upto(QRY + 9)
            dve.wait_ge(S("key_scores_read"), PEER_HEADS)
            for tt in range(TT):
                dve.memset(v_acc[:, tt, :], 0.0).then_inc(S("v_zero"), 1)
            top_experts(dve, o, 0)
            dve.wait_ge(S("h2tok"), 4)
            dve.wait_ge(S("v_open"), 1)
            for tt in range(TT):
                with dve.Fori(0, PER) as it:
                    use = it + PER * 2 * tt
                    for s in range(RROWS):
                        dve.wait_ge(S(f"row{s}"), use * 16 + 16)
                        dve.scalar_tensor_tensor(out=ring_rows[s], in0=ring_rows[s], scalar=1.0, in1=h2tok[:, tt, :],
                                                 op0=ALU.mult, op1=ALU.mult,
                                                 accum_out=dots[:, bass.ds(it * RROWS + (tt * P + s), 1)])\
                           .then_inc(S(f"row_used{s}"), 1)
                dve.wait_ge(S("gelu"), tt + 1)
                dve.tensor_tensor(dots[:, tt * P:(tt + 1) * P], dots[:, tt * P:(tt + 1) * P], gates[:, tt, :], ALU.mult)\
                   .then_inc(S("v_coef"), 1)
                if tt == 0:
                    top_experts(dve, o, 1)
                dve.wait_ge(S("v_coef"), tt + 1)
                for s0, s1, mine in V_SHARES[tt]:
                    if not mine:
                        continue
                    with dve.Fori(s0, s1) as it:
                        use = it + PER * (2 * tt + 1)
                        for i, s in enumerate(mine):
                            dve.wait_ge(S(f"row{s}"), use * 16 + 16)
                            dve.wait_ge(S(f"row_used{mine[i - 1]}"), use + min(i, 1))
                            dve.scalar_tensor_tensor(out=v_acc[:, tt, :], in0=ring_rows[s],
                                                     scalar=dots[:, bass.ds(it * RROWS + (tt * P + s), 1)],
                                                     in1=v_acc[:, tt, :], op0=ALU.mult, op1=ALU.add)\
                               .then_inc(S(f"row_used{s}"), 1)
            for tt in range(TT):
                for s in (RROWS - 1, V_SHARES[tt][-1][2][-1]):
                    dve.wait_ge(S(f"row_used{s}"), PER * (2 * tt + 2))
                for half in range(2):
                    part = slice(half * 512, (half + 1) * 512)
                    o(dve.tensor_tensor(v_acc[:, tt, part], v_acc[:, tt, part], bank[4 + 2 * tt + half][:, :], ALU.add))
                o.wait()
                o(dve.tensor_tensor(v_acc[:, tt, :], v_acc[:, tt, :], gt2, ALU.mult))
                o.wait()
                dve.tensor_tensor(x[:, tt, :], x[:, tt, :], v_acc[:, tt, :], ALU.add).then_inc(S("peer_x"), 1)
            dve.wait_ge(S("final_rstd"), 1)
            dve.wait_ge(S("final_gain"), 16)
            for tt in range(TT):
                dve.scalar_tensor_tensor(out=x[:, tt, :], in0=x[:, tt, :], scalar=stat[:, 12 + tt:13 + tt], in1=final_gain,
                                         op0=ALU.mult, op1=ALU.mult).then_inc(S("x_ready"), 1)

        RKV = BASE["rkv"]
        dx, gate_fm = fm(bigs(0)), fm(bigs(0))
        mixed = [fm(bigs(1)), fm(bigs(2))]
        rT, kkT, keyT, vrw, sig, aT = fm(bigs(3)), fm(bigs(1)), fm(bigs(4)), tm(bigs(5)), fm(bigs(6)), fm(bigs(7))
        scratch = fm(bigs(2))
        lw1 = aux[:, 0:512].rearrange("p (k c) -> p k c", k=KT)
        la1 = aux[:, 512:1024].rearrange("p (k c) -> p k c", k=KT)
        lg1 = aux[:, 1024:2304].rearrange("p (k c) -> p k c", k=KT)
        lw2, la2 = aux[0:LORA, 2304:3328], aux[LORA:2 * LORA, 2304:3328]
        lg2 = [aux[:, 3328:4352], aux[0:LORA_G - P, 4352:5376]]
        mid_w, mid_a = amask[0:LORA, 0:T], amask[LORA:2 * LORA, 0:T]
        mid_g = [big[:, SLOTW:SLOTW + T], big[0:LORA_G - P, SLOTW + T:SLOTW + 2 * T]]
        tile_mid = small[:, 128:144]
        y_stat, y_mean, bonus = small[:, 144:176], small[:, 176:208], small[:, 208:240]
        carry = small[:, 240:248]
        one_minus_ka = small[:, 248:256]
        flat = "p k t -> p (k t)"
        tok_bk = bigs(6)
        y_tok = hf[:, :, :].rearrange(flat)

        def head_groups(tile2048):
            return tile2048.rearrange("p (g c) -> p g c", c=DH)

        mats = [[aux[:, 512 * i:512 * (i + 1)] for i in range(7)],
                [aux[:, 3584 + 512 * i:3584 + 512 * (i + 1)] for i in range(5)]
                + [big[:, 2 * SLOTW + 512 * i:2 * SLOTW + 512 * (i + 1)] for i in range(2)]]
        vecs = [[big[:, 2 * SLOTW + 1024 + 256 * (2 * g + i):2 * SLOTW + 1024 + 256 * (2 * g + i + 1)] for i in range(2)]
                for g in range(2)]
        state = [aux[:, 6144:6400].rearrange("p (k c) -> p k c", c=DH), amask[:, 0:256].rearrange("p (k c) -> p k c", c=DH)]
        PAIRS = [(tt, qq) for tt in range(TT) for qq in range(2)]
        STAGES = 11
        ACT_STAGES = [1, 2, 3, 5, 6, 7, 10]

        def event(pr, st, g):
            return (pr * STAGES + st) * 2 + g + 1

        def dve_event(pr, st, g):
            return event(pr, st, g) - 2 * max(0, pr - 2)

        def act_event(pr, st, g):
            return (pr * len(ACT_STAGES) + ACT_STAGES.index(st)) * 2 + g + 1

        def masks_pool(pool):
            o = pool_order[0]
            for m in (low16, low_far, up16, up_strict, up_incl, head_ones[:, :], half_ones[:, :]):
                o(pool.memset(m, 1.0))
            o.wait()

            def keep(m, pattern, base, mult, op):
                o(pool.affine_select(out=m, in_=m, compare_op=op, fill=0.0, base=base, pattern=pattern,
                                     channel_multiplier=mult))
                o.wait()
            start, end = [[-16, 8], [0, 16]], [[16, 8], [0, 16]]
            keep(low16, start, 0, 1, ALU.is_ge)
            keep(low16, end, 15, -1, ALU.is_ge)
            keep(low16, [[-1, P]], 0, 1, ALU.is_gt)
            keep(low_far, start, -16, 1, ALU.is_ge)
            keep(up16, start, 0, 1, ALU.is_ge)
            keep(up16, end, 15, -1, ALU.is_ge)
            keep(up16, [[1, P]], 0, -1, ALU.is_gt)
            keep(up_strict, [[1, P]], 0, -1, ALU.is_gt)
            keep(up_incl, [[1, P]], 0, -1, ALU.is_ge)
            keep(head_ones[:, :], [[-DH, 2], [0, DH]], 0, 1, ALU.is_ge)
            keep(head_ones[:, :], [[DH, 2], [0, DH]], DH - 1, -1, ALU.is_ge)
            keep(half_ones[:, :], [[-DH, 2]], 0, 1, ALU.is_ge)
            pool.affine_select(out=half_ones[:, :], in_=half_ones[:, :], compare_op=ALU.is_ge, fill=0.0, base=DH - 1,
                               pattern=[[DH, 2]], channel_multiplier=-1).then_inc(S("masks"), 1)

        def lora_loads(act):
            act.wait_ge(S("x_ready"), XREADY[2])
            for dst, src in ((lw1, A["rwkv_w1_2"][0].rearrange("(k p) c -> p k c", p=P)),
                             (la1, A["rwkv_a1_2"][0].rearrange("(k p) c -> p k c", p=P)),
                             (lg1, A["rwkv_g1_2"][0].rearrange("(k p) c -> p k c", p=P)),
                             (lw2, A["rwkv_w2_2"][0]), (la2, A["rwkv_a2_2"][0]),
                             (lg2[0], A["rwkv_g2_2"][0, 0:P]), (lg2[1], A["rwkv_g2_2"][0, P:LORA_G])):
                act.dma_start(dst, src).then_inc(S("lora_w"), 16)

        def rwkv_pe(pe):
            norm_pe(pe, 3)
            for m, name in enumerate(("mix_r", "mix_k", "mix_v")):
                pe.wait_ge(S("act_split"), SPLITS[name])
                for n in range(RKV + 4 * m, RKV + 4 * m + 4):
                    project(pe, n, hh, hl, "T" if m == 2 else "F")
            pe.wait_ge(S("lora_w"), 16 * 7)
            for m, (w, o_) in enumerate(((lw1, bank[2][0:LORA, 0:T]), (la1, bank[3][LORA:2 * LORA, 0:T]))):
                pe.wait_ge(S("mixed"), 4 + m)
                for k in range(KT):
                    mm = pe.matmul(o_, w[:, k, :], mixed[(3 + m) % 2][:, k, :], start=(k == 0), stop=(k == KT - 1))
                mm.then_inc(S("lora_mid"), 1)
            pe.wait_ge(S("mixed"), 6)
            for b, c0, c1 in ((6, 0, P), (7, P, LORA_G)):
                for k in range(KT):
                    mm = pe.matmul(bank[b][0:c1 - c0, 0:T], lg1[:, k, c0:c1], mixed[1][:, k, :],
                                   start=(k == 0), stop=(k == KT - 1))
            mm.then_inc(S("lora_mid"), 1)
            for m in range(3):
                pe.wait_ge(S("lora_act"), m + 1)
                for kp in range(4):
                    q = 4 * m + kp
                    if q >= 2:
                        pe.wait_ge(S("lora_out_read"), q - 1)
                    for k in (2 * kp, 2 * kp + 1):
                        o_ = bank[4 + q % 2][:, (k % 2) * T:(k % 2 + 1) * T]
                        cols = slice(k * P, (k + 1) * P)
                        if m < 2:
                            mm = pe.matmul(o_, (lw2, la2)[m][:, cols], (mid_w, mid_a)[m], start=True, stop=True)
                        else:
                            pe.matmul(o_, lg2[0][:, cols], mid_g[0], start=True, stop=False)
                            mm = pe.matmul(o_, lg2[1][:, cols], mid_g[1], start=False, stop=True)
                    mm.then_inc(S("lora_out"), 1)
            pe.wait_ge(S("masks"), 1)
            pe.wait_ge(S("kk_square"), 1)
            pe.wait_ge(S("lora_out_read"), 12)
            for kp in range(4):
                pe.matmul(bank[4 + kp][:, :], head_ones[:, :], hf[:, 2 * kp:2 * kp + 2, :], start=True, stop=True)\
                  .then_inc(S("kk_norm"), 1)
            pe.wait_ge(S("bonus_rk"), 1)
            for tt in range(TT):
                for k in range(KT):
                    mm = pe.matmul(bank[2][:, tt * HEADS + 2 * k:tt * HEADS + 2 * k + 2],
                                   scratch[:, k, tt * P:(tt + 1) * P], half_ones[:, :], start=True, stop=True)
            mm.then_inc(S("bonus_sum"), 1)
            pe.wait_ge(S("wkv_in"), 3)
            pe.wait_ge(S("kk_read"), 4)
            for w, src in enumerate((aT, keyT)):
                for half in range(2):
                    for j in range(4):
                        mm = pe.transpose(bank[4 + 2 * w + half][:, j * P:(j + 1) * P], src[:, 4 * half + j, 0:P],
                                          ident[:, :])
                    mm.then_inc(S("bk_turned"), 1)
            pe.wait_ge(S("bk_tok"), 4)
            pe.wait_ge(S("bonus_read"), 1)
            for b in range(2):
                pe.wait_ge(S(f"proj_free{b}"), (projection_number(RKV + 12) + 1 - b) // 2)
            for pr, (tt, qq) in enumerate(PAIRS):
                for st in range(STAGES):
                    for g in range(2):
                        wkv_stage(pe, pr, tt, qq, st, g)
            pe.wait_ge(S("mix_normed"), 1)
            pe.wait_ge(S("bonus_v"), 1)
            for kp in range(4):
                for b, src in ((4 + kp, y_tok), (kp, bigs(5))):
                    for k in (2 * kp, 2 * kp + 1):
                        for tt in range(TT):
                            mm = pe.transpose(bank[b][:, (k % 2) * T + tt * P:(k % 2) * T + (tt + 1) * P],
                                              src[:, tt * D + k * P:tt * D + (k + 1) * P], ident[:, :])
                mm.then_inc(S("mix_turned"), 1)
            pe.wait_ge(S("act_split"), SPLITS["rwkv_y"])
            for n in range(BASE["rwkv_o"], BASE["rwkv_o"] + 4):
                project(pe, n, hh, hl, "T")

        def wkv_stage(pe, pr, tt, qq, st, g):
            b = bank[4 * g:4 * g + 4]
            mD, mDt, mD2, mD2t, mT, mE, mK = mats[g]
            xin, u = vecs[g]
            if st > 0 or pr > 0:
                prev = (pr, st - 1) if st else (pr - 1, STAGES - 1)
                if not (prev[1] == STAGES - 1 and prev[0] >= 2):
                    pe.wait_ge(S("wkv_dve"), dve_event(*prev, g))
                if prev[1] in ACT_STAGES:
                    pe.wait_ge(S("wkv_act"), act_event(*prev, g))
            tok = slice(tt * P, (tt + 1) * P)
            for i in range(4):
                h, k = 8 * qq + 2 * i + g, 4 * qq + i
                ch = slice(g * DH, (g + 1) * DH)
                al, be, ka, rh = (t[ch, k, tok] for t in (kkT, aT, keyT, rT))
                v = vrw[:, tt, h * DH:(h + 1) * DH]
                s_in = state[qq][ch, i, :]
                c = slice(i * P, (i + 1) * P)
                d = slice(i * DH, (i + 1) * DH)

                def mul(bk, cols, lhsT, rhs, start=True, stop=True):
                    return pe.matmul(b[bk][:, cols], lhsT, rhs, start=start, stop=stop)
                if st == 0:
                    mul(0, c, al, be)
                    mul(1, c, be, al)
                    mm = mul(2, c, ka, al)
                elif st == 1:
                    mul(0, c, mDt[:, c], mD[:, c])
                    mm = mul(1, c, mD[:, c], mDt[:, c])
                elif st == 2:
                    mul(0, c, mD2t[:, c], mD2[:, c])
                    mul(1, c, mD2[:, c], mD2t[:, c])
                    mm = mul(2, c, mD2[:, c], mT[:, c])
                elif st == 3:
                    mul(0, c, mDt[:, c], mD[:, c])
                    mm = mul(1, c, mD[:, c], mT[:, c])
                elif st == 4:
                    mm = mul(0, c, mD2[:, c], mT[:, c])
                elif st == 5:
                    mul(0, c, mT[:, c], mE[:, c])
                    mul(1, c, mE[:, c], mT[:, c])
                    mm = mul(2, d, mK[:, c], v, stop=(tt == 0))
                    if tt:
                        mm = mul(2, d, al, s_in, start=False)
                elif st == 6:
                    mul(0, c, mD[:, c], mD2t[:, c])
                    mul(1, c, mD2t[:, c], mD[:, c])
                    mul(2, d, mT[:, c], xin[:, d])
                    mm = mul(3, c, be, rh)
                elif st == 7:
                    mul(0, c, mE[:, c], mDt[:, c])
                    mul(1, d, mD[:, c], u[:, d])
                    mm = mul(3, c, ka, rh)
                elif st == 8:
                    mm = mul(0, d, mDt[:, c], u[:, d])
                elif st == 9:
                    mm = mul(0, d, mD2[:, c], u[:, d])
                else:
                    mul(0, d, mK[:, c], u[:, d], stop=False)
                    mm = mul(0, d, mD2t[:, c], v, start=False, stop=(tt == 0))
                    if tt:
                        mm = mul(0, d, rh, s_in, start=False)
                    else:
                        o_ = b[1][ch, d]
                        pe.matmul(o_, tok_bk[:, h * DH:(h + 1) * DH], u[:, d], start=True, stop=False)
                        mm = pe.matmul(o_, tok_bk[:, D + h * DH:D + (h + 1) * DH], v, start=False, stop=True)
            mm.then_inc(S("wkv_mm"), 1)

        def wkv_act(act):
            for pr, (tt, qq) in enumerate(PAIRS):
                for st in ACT_STAGES:
                    for g in range(2):
                        b = bank[4 * g:4 * g + 4]
                        mD, mDt, mD2, mD2t, mT, mE, mK = mats[g]
                        xin, u = vecs[g]
                        act.wait_ge(S("wkv_mm"), event(pr, st, g))
                        y_group = y_tok[:, tt * D + qq * 512:tt * D + (qq + 1) * 512]\
                            .rearrange("p (i g c) -> p i g c", g=2, c=DH)[:, :, g, :]
                        y_bank = b[0][:, 0:T].rearrange("p (i c) -> p i c", c=DH)
                        moves = {1: [(mD2, b[0][:, :])], 2: [(mD, b[0][:, :])], 3: [(mD2, b[0][:, :])],
                                 5: [(mD2t, b[0][:, :]), (xin, b[2][:, 0:T])], 6: [(mE, b[0][:, :]), (u, b[2][:, 0:T])],
                                 7: [(mD2, b[0][:, :])],
                                 10: [(y_group, y_bank)]}[st]
                        for dst, src in moves:
                            a = act.activation(dst, src, ACT.Copy)
                        a.then_inc(S("wkv_act"), 1)

        def wkv_dve(dve):
            def heads(m):
                return m.rearrange("p (h n) -> p h n", h=4)

            def each(mask):
                return mask.unsqueeze(1).to_broadcast([P, 4, P])
            for pr, (tt, qq) in enumerate(PAIRS):
                for st in range(STAGES):
                    for g in range(2):
                        b = [x_[:, :] for x_ in bank[4 * g:4 * g + 4]]
                        mD, mDt, mD2, mD2t, mT, mE, mK = mats[g]
                        xin, u = vecs[g]
                        ch = slice(g * DH, (g + 1) * DH)
                        if st == STAGES - 1 and tt == TT - 1:
                            continue
                        dve.wait_ge(S("wkv_mm"), event(pr, st, g))
                        if st == 0:
                            dve.tensor_tensor(heads(mDt), heads(b[1]), each(up16), ALU.mult).then_inc(S("wkv_dt"), 1)
                            dve.tensor_tensor(heads(mD), heads(b[0]), each(low16), ALU.mult)
                            dve.tensor_tensor(heads(mE), heads(b[0]), each(low_far), ALU.mult)
                            dve.tensor_tensor(heads(mK), heads(b[2]), each(up_strict), ALU.mult)
                            dve.wait_ge(S("wkv_dt"), 2 * pr + g + 1)
                            v = dve.tensor_tensor(heads(mT), heads(mDt), each(ident[:, :]), ALU.add)
                        elif st == 1:
                            v = dve.tensor_copy(mD2t, b[1])
                        elif st == 2:
                            dve.tensor_copy(mDt, b[1])
                            v = dve.tensor_tensor(mT, mT, b[2], ALU.add)
                        elif st == 3:
                            v = dve.tensor_tensor(mT, mT, b[1], ALU.add)
                        elif st == 4:
                            v = dve.tensor_tensor(mT, mT, b[0], ALU.add)
                        elif st == 5:
                            v = dve.tensor_copy(mD, b[1])
                        elif st == 6:
                            dve.tensor_copy(mDt, b[1])
                            v = dve.tensor_tensor(heads(mK), heads(b[3]), each(up_incl), ALU.mult)
                        elif st == 7:
                            dve.tensor_tensor(heads(mD2t), heads(b[3]), each(up_incl), ALU.mult)
                            v = dve.tensor_tensor(u, u, b[1][:, 0:T], ALU.add)
                        elif st in (8, 9):
                            v = dve.tensor_tensor(u, u, b[0][:, 0:T], ALU.add)
                        else:
                            carried = carry[ch, 4 * qq:4 * qq + 4].unsqueeze(2).to_broadcast([DH, 4, DH])
                            v = dve.tensor_tensor(state[qq][ch, :, :], b[1][ch, 0:T].rearrange("p (i c) -> p i c", c=DH),
                                                  carried, ALU.mult)
                        v.then_inc(S("wkv_dve"), 1)

        def rwkv_act(act, hi):
            norm_act(act, 3, hi)
            for m in range(3):
                act.wait_ge(S("mixed"), m + 1)
                act.wait_ge(S("slot_done"), RKV + 4 * m)
                act.activation(hh[:, :, :], mixed[m % 2], ACT.Copy).then_inc(S("mix_hi"), 1)
                for n in range(RKV + 4 * m, RKV + 4 * m + 4):
                    hi.upto(n + 2)
                    if m < 2:
                        b, free = evac_ready(act, n)
                        j = 2 * (n - RKV - 4 * m)
                        act.activation((rT, keyT)[m][:, j:j + 2, :], b[:, :], ACT.Copy).then_inc(free, 1)
            act.wait_ge(S("lora_mid"), 1)
            act.activation(mid_w, bank[2][0:LORA, 0:T], ACT.Tanh).then_inc(S("lora_act"), 1)
            act.wait_ge(S("lora_mid"), 2)
            act.activation(mid_a, bank[3][LORA:2 * LORA, 0:T], ACT.Copy).then_inc(S("lora_act"), 1)
            act.wait_ge(S("lora_mid"), 3)
            act.activation(mid_g[0], bank[6][:, 0:T], ACT.Sigmoid)
            act.activation(mid_g[1], bank[7][0:LORA_G - P, 0:T], ACT.Sigmoid).then_inc(S("lora_act"), 1)
            for q in range(12):
                m, kp = q // 4, q % 4
                act.wait_ge(S("lora_out"), q + 1)
                for k in (2 * kp, 2 * kp + 1):
                    src = bank[4 + q % 2][:, (k % 2) * T:(k % 2 + 1) * T]
                    if m == 2:
                        a = act.activation(gate_fm[:, k, :], src, ACT.Copy)
                    else:
                        a = act.activation((sig, aT)[m][:, k, :], src, ACT.Sigmoid, bias=col(("w0", "a0")[m], k))
                a.then_inc(S("lora_out_read"), 1)
            for k in range(KT):
                a = act.activation(kkT[:, k, :], keyT[:, k, :], ACT.Copy, scale=col("k_k", k))
            a.then_inc(S("kk"), 1)
            act.wait_ge(S("kk"), 1)
            act.activation(hf[:, :, :], kkT, ACT.Square).then_inc(S("kk_square"), 1)
            act.wait_ge(S("one_minus_ka"), 1)
            for k in range(KT):
                a = act.activation(scratch[:, k, :], aT[:, k, :], ACT.Identity, scale=col("k_a", k),
                                   bias=one_minus_ka[:, k:k + 1])
            a.then_inc(S("key_factor"), 1)
            act.wait_ge(S("kk_read"), 4)
            act.activation(hf[:, :, :], hf[:, :, :], ACT.Sqrt).then_inc(S("kk_root"), 1)
            act.wait_ge(S("decay_sums"), 1)
            act.wait_ge(S("bonus_sum"), 1)
            act.activation(scratch, hf[:, :, :], ACT.Exp, scale=DECAY).then_inc(S("decays"), 1)
            act.wait_ge(S("decays"), 1)
            act.activation(carry, carry, ACT.Exp, scale=-DECAY)
            act.activation(hf[:, :, :], hf[:, :, :], ACT.Exp, scale=-DECAY).then_inc(S("decays"), 1)
            act.activation(sig, sig, ACT.Exp, scale=-DECAY).then_inc(S("decays"), 1)
            act.wait_ge(S("wkv_in"), 4)
            for j in range(4):
                act.wait_ge(S("bk_turned"), j + 1)
                act.activation(tok_bk[:, j * 512:(j + 1) * 512], bank[4 + j][:, :], ACT.Copy).then_inc(S("bk_tok"), 1)
            wkv_act(act)
            act.wait_ge(S("y_centred"), 1)
            act.activation(bigs(2), y_tok, ACT.Square).then_inc(S("y_square"), 1)
            act.wait_ge(S("mix_normed"), 1)
            for kp in range(4):
                act.wait_ge(S("mix_turned"), kp + 1)
                for k in (2 * kp, 2 * kp + 1):
                    a = act.activation(scratch[:, k, :], bank[4 + kp][:, (k % 2) * T:(k % 2 + 1) * T], ACT.Identity,
                                       scale=col("ln_g", k), bias=col("ln_b", k))
                a.then_inc(S("y_affine"), 1)
            act.wait_ge(S("mix_scaled"), 4)
            act.activation(hh[:, :, :], scratch, ACT.Copy).then_inc(S("mix_out_hi"), 1)
            hi.upto(BASE["rwkv_o"] + 5)

        def rwkv_dve(dve, lo, o):
            norm_dve(dve, 3, lambda k: col("mix0", k))
            dve.wait_ge(S("norm_hf"), 16)
            o(dve.tensor_scalar(dx[:, :, 0:1], hf[:, :, 0:1], -1.0, None, ALU.mult))
            o(dve.tensor_tensor(dx[:, :, 1:T], hf[:, :, 0:T - 1], hf[:, :, 1:T], ALU.subtract))
            o.wait()

            def mix(m):
                if m in (2, 3):
                    dve.wait_ge(S("act_split"), SPLITS[("mix_r", "mix_k")[m - 2]])
                if m == 4:
                    dve.wait_ge(S("act_split"), SPLITS["mix_v"])
                if m == 5:
                    dve.wait_ge(S("lora_mid"), 1)
                for k in range(KT):
                    v = dve.scalar_tensor_tensor(out=mixed[m % 2][:, k, :], in0=dx[:, k, :], scalar=col(f"mu{m}", k),
                                                 in1=hf[:, k, :], op0=ALU.mult, op1=ALU.add)
                v.then_inc(S("mixed"), 1)

            def rest(m):
                dve.wait_ge(S("mix_hi"), m + 1)
                dve.tensor_tensor(hl[:, :, :], mixed[m % 2], hh[:, :, :].bitcast(F32), ALU.subtract)\
                   .then_inc(S("act_split"), 1)
            mix(0)
            rest(0)
            for m in range(3):
                mix(m + 1)
                for n in range(RKV + 4 * m, RKV + 4 * m + 4):
                    lo.upto(n + 2)
                    if m == 2:
                        b, free = evac_ready(dve, n)
                        j = n - RKV - 8
                        dve.tensor_copy(vrw[:, :, j * CW:(j + 1) * CW], b[:, :].rearrange("p (a c) -> p a c", a=TT))\
                           .then_inc(free, 1)
                if m < 2:
                    rest(m + 1)
            mix(4)
            mix(5)
            dve.tensor_scalar(one_minus_ka, vec[:, COL["k_a"]:COL["k_a"] + KT], -1.0, 1.0, ALU.mult, ALU.add)\
               .then_inc(S("one_minus_ka"), 1)
            dve.wait_ge(S("key_factor"), 1)
            o(dve.tensor_tensor(keyT, keyT, scratch, ALU.mult))
            o.wait()
            for k in range(KT):
                v = dve.scalar_tensor_tensor(out=scratch[:, k, :], in0=rT[:, k, :], scalar=col("r_k", k),
                                             in1=keyT[:, k, :], op0=ALU.mult, op1=ALU.mult)
            v.then_inc(S("bonus_rk"), 1)
            for kp in range(4):
                dve.wait_ge(S("kk_norm"), 4)
                dve.tensor_scalar(hf[:, 2 * kp:2 * kp + 2, :], bank[4 + kp][:, :].rearrange("p (a t) -> p a t", a=2),
                                  1e-24, None, ALU.max).then_inc(S("kk_read"), 1)
            dve.wait_ge(S("kk_root"), 1)
            o(dve.reciprocal(hf[:, :, :], hf[:, :, :]))
            o.wait()
            o(dve.tensor_tensor(kkT, kkT, hf[:, :, :], ALU.mult))
            dve.wait_ge(S("bonus_sum"), 1)
            dve.tensor_copy(bonus, bank[2][:, 0:2 * HEADS]).then_inc(S("bonus_read"), 1)
            o.wait()
            sums = hf[:, :, :].rearrange(flat)
            sig_flat = bigs(6)
            for j in range(KT * TT):
                o(dve.tensor_tensor_scan(sums[:, j * P:(j + 1) * P], ones[:, 0:P], sig_flat[:, j * P:(j + 1) * P], 0.0,
                                         ALU.mult, ALU.add))
            o(dve.tensor_tensor(aT, aT, kkT, ALU.mult))
            o.wait()
            tiles = sums.rearrange("p (j t) -> p j t", t=P)
            o(dve.tensor_copy(tile_mid.unsqueeze(2), tiles[:, :, P // 2 - 1:P // 2]))
            o.wait()
            o(dve.tensor_tensor(tiles, tiles, tile_mid.unsqueeze(2).to_broadcast([P, KT * TT, P]), ALU.subtract))
            o.wait()
            o(dve.tensor_tensor(sig_flat, sums, sig_flat, ALU.subtract))
            o(dve.tensor_tensor(carry.unsqueeze(2), tiles.rearrange("p (k a) t -> p k a t", a=TT)[:, :, 0, P - 1:P],
                                tile_mid.rearrange("p (k a) -> p k a", a=TT)[:, :, 1:2], ALU.add))
            o.wait()
            dve.sem_inc(S("decay_sums"), 1)
            dve.wait_ge(S("decays"), 1)
            dve.tensor_tensor(keyT, keyT, scratch, ALU.mult).then_inc(S("wkv_in"), 1)
            dve.tensor_tensor(aT, aT, scratch, ALU.mult).then_inc(S("wkv_in"), 1)
            dve.wait_ge(S("decays"), 2)
            dve.tensor_tensor(rT, rT, hf[:, :, :], ALU.mult).then_inc(S("wkv_in"), 1)
            dve.wait_ge(S("decays"), 3)
            dve.scalar_tensor_tensor(out=kkT, in0=kkT, scalar=-1.0, in1=sig, op0=ALU.mult, op1=ALU.mult)\
               .then_inc(S("wkv_in"), 1)
            wkv_dve(dve)
            dve.wait_ge(S("wkv_act"), act_event(len(PAIRS) - 1, STAGES - 1, 1))
            v3 = head_groups(bigs(5))
            dve.tensor_tensor(v3, v3, bonus.unsqueeze(2).to_broadcast([P, 2 * HEADS, DH]), ALU.mult)\
               .then_inc(S("bonus_v"), 1)
            y3 = head_groups(y_tok)
            o(dve.tensor_reduce(y_stat, y3, AXX, ALU.add))
            o.wait()
            o(dve.tensor_scalar(y_mean, y_stat, 1.0 / DH, None, ALU.mult))
            o.wait()
            dve.tensor_tensor(y3, y3, y_mean.unsqueeze(2).to_broadcast([P, 2 * HEADS, DH]), ALU.subtract)\
               .then_inc(S("y_centred"), 1)
            dve.wait_ge(S("y_square"), 1)
            dve.tensor_reduce(y_stat, head_groups(bigs(2)), AXX, ALU.add).then_inc(S("y_ss"), 1)
            dve.wait_ge(S("y_rstd"), 1)
            dve.tensor_tensor(y3, y3, y_stat.unsqueeze(2).to_broadcast([P, 2 * HEADS, DH]), ALU.mult)\
               .then_inc(S("mix_normed"), 1)
            for kp in range(4):
                dve.wait_ge(S("y_affine"), kp + 1)
                part = scratch[:, 2 * kp:2 * kp + 2, :]
                o(dve.tensor_tensor(part, part, bank[kp][:, :].rearrange("p (a t) -> p a t", a=2), ALU.add))
                o.wait()
                dve.tensor_tensor(part, part, gate_fm[:, 2 * kp:2 * kp + 2, :], ALU.mult).then_inc(S("mix_scaled"), 1)
            dve.wait_ge(S("mix_out_hi"), 1)
            dve.tensor_tensor(hl[:, :, :], scratch, hh[:, :, :].bitcast(F32), ALU.subtract).then_inc(S("act_split"), 1)
            residual(dve, lo, BASE["rwkv_o"])

        def rwkv_pool(pool):
            norm_pool(pool, 3)
            exponent = y_mean
            pool.wait_ge(S("y_ss"), 1)
            o = pool_order[0]
            o(pool.tensor_scalar(y_stat, y_stat, 1.0 / DH, RWKV_EPS, ALU.mult, ALU.add))
            o(pool.memset(exponent, -0.5))
            o.wait()
            pool.tensor_tensor(y_stat, y_stat, exponent, ALU.pow).then_inc(S("y_rstd"), 1)

        KV, DQ = BASE["kv"], BASE["diff_q"]
        k_sh, v_sh, q_df = fm(bigs(0)), tm(bigs(1)), fm(bigs(2))
        HEAD_NORMS = [(k_sh, fm(bigs(2)), fm(bigs(3))), (q_df, fm(bigs(3)), fm(bigs(4)))]

        def head_norm_pe(pe, i):
            squares = HEAD_NORMS[i][1]
            pe.wait_ge(S("head_squares"), i + 1)
            for kp in range(4):
                pe.matmul(bank[4 + kp][:, :], head_ones[:, :], squares[:, 2 * kp:2 * kp + 2, :], start=True, stop=True)\
                  .then_inc(S("head_sums"), 1)

        def head_norm_square(act, i, last_slot):
            for n in (last_slot - 1, last_slot):
                act.wait_ge(S(f"proj_free{projection_number(n) % 2}"), projection_number(n) // 2 + 1)
            act.activation(HEAD_NORMS[i][1], HEAD_NORMS[i][0], ACT.Square).then_inc(S("head_squares"), 1)

        def head_norm_root(act, i):
            root = HEAD_NORMS[i][2]
            act.wait_ge(S("head_ms"), 4 * (i + 1))
            act.activation(root, root, ACT.Sqrt).then_inc(S("head_root"), 1)

        def head_norm_dve(dve, o, i, gain):
            values, _, root = HEAD_NORMS[i]
            for kp in range(4):
                dve.wait_ge(S("head_sums"), 4 * i + kp + 1)
                dve.tensor_scalar(root[:, 2 * kp:2 * kp + 2, :], bank[4 + kp][:, :].rearrange("p (a t) -> p a t", a=2),
                                  1.0 / DH, EPS, ALU.mult, ALU.add).then_inc(S("head_ms"), 1)
            dve.wait_ge(S("head_root"), i + 1)
            o(dve.reciprocal(root, root))
            o.wait()
            dve.scalar_tensor_tensor(out=values, in0=values, scalar=gain, in1=root, op0=ALU.mult, op1=ALU.mult)\
               .then_inc(S("head_normed"), 1)

        def kv_pe(pe):
            norm_pe(pe, 5)
            pe.wait_ge(S("act_split"), SPLITS["norm5"])
            for j in range(8):
                project(pe, KV + j, hh, hl, "F" if j < 4 else "T")
                if j == 5:
                    head_norm_pe(pe, 0)

        def kv_act(act, hi):
            norm_act(act, 5, hi)
            for j in range(8):
                hi.upto(KV + j + 2)
                if j < 4:
                    b, free = evac_ready(act, KV + j)
                    act.activation(k_sh[:, 2 * j:2 * j + 2, :], b[:, :], ACT.Copy).then_inc(free, 1)
                if j == 3:
                    head_norm_square(act, 0, KV + 3)
            head_norm_root(act, 0)

        def kv_dve(dve, lo, o):
            norm_dve(dve, 5, lambda k: col("kv_norm", k))
            for j in range(8):
                lo.upto(KV + j + 2)
                if j >= 4:
                    b, free = evac_ready(dve, KV + j)
                    dve.tensor_copy(v_sh[:, :, (j - 4) * CW:(j - 3) * CW], b[:, :].rearrange("p (a c) -> p a c", a=TT))\
                       .then_inc(free, 1)
            head_norm_dve(dve, o, 0, col("k_norm", 0))

        df_s = big[:, 5 * SLOTW:5 * SLOTW + 4 * 384].rearrange("p (b c n) -> p b c n", b=2, c=2)
        df_pT = big[:, 6 * SLOTW:6 * SLOTW + 2 * 384].rearrange("p (b n) -> p b n", b=2)
        df_junk = big[:, 4 * SLOTW:4 * SLOTW + 2 * 2 * P].rearrange("p (b a n) -> p b a n", b=2, a=TT)
        o_tok = tm(bigs(7))
        q_gain, neg_lambda, subln_gain = small[:, 128:129], small[:, 129:130], small[:, 130:131]
        df_max, df_sum, df_inv = (small[:, 144 + 8 * i:152 + 8 * i].rearrange("p (b c a) -> p b c a", b=2, c=2)
                                  for i in range(3))
        df_coef = small[:, 168:172].rearrange("p (b a) -> p b a", b=2)
        o_ss, o_rstd, o_power = small[:, 176:192], small[:, 192:208], small[:, 208:224]
        lam_rows = aux[0:1, 0:4 * DH].rearrange("p (a b c) -> p a b c", a=2, b=2)
        lam_products = aux[0:1, 256:256 + 2 * DH].rearrange("p (a c) -> p a c", a=2)
        lam_exp, lam_row = aux[0:1, 384:386], aux[0:1, 386:387]
        distances = amask[:, :]

        def key_span(qt):
            return slice(P * qt, P * qt + P * (qt + 1))

        def distance_pool(pool):
            pool.wait_ge(S("x_ready"), XREADY[4])
            o = pool_order[0]
            for qt in range(TT):
                o(pool.iota(distances[:, key_span(qt)], pattern=[[1, P * (qt + 1)]], base=-P * qt, channel_multiplier=-1,
                            allow_small_or_imprecise_dtypes=True))
            o.wait()
            for c0 in (0, 2 * P):
                pool.affine_select(out=distances[:, c0:c0 + P], in_=distances[:, c0:c0 + P], compare_op=ALU.is_ge,
                                   fill=NEG, base=0, pattern=[[-1, P]], channel_multiplier=1)\
                    .then_inc(S("distances"), 1)

        def diff_pool(pool):
            norm_pool(pool, 7)
            o = pool_order[0]
            o(pool.memset(o_power, -0.5))
            pool.wait_ge(S("df_out"), DIFF_HEADS)
            o(pool.tensor_scalar(o_ss, o_ss, 1.0 / (2 * DH), SUBLN_EPS, ALU.mult, ALU.add))
            o.wait()
            pool.tensor_tensor(o_rstd, o_ss, o_power, ALU.pow).then_inc(S("o_rstd"), 1)

        def diff_pe(pe):
            norm_pe(pe, 7)
            pe.wait_ge(S("act_split"), SPLITS["norm7"])
            for n in range(DQ, DQ + 4):
                project(pe, n, hh, hl, "F")
            pe.wait_ge(S("lam_row"), 1)
            pe.matmul(bank[2][:, 0:1], ones[0:1, 0:P], lam_row, start=True, stop=True).then_inc(S("lam_column"), 1)
            head_norm_pe(pe, 1)
            pe.wait_ge(S("lam_read"), 1)
            pe.wait_ge(S("head_normed"), 2)

            def scores(h):
                for c in range(2):
                    if h >= 1:
                        pe.wait_ge(S("df_masked"), 2 * h - 1 + c)
                    ch = slice(DH * c, DH * (c + 1))
                    for qt in range(TT):
                        mm = pe.matmul(bank[2 + c][:, key_span(qt)], q_df[ch, h, qt * P:(qt + 1) * P],
                                       k_sh[ch, h, 0:P * (qt + 1)], start=True, stop=True)
                    mm.then_inc(S("df_scores"), 1)

            def turn(h):
                pe.wait_ge(S("df_attn"), h + 1)
                if h >= 2:
                    pe.wait_ge(S("df_pT"), h - 1)
                for j in range(3):
                    mm = pe.transpose(bank[4 + h % 2][:, j * P:(j + 1) * P], df_s[:, h % 2, 0, j * P:(j + 1) * P],
                                      ident[:, :])
                mm.then_inc(S("df_turned"), 1)

            def values(h):
                pe.wait_ge(S("df_pT"), h + 1)
                if h >= 2:
                    pe.wait_ge(S("df_out"), h - 1)
                for qt, j, kt in ((0, 0, 0), (1, 1, 0), (1, 2, 1)):
                    mm = pe.matmul(bank[6 + h % 2][:, qt * P:(qt + 1) * P], df_pT[:, h % 2, j * P:(j + 1) * P],
                                   v_sh[:, kt, h * P:(h + 1) * P], start=(kt == 0), stop=(kt == qt))
                mm.then_inc(S("df_pv"), 1)
            for h in range(DIFF_HEADS + 2):
                if h < DIFF_HEADS:
                    scores(h)
                if 1 <= h <= DIFF_HEADS:
                    turn(h - 1)
                if h >= 2:
                    values(h - 2)
            pe.wait_ge(S("mix_normed"), 2)
            for kp in range(4):
                for k in (2 * kp, 2 * kp + 1):
                    for tt in range(TT):
                        mm = pe.transpose(bank[4 + kp][:, (k % 2) * T + tt * P:(k % 2) * T + (tt + 1) * P],
                                          o_tok[:, tt, k * P:(k + 1) * P], ident[:, :])
                mm.then_inc(S("mix_turned"), 1)
            pe.wait_ge(S("act_split"), SPLITS["diff_y"])
            for n in range(BASE["diff_o"], BASE["diff_o"] + 4):
                project(pe, n, hh, hl, "T")

        def diff_act(act, hi):
            act.wait_ge(S("x_ready"), XREADY[4])
            act.dma_start(lam_rows, A["diff_lambda_2"].rearrange("o (a b) c -> o a b c", a=2)).then_inc(S("lam_loaded"), 16)
            norm_act(act, 7, hi)
            act.wait_ge(S("lam_sums"), 1)
            act.activation(lam_exp, lam_exp, ACT.Exp).then_inc(S("lam_exp"), 1)
            for j in range(4):
                hi.upto(DQ + j + 2)
                b, free = evac_ready(act, DQ + j)
                act.activation(q_df[:, 2 * j:2 * j + 2, :], b[:, :], ACT.Copy).then_inc(free, 1)
            head_norm_square(act, 1, DQ + 3)
            head_norm_root(act, 1)
            hi.upto(DQ + 6)

            def exps(h):
                for c in range(2):
                    act.wait_ge(S("df_max"), 2 * h + c + 1)
                    for qt in range(TT):
                        s = df_s[:, h % 2, c, key_span(qt)]
                        a = act.activation(s, s, ACT.Exp, bias=df_max[:, h % 2, c, qt:qt + 1],
                                           accum_out=df_sum[:, h % 2, c, qt:qt + 1])
                    a.then_inc(S("df_exp"), 1)

            def copy_out(h):
                act.wait_ge(S("df_turned"), h + 1)
                if h >= 2:
                    act.wait_ge(S("df_pv"), h - 1)
                act.activation(df_pT[:, h % 2, :], bank[4 + h % 2][:, 0:384], ACT.Copy).then_inc(S("df_pT"), 1)

            def outputs(h):
                act.wait_ge(S("df_pv"), h + 1)
                if h >= 2:
                    act.wait_ge(S("df_out"), h - 1)
                for qt in range(TT):
                    src, inv = bank[6 + h % 2][:, qt * P:(qt + 1) * P], df_inv[:, h % 2, 0, qt:qt + 1]
                    act.activation(o_tok[:, qt, h * P:(h + 1) * P], src, ACT.Copy, scale=inv)
                    a = act.activation(df_junk[:, h % 2, qt, :], src, ACT.Square, scale=inv,
                                       accum_out=o_ss[:, qt * DIFF_HEADS + h:qt * DIFF_HEADS + h + 1])
                a.then_inc(S("df_out"), 1)
            for h in range(DIFF_HEADS + 2):
                if h < DIFF_HEADS:
                    exps(h)
                if 1 <= h <= DIFF_HEADS:
                    copy_out(h - 1)
                if h >= 2:
                    outputs(h - 2)
            for kp in range(4):
                act.wait_ge(S("mix_scaled"), kp + 5)
                act.activation(hh[:, 2 * kp:2 * kp + 2, :], hf[:, 2 * kp:2 * kp + 2, :], ACT.Copy).then_inc(S("mix_out_hi"), 1)
            hi.upto(BASE["diff_o"] + 5)

        def diff_dve(dve, lo, o):
            o(dve.tensor_scalar(q_gain, col("q_norm", 0), DH ** -0.5, None, ALU.mult))
            o(dve.tensor_scalar(subln_gain, col("subln", 0), 1.0 - LAM_INIT, None, ALU.mult))
            dve.wait_ge(S("lam_loaded"), 16)
            o(dve.tensor_tensor(lam_products, lam_rows[:, :, 0, :], lam_rows[:, :, 1, :], ALU.mult))
            o.wait()
            dve.tensor_reduce(lam_exp, lam_products, AXX, ALU.add).then_inc(S("lam_sums"), 1)
            norm_dve(dve, 7, lambda k: col("mix1", k))
            dve.wait_ge(S("lam_exp"), 1)
            dve.scalar_tensor_tensor(out=lam_row, in0=lam_exp[:, 1:2], scalar=-LAM_INIT, in1=lam_exp[:, 0:1],
                                     op0=ALU.add, op1=ALU.subtract).then_inc(S("lam_row"), 1)
            for j in range(4):
                lo.upto(DQ + j + 2)
            dve.wait_ge(S("lam_column"), 1)
            dve.tensor_copy(neg_lambda, bank[2][:, 0:1]).then_inc(S("lam_read"), 1)
            head_norm_dve(dve, o, 1, q_gain)
            lo.upto(DQ + 6)
            dve.wait_ge(S("distances"), 2)

            def mask_max(h):
                for c in range(2):
                    dve.wait_ge(S("df_scores"), 2 * h + c + 1)
                    if h >= 2:
                        dve.wait_ge(S("df_turned"), h - 1)
                    dve.scalar_tensor_tensor(out=df_s[:, h % 2, c, :], in0=distances, scalar=2.0 ** -(h + 1),
                                             in1=bank[2 + c][:, 0:384], op0=ALU.mult, op1=ALU.add)\
                       .then_inc(S("df_masked"), 1)
                for c in range(2):
                    dve.wait_ge(S("df_masked"), 2 * h + c + 1)
                    for qt in range(TT):
                        v = dve.tensor_reduce(df_max[:, h % 2, c, qt:qt + 1], df_s[:, h % 2, c, key_span(qt)], AXX,
                                              ALU.max, negate=True)
                    v.then_inc(S("df_max"), 1)

            def combine(h):
                dve.wait_ge(S("df_exp"), 2 * h + 2)
                if h >= 2:
                    dve.wait_ge(S("df_out"), h - 1)
                o(dve.reciprocal(df_inv[:, h % 2, :, :], df_sum[:, h % 2, :, :]))
                o.wait()
                o(dve.scalar_tensor_tensor(out=df_coef[:, h % 2, :], in0=df_sum[:, h % 2, 0, :], scalar=neg_lambda,
                                           in1=df_inv[:, h % 2, 1, :], op0=ALU.mult, op1=ALU.mult))
                o.wait()
                for qt in range(TT):
                    s0, s1 = (df_s[:, h % 2, c, key_span(qt)] for c in range(2))
                    v = dve.scalar_tensor_tensor(out=s0, in0=s1, scalar=df_coef[:, h % 2, qt:qt + 1], in1=s0,
                                                 op0=ALU.mult, op1=ALU.add)
                v.then_inc(S("df_attn"), 1)
            for h in range(DIFF_HEADS + 1):
                if h < DIFF_HEADS:
                    mask_max(h)
                if h >= 1:
                    combine(h - 1)
            dve.wait_ge(S("o_rstd"), 1)
            o3 = bigs(7).rearrange("p (g c) -> p g c", c=2 * DH)
            dve.tensor_tensor(o3, o3, o_rstd.unsqueeze(2).to_broadcast([P, TT * DIFF_HEADS, 2 * DH]), ALU.mult)\
               .then_inc(S("mix_normed"), 1)
            for kp in range(4):
                dve.wait_ge(S("mix_turned"), kp + 5)
                dve.tensor_scalar(hf[:, 2 * kp:2 * kp + 2, :], bank[4 + kp][:, :].rearrange("p (a t) -> p a t", a=2),
                                  subln_gain, None, ALU.mult).then_inc(S("mix_scaled"), 1)
            dve.wait_ge(S("mix_out_hi"), 5)
            dve.tensor_tensor(hl[:, :, :], hf[:, :, :], hh[:, :, :].bitcast(F32), ALU.subtract)\
               .then_inc(S("act_split"), 1)
            residual(dve, lo, BASE["diff_o"])

        block = ctx.enter_context(nc.Block())

        @block.sync
        def _(sp):
            for name, count in PHASES:
                if name.startswith("ffn"):
                    ffn_sp(sp, int(name[3]))
                else:
                    for n in range(BASE[name], BASE[name] + count):
                        load_slot(sp, n, n % WRING, slot_source(n))
            sp.wait_ge(S("x_ready"), 30)
            sp.dma_start(out[0].rearrange("(a p) d -> p a d", p=P), x[:, :, :]).then_inc(S("stored"), 16)
            sp.wait_ge(S("stored"), 16)

        @block.gpsimd
        def _(pool):
            setup_pool(pool)
            norm_pool(pool, 0)
            masks_pool(pool)
            peer_pool(pool)
            norm_pool(pool, 2)
            rwkv_pool(pool)
            norm_pool(pool, 4)
            norm_pool(pool, 5)
            distance_pool(pool)
            norm_pool(pool, 6)
            diff_pool(pool)
            norm_pool(pool, 8)

        @block.scalar
        def _(act):
            hi = HiStream(act)
            setup_act(act)
            hi.upto(1)
            for n in range(24):
                hi.upto(n + 2)
            block1_act(act, hi)
            peer_act(act, hi)
            lora_loads(act)
            ffn_act(act, 0, hi)
            rwkv_act(act, hi)
            ffn_act(act, 1, hi)
            kv_act(act, hi)
            ffn_act(act, 2, hi)
            diff_act(act, hi)
            ffn_act(act, 3, hi)

        @block.vector
        def _(dve):
            lo = LoStream(dve)
            o = setup_dve(dve, lo)
            block1_dve(dve, lo, o)
            peer_dve(dve, lo, o)
            ffn_dve(dve, 0, lo)
            rwkv_dve(dve, lo, o)
            ffn_dve(dve, 1, lo)
            kv_dve(dve, lo, o)
            ffn_dve(dve, 2, lo)
            diff_dve(dve, lo, o)
            ffn_dve(dve, 3, lo)

        @block.tensor
        def _(pe):
            setup_pe(pe)
            block1_pe(pe)
            peer_pe(pe)
            ffn_pe(pe, 0)
            rwkv_pe(pe)
            ffn_pe(pe, 1)
            kv_pe(pe)
            ffn_pe(pe, 2)
            diff_pe(pe)
            ffn_pe(pe, 3)


_INS = ["x", "c", "w_mod", "b_mod", "norm1_g", "w_in", "b_f", "w_pool", "pool_scale", "w_out", "norm2_g", "peer_w_query",
        "peer_sub_keys", "peer_u", "peer_v", "final_g", "ffn_norm_2", "ffn_w_in_2", "ffn_w_out_2", "mix_norm_2",
        "rwkv_mu_2", "rwkv_w_rkv_2", "rwkv_w0_2", "rwkv_w1_2", "rwkv_w2_2", "rwkv_a0_2", "rwkv_a1_2", "rwkv_a2_2",
        "rwkv_g1_2", "rwkv_g2_2", "rwkv_k_k_2", "rwkv_k_a_2", "rwkv_r_k_2", "rwkv_ln_g_2", "rwkv_ln_b_2",
        "rwkv_w_o_2", "kv_norm_2", "w_kv_2", "k_norm_2", "diff_w_q_2", "diff_q_norm_2", "diff_lambda_2",
        "diff_subln_2", "diff_w_o_2"]


def kernel(**inputs):
    import numpy as np
    import concourse.bacc as bacc
    from concourse.bass_utils import run_bass_kernel_spmd

    nc = bacc.Bacc("TRN2", target_bir_lowering=False, num_devices=1)
    arrays, aps = {}, {}
    for name in _INS:
        a = np.ascontiguousarray(inputs[name])
        arrays[f"in_{name}"] = a
        aps[name] = nc.dram_tensor(f"in_{name}", a.shape, mybir.dt.from_np(a.dtype), kind="ExternalInput").ap()
    out = nc.dram_tensor("out", (1, T, D), F32, kind="ExternalOutput").ap()
    build_program(nc, aps, out)
    return run_bass_kernel_spmd(nc, [arrays], core_ids=[0]).results[0]["out"]
```

```python
import math
from contextlib import ExitStack

import concourse.bass as bass
from concourse import mybir

F32 = mybir.dt.float32
F32R = mybir.dt.float32r
U32 = mybir.dt.uint32
I32 = mybir.dt.int32
ALU = mybir.AluOpType
ACT = mybir.ActivationFunctionType
AXX = mybir.AxisListType.X

P = 128
D = 1024
T = 256
KT = D // P
TT = T // P
WRING = 3
SLOTW = 2048
CW = SLOTW // KT
EPS = 1e-6
NEG = -1e30
HEADS, DH = 16, 64
PEER_HEADS, TOPK, NKEYS = 8, 16, 128
POOL_WINDOWS = (2, 4, 8, 16)
FF = 2816
FTILES = FF // CW
LORA, LORA_G = 64, 160
RWKV_EPS, SUBLN_EPS = 64e-5, 1e-5
DECAY = math.exp(-0.5)
LAM_INIT = 0.8 - 0.6 * math.exp(-0.3 * 1)
DIFF_HEADS = 8
RROWS = 8

PHASES = [("mod", 24), ("w_in", 22), ("w_out", 4), ("query", 8), ("ffn0", 33), ("rkv", 12), ("rwkv_o", 4),
          ("ffn1", 33), ("kv", 8), ("ffn2", 33), ("diff_q", 4), ("diff_o", 4), ("ffn3", 33)]
BASE, NSLOTS = {}, 0
for _name, _count in PHASES:
    BASE[_name] = NSLOTS
    NSLOTS += _count


def projection_number(n):
    return n - 33 * sum(n >= BASE[f"ffn{f}"] + 33 for f in range(4))


VEC_A = ["mu0", "mu1", "mu2", "mu3", "mu4", "mu5", "ffn0", "ffn1", "ffn2", "ffn3", "mix0", "mix1",
         "norm1_g", "norm2_g", "pool_scale", "w0"]
VEC_B = ["a0", "k_k", "k_a", "r_k", "ln_g", "ln_b", "kv_norm"]
COL = {name: KT * i for i, name in enumerate(VEC_A + VEC_B)}
COL["k_norm"], COL["q_norm"], COL["subln"] = (KT * (len(VEC_A) + len(VEC_B)) + i for i in range(3))
NVEC_B = KT * len(VEC_B) + 3
NVEC = P + NVEC_B


class Order:

    def __init__(self, engine, done):
        self.engine, self.done, self.count = engine, done, 0

    def __call__(self, instruction):
        instruction.then_inc(self.done, 1)
        self.count += 1

    def wait(self):
        if self.count:
            self.engine.wait_ge(self.done, self.count)


def build_program(nc, A, out):
    ctx = ExitStack()
    with ctx:
        def sb(name, shape, dt=F32):
            return ctx.enter_context(nc.sbuf_tensor(name, shape, dt))

        sems = {}

        def S(name):
            if name not in sems:
                sems[name] = ctx.enter_context(nc.semaphore(name))
            return sems[name]

        w_raw = [sb(f"w_raw{i}", [P, SLOTW]) for i in range(WRING)]
        w_hi = [sb(f"w_hi{i}", [P, SLOTW], F32R) for i in range(WRING)]
        w_lo = [sb(f"w_lo{i}", [P, SLOTW], F32R) for i in range(WRING)]
        x = sb("x", [P, TT, D])
        hf = sb("hf", [P, KT, T])
        hh = sb("hh", [P, KT, T], F32R)
        hl = sb("hl", [P, KT, T], F32R)
        act_hi = sb("act_hi", [P, 512], F32R)
        act_lo = sb("act_lo", [P, 512], F32R)
        big = sb("big", [P, 8 * SLOTW])
        aux = sb("aux", [P, 6400])
        ident = sb("ident", [P, P])
        ones = sb("ones", [P, T])
        amask = sb("amask", [P, 384])
        wkv_masks = sb("wkv_masks", [P, 5, P])
        head_pick = sb("head_pick", [P, KT // 2, HEADS // 2])
        head_rows = sb("head_rows", [HEADS // 2, D // 2])
        half_ones = sb("half_ones", [P, 2])
        vec = sb("vec", [P, NVEC])
        modc = sb("modc", [P, 6 * KT])
        small = sb("small", [P, 256])
        stat = sb("stat", [P, 24])
        w_f = sb("w_f", [P, KT, HEADS])
        bank = [ctx.enter_context(nc.psum_tensor(f"bank{i}", [P, 512], F32)) for i in range(8)]

        def bigs(i, count=1):
            return big[:, i * SLOTW:(i + count) * SLOTW]

        def fm(flat):
            return flat.rearrange("p (k t) -> p k t", t=T)

        def tm(flat):
            return flat.rearrange("p (a d) -> p a d", a=TT)

        def col(name, k):
            return vec[:, COL[name] + k:COL[name] + k + 1]

        squares, norm_row = tm(bigs(7)), big[:, 7 * SLOTW:7 * SLOTW + T]
        low16, low_far, up16, up_strict, up_incl = (wkv_masks[:, i, :] for i in range(5))
        silu_g = big[:, 6 * SLOTW:6 * SLOTW + 512]
        act_f = big[:, 6 * SLOTW + 512:6 * SLOTW + 1024]

        vec_rows = bigs(5)
        c_rows = vec_rows[0:KT, 512:640]
        b_mod_row = big[0:1, 0:6 * D]
        gt1, gt2 = aux[:, 0:D], aux[:, D:2 * D]
        h2tok = aux[:, 2 * D:4 * D].rearrange("p (a d) -> p a d", a=TT)
        mod_tmp = big[:, 3 * SLOTW:5 * SLOTW]

        def mod_place(j):
            part, c0 = j // 4, (j % 4) * CW
            if part in (2, 5):
                return (gt1 if part == 2 else gt2)[:, c0:c0 + CW]
            q = {0: 0, 1: 1, 3: 2, 4: 3}[part]
            return mod_tmp[:, q * D + c0:q * D + c0 + CW]

        qT, kT, vtok = fm(bigs(0)), fm(bigs(1)), tm(bigs(2))
        upool, ga, gb = bigs(3)[:, 0:4 * T].rearrange("p (g t) -> p g t", t=T), fm(bigs(4)), fm(bigs(5))
        pool_win = bigs(3)[:, 4 * T:8 * T].rearrange("p (a t) -> p a t", t=T)
        w_pool = bigs(6)[:, 0:4 * T].rearrange("p (g d) -> p g d", g=4)
        pooled = bigs(6)[:, 4 * T:8 * T].rearrange("p (g t) -> p g t", g=4)
        inv_count = small[:, 0:64].rearrange("p (g t) -> p g t", g=4)
        logf, cumf, negf, ftmp = (aux[0:HEADS, 4096 + i * T:4096 + (i + 1) * T] for i in range(4))
        att_s = big[:, 7 * SLOTW:7 * SLOTW + 4 * 384].rearrange("p (b n) -> p b n", b=4)
        att_pT = big[:, 6 * SLOTW:6 * SLOTW + 768].rearrange("p (b n) -> p b n", b=2)
        mask_r, ident_r = act_hi[:, 0:384], act_hi[:, 384:512]
        negf_hi, negf_lo = act_lo[0:HEADS, 0:T], act_lo[0:HEADS, T:2 * T]
        b_f = small[0:HEADS, 64:65]
        att_stat = aux[:, 5120:5120 + 8 * 4].rearrange("p (b n) -> p b n", b=4)

        def slot_source(n):
            for name, count in PHASES:
                if BASE[name] <= n < BASE[name] + count:
                    j = n - BASE[name]
                    break
            def columns(w, c0):
                return w.rearrange("(k p) c -> p k c", p=P)[:, :, c0:c0 + CW]
            if name == "mod":
                return columns(A["w_mod"][0], j * CW)
            if name == "w_in":
                starts = [512 + CW * i for i in range(12)] + [0, 256] + [3600 + CW * i for i in range(8)]
                return columns(A["w_in"][0], starts[j])
            if name == "w_out":
                return columns(A["w_out"][0], j * CW)
            if name == "query":
                return columns(A["peer_w_query"][0], j * CW)
            if name == "rkv":
                return columns(A["rwkv_w_rkv_2"][0, j // 4], (j % 4) * CW)
            if name == "rwkv_o":
                return columns(A["rwkv_w_o_2"][0], j * CW)
            if name == "kv":
                return columns(A["w_kv_2"], j * CW)
            if name == "diff_q":
                return columns(A["diff_w_q_2"][0], j * CW)
            return columns(A["diff_w_o_2"][0], j * CW)

        def slot_view(tile):
            return tile[:, :].rearrange("p (k c) -> p k c", k=KT)

        def load_slot(sp, n, i, src):
            if not (isinstance(n, int) and n < WRING):
                sp.wait_ge(S("w_lo"), n - (WRING - 1))
            k = src.shape[1]
            sp.dma_start(w_raw[i][:, :].rearrange("p (k c) -> p k c", k=k), src).then_inc(S(f"w_loaded{i}"), 16)

        def ffn_sp(sp, f):
            base = BASE[f"ffn{f}"]
            w_in = A["ffn_w_in_2"][f // 2, f % 2].rearrange("(k p) c -> p k c", p=P)
            w_out = A["ffn_w_out_2"][f // 2, f % 2].rearrange("(a p) d -> p a d", p=P)

            def g(n, i, r):
                load_slot(sp, n, r, w_in[:, :, bass.ds(i * CW, CW)])

            def u(n, i, r):
                load_slot(sp, n, r, w_in[:, :, bass.ds(i * CW + FF, CW)])

            def o(n, i, r):
                load_slot(sp, n, r, w_out[:, bass.ds(i * 2, 2), :])
            g(base, 0, base % WRING)
            u(base + 1, 0, (base + 1) % WRING)
            with sp.Fori(0, FTILES - 1) as i:
                n = i * 3 + (base + 2)
                g(n, i + 1, (base + 2) % WRING)
                u(n + 1, i + 1, (base + 3) % WRING)
                o(n + 2, i, (base + 4) % WRING)
            o(base + 32, FTILES - 1, (base + 32) % WRING)

        def split_hi(act, n, i, loaded):
            act.wait_ge(S(f"w_loaded{i}"), loaded)
            if not (isinstance(n, int) and n < WRING):
                act.wait_ge(S("slot_done"), n - (WRING - 1))
            act.activation(w_hi[i][:, :], w_raw[i][:, :], ACT.Copy).then_inc(S("w_hi"), 1)

        def split_lo(dve, n, i):
            dve.wait_ge(S("w_hi"), n + 1)
            dve.tensor_tensor(w_lo[i][:, :], w_raw[i][:, :], w_hi[i][:, :].bitcast(F32), ALU.subtract)\
               .then_inc(S("w_lo"), 1)

        class HiStream:
            def __init__(self, act):
                self.act, self.next = act, 0

            def upto(self, n):
                while self.next <= min(n, NSLOTS - 1):
                    m = self.next
                    split_hi(self.act, m, m % WRING, 16 * (m // WRING + 1))
                    self.next += 1

        class LoStream:
            def __init__(self, dve):
                self.dve, self.next = dve, 0

            def upto(self, n):
                while self.next <= min(n, NSLOTS - 1):
                    split_lo(self.dve, self.next, self.next % WRING)
                    self.next += 1

        def project(pe, n, hi, lo, mode):
            number = projection_number(n)
            b = bank[number % 2]
            wh, wl = slot_view(w_hi[n % WRING]), slot_view(w_lo[n % WRING])
            pe.wait_ge(S("w_lo"), n + 1)
            if number >= 2:
                pe.wait_ge(S(f"proj_free{number % 2}"), number // 2)
            for part in range(1 if mode == "M" else 2):
                for k in range(KT):
                    for m, (wp, ap) in enumerate(((wh, hi), (wh, lo), (wl, hi))):
                        if mode == "F":
                            lhs, rhs = wp[:, k, part * P:(part + 1) * P], ap[:, k, :]
                        else:
                            lhs, rhs = ap[:, k, part * P:(part + 1) * P], wp[:, k, :]
                        mm = pe.matmul(b[:, part * CW:(part + 1) * CW], lhs, rhs, start=(k == 0 and m == 0),
                                       stop=(mode != "M" and k == KT - 1 and m == 2))
            if mode == "M":
                j = n - BASE["mod"]
                mm = pe.matmul(b[:, 0:CW], ones[0:1, 0:P], b_mod_row[:, j * CW:(j + 1) * CW], start=False, stop=True)
            mm.then_inc(S("slot_done"), 1)

        def evac_ready(eng, n):
            eng.wait_ge(S("slot_done"), n + 1)
            return bank[projection_number(n) % 2], S(f"proj_free{projection_number(n) % 2}")

        part_ss = stat[:, 16:24].rearrange("p (a i) -> p a i", a=TT)

        def norm_parts(n):
            if n in (0, 2):
                parts = [[(tt, slice(0, D))] for tt in range(TT)]
            elif n in (1, 4, 8):
                parts = [[(tt, slice(j * CW, (j + 1) * CW)) for tt in range(TT)] for j in range(4)]
            else:
                parts = [[(tt, slice(half * 512, (half + 1) * 512))] for tt in range(TT) for half in range(2)]
            return [(XREADY.get(n, 0) - len(parts) + i + 1, p) for i, p in enumerate(parts)]

        def norm_squares(act, n):
            seen = [0] * TT
            for ready, pieces in norm_parts(n):
                if n > 0:
                    act.wait_ge(S("x_ready"), ready)
                for tt, cols in pieces:
                    a = act.activation(squares[:, tt, cols], x[:, tt, cols], ACT.Square,
                                       accum_out=part_ss[:, tt, seen[tt]:seen[tt] + 1])
                    seen[tt] += 1
            a.then_inc(S("norm_ss"), 1)

        def norm_act(act, n, hi):
            if n > 0:
                norm_squares(act, n)
            if n == 0:
                act.wait_ge(S("slot_done"), BASE["w_in"])
            if n in SPLIT:
                for kp in range(4):
                    act.wait_ge(S("norm_hf"), 4 * n + kp + 1)
                    act.activation(hh[:, 2 * kp:2 * kp + 2, :], hf[:, 2 * kp:2 * kp + 2, :], ACT.Copy)\
                       .then_inc(S("norm_hh"), 1)

        def norm_pool(pool, n):
            pieces = sum(len(p) for _, p in norm_parts(n)) // TT
            pool.wait_ge(S("norm_ss"), n + 1)
            ss = part_ss[:, :, 0:1]
            o = pool_order[0]
            if pieces > 1:
                ss = stat[:, 0:2].unsqueeze(2)
                for i in range(1, pieces):
                    o(pool.tensor_tensor(ss, ss if i > 1 else part_ss[:, :, 0:1], part_ss[:, :, i:i + 1], ALU.add))
                    o.wait()
            pool.tensor_scalar(stat[:, 2:4].unsqueeze(2), ss, 1.0 / D, EPS, ALU.mult, ALU.add).then_inc(S("norm_ms"), 1)
            pool.wait_ge(S("norm_ms"), n + 1)
            pool.tensor_tensor(stat[:, 4:6], stat[:, 2:4], stat[:, 6:8], ALU.pow).then_inc(S("norm_rstd"), 1)

        def keep_warm(pe, products, b=2):
            for _ in range(products):
                pe.matmul(bank[b][:, 0:T], ident[:, :], ones[:, :], start=True, stop=True)

        def norm_pe(pe, n):
            ready = norm_parts(n)
            if n == 0:
                pe.wait_ge(S("params"), N_PARAMS)
            for kp in range(4):
                if n > 0:
                    pe.wait_ge(S("x_ready"), ready[kp][0] if len(ready[0][1]) > 1 else XREADY[n])
                for k in (2 * kp, 2 * kp + 1):
                    for tt in range(TT):
                        mm = pe.transpose(bank[4 + kp][:, (k % 2) * T + tt * P:(k % 2) * T + (tt + 1) * P],
                                          x[:, tt, k * P:(k + 1) * P], ident[:, :])
                mm.then_inc(S("norm_tr"), 1)
            pe.wait_ge(S("norm_rstd"), n + 1)
            for tt in range(TT):
                mm = pe.matmul(bank[3][:, tt * P:(tt + 1) * P], stat[:, 4 + tt:5 + tt].to_broadcast([P, P]), ident[:, :],
                               start=True, stop=True)
            mm.then_inc(S("norm_spread"), 1)
            if n > 0:
                keep_warm(pe, 14)

        def norm_dve(dve, n, scale):
            dve.wait_ge(S("norm_spread"), n + 1)
            dve.tensor_copy(norm_row, bank[3][:, 0:T]).then_inc(S("norm_row"), 1)
            dve.wait_ge(S("norm_row"), n + 1)
            for kp in range(4):
                dve.wait_ge(S("norm_tr"), 4 * n + kp + 1)
                if scale is None:
                    dve.tensor_tensor(hf[:, 2 * kp:2 * kp + 2, :], bank[4 + kp][:, :].rearrange("p (a t) -> p a t", a=2),
                                      norm_row.unsqueeze(1).to_broadcast([P, 2, T]), ALU.mult)\
                       .then_inc(S("norm_scaled"), 1)
                    continue
                for k in (2 * kp, 2 * kp + 1):
                    src = bank[4 + kp][:, (k % 2) * T:(k % 2 + 1) * T]
                    v = dve.scalar_tensor_tensor(out=hf[:, k, :], in0=src, scalar=scale(k), in1=norm_row,
                                                 op0=ALU.mult, op1=ALU.mult)
                v.then_inc(S("norm_hf"), 1)
            if n > 0:
                norm_rest(dve, n)

        def norm_rest(dve, n):
            if n < 2:
                dve.wait_ge(S("modc"), 2)
                for kp in range(4):
                    dve.wait_ge(S("norm_scaled"), 4 * n + kp + 1)
                    for k in (2 * kp, 2 * kp + 1):
                        v = dve.tensor_scalar(hf[:, k, :], hf[:, k, :], modc[:, 32 + KT * n + k:33 + KT * n + k],
                                              modc[:, 16 * n + k:16 * n + k + 1], ALU.mult, ALU.add)
                    v.then_inc(S("norm_hf"), 1)
            if n in SPLIT:
                for half in range(2):
                    dve.wait_ge(S("norm_hh"), 4 * SPLIT.index(n) + 2 * half + 2)
                    k0 = 4 * half
                    dve.tensor_tensor(hl[:, k0:k0 + 4, :], hf[:, k0:k0 + 4, :], hh[:, k0:k0 + 4, :].bitcast(F32),
                                      ALU.subtract).then_inc(S("act_split"), 1)

        SPLIT = [0, 1, 2, 4, 5, 6, 7, 8]
        XREADY = {1: 4, 2: 6, 3: 10, 4: 14, 5: 18, 6: 18, 7: 22, 8: 26}
        SPLITS = {}
        _total = 0
        for _step, _n in [("norm0", 2), ("y1", 1), ("norm1", 2), ("norm2", 2), ("mix_r", 1), ("mix_k", 1),
                          ("mix_v", 1), ("rwkv_y", 1), ("norm4", 2), ("norm5", 2), ("norm6", 2), ("norm7", 2),
                          ("diff_y", 1), ("norm8", 2)]:
            _total += _n
            SPLITS[_step] = _total

        def ffn_pe(pe, f):
            base = BASE[f"ffn{f}"]
            norm = {0: 2, 1: 4, 2: 6, 3: 8}[f]
            norm_pe(pe, norm)
            pe.wait_ge(S("act_split"), SPLITS[f"norm{norm}"])

            def up(n, i, r, b, freed):
                pe.wait_ge(S("w_lo"), n + 1)
                if not (isinstance(i, int) and i + f == 0):
                    pe.wait_ge(S(freed), i + FTILES * f)
                wh, wl = slot_view(w_hi[r]), slot_view(w_lo[r])
                for part in range(2):
                    for k in range(KT):
                        for m, (wp, ap) in enumerate(((wh, hh), (wh, hl), (wl, hh))):
                            mm = pe.matmul(b[:, part * T:(part + 1) * T], wp[:, k, part * P:(part + 1) * P],
                                           ap[:, k, :], start=(k == 0 and m == 0), stop=(k == KT - 1 and m == 2))
                mm.then_inc(S("slot_done"), 1)

            def down(n, i, r, first, last):
                pe.wait_ge(S("w_lo"), n + 1)
                pe.wait_ge(S("ffn_act"), i + (FTILES * f + 1))
                wh = w_hi[r][:, :].rearrange("p (a d) -> p a d", a=2)
                wl = w_lo[r][:, :].rearrange("p (a d) -> p a d", a=2)
                for tt in range(TT):
                    for half in range(2):
                        for a in range(2):
                            rows = slice(a * T + tt * P, a * T + (tt + 1) * P)
                            for m, (ap, wp) in enumerate(((act_hi, wh), (act_lo, wh), (act_hi, wl))):
                                mm = pe.matmul(bank[4 + 2 * tt + half][:, :], ap[:, rows],
                                               wp[:, a, half * 512:(half + 1) * 512],
                                               start=(first and a == 0 and m == 0), stop=(last and a == 1 and m == 2))
                mm.then_inc(S("slot_done"), 1)

            def step(i, first):
                n = i * 3 + (base + 2)
                up(n, i + 1, (base + 2) % WRING, bank[2], "ffn_silu")
                up(n + 1, i + 1, (base + 3) % WRING, bank[3], "ffn_mult")
                down(n + 2, i, (base + 4) % WRING, first, False)
            up(base, 0, base % WRING, bank[2], "ffn_silu")
            up(base + 1, 0, (base + 1) % WRING, bank[3], "ffn_mult")
            step(0, True)
            with pe.Fori(1, FTILES - 1) as i:
                step(i, False)
            down(base + 32, FTILES - 1, (base + 32) % WRING, False, True)

        def ffn_act(act, f, hi):
            base = BASE[f"ffn{f}"]
            norm_act(act, {0: 2, 1: 4, 2: 6, 3: 8}[f], hi)
            hi.upto(base + 1)

            def silu(i, n):
                act.wait_ge(S("slot_done"), n + 1)
                if not (isinstance(i, int) and i + f == 0):
                    act.wait_ge(S("ffn_mult"), i + FTILES * f)
                act.activation(silu_g, bank[2][:, :], ACT.Silu).then_inc(S("ffn_silu"), 1)

            def act_round(i, n):
                act.wait_ge(S("ffn_mult"), i + (FTILES * f + 1))
                act.wait_ge(S("slot_done"), n)
                act.activation(act_hi[:, :], act_f, ACT.Copy).then_inc(S("ffn_act_hi"), 1)

            def step(i, split):
                n = i * 3 + (base + 2)
                split(n + 2, 2, i)
                silu(i + 1, n)
                split(n + 3, 3, i)
                split(n + 4, 4, i)
                act_round(i + 1, n + 3)

            def split_static(n, j, i):
                hi.upto(n)

            def split_loop(n, j, i):
                slot0 = base + 2 + j
                split_hi(act, n, slot0 % WRING, i * 16 + 16 * (slot0 // WRING + 1))
            hi.upto(base + 2)
            silu(0, base)
            hi.upto(base + 3)
            act_round(0, base)
            step(0, split_static)
            with act.Fori(1, FTILES - 2) as i:
                step(i, split_loop)
            hi.next = base + 2 + 3 * (FTILES - 2) + 2
            step(FTILES - 2, split_static)
            hi.upto(base + 34)

        def ffn_dve(dve, f, lo):
            base = BASE[f"ffn{f}"]
            n_norm = {0: 2, 1: 4, 2: 6, 3: 8}[f]
            norm_dve(dve, n_norm, lambda k: col(f"ffn{f}", k))
            lo.upto(base + 1)

            def mult(i, n):
                dve.wait_ge(S("ffn_silu"), i + (FTILES * f + 1))
                dve.wait_ge(S("slot_done"), n + 1)
                if not (isinstance(i, int) and i + f == 0):
                    dve.wait_ge(S("ffn_act"), i + FTILES * f)
                dve.tensor_tensor(act_f, silu_g, bank[3][:, :], ALU.mult).then_inc(S("ffn_mult"), 1)

            def act_rest(i):
                dve.wait_ge(S("ffn_act_hi"), i + (FTILES * f + 1))
                dve.tensor_tensor(act_lo[:, :], act_f, act_hi[:, :].bitcast(F32), ALU.subtract)\
                   .then_inc(S("ffn_act"), 1)

            def step(i, split):
                n = i * 3 + (base + 2)
                split(n + 2, 2)
                split(n + 3, 3)
                mult(i + 1, n + 1)
                split(n + 4, 4)
                act_rest(i + 1)

            def split_static(n, j):
                lo.upto(n)

            def split_loop(n, j):
                split_lo(dve, n, (base + 2 + j) % WRING)
            lo.upto(base + 2)
            mult(0, base + 1)
            lo.upto(base + 3)
            act_rest(0)
            step(0, split_static)
            with dve.Fori(1, FTILES - 2) as i:
                step(i, split_loop)
            lo.next = base + 2 + 3 * (FTILES - 2) + 2
            step(FTILES - 2, split_static)
            lo.upto(base + 34)
            dve.wait_ge(S("slot_done"), base + 33)
            for tt in range(TT):
                for half in range(2):
                    part = x[:, tt, half * 512:(half + 1) * 512]
                    dve.scalar_tensor_tensor(out=part, in0=bank[4 + 2 * tt + half][:, :], scalar=0.5, in1=part,
                                             op0=ALU.mult, op1=ALU.add).then_inc(S("x_ready"), 1)

        cT = small[:, 72:80]

        def rows(v):
            return v.rearrange("(k p) -> k p", p=P)

        SETUP_LOADS = 20

        def setup_act(act):
            def load(dst, src):
                act.dma_start(dst, src).then_inc(S("params"), 16)
            load(c_rows, rows(A["c"][0]))
            load(b_mod_row, A["b_mod"])
            load(x[:, :, :], A["x"][0].rearrange("(a p) d -> p a d", p=P))
            r = 0
            for src in ([A["rwkv_mu_2"].rearrange("a m (k p) -> (a m k) p", p=P),
                         A["ffn_norm_2"].rearrange("a m (k p) -> (a m k) p", p=P),
                         A["mix_norm_2"].rearrange("a (k p) -> (a k) p", p=P)]
                        + [rows(A[n][0]) for n in ("norm1_g", "norm2_g", "pool_scale", "rwkv_w0_2")]):
                load(vec_rows[r:r + src.shape[0], 0:P], src)
                r += src.shape[0]
            r = 0
            for src in ([rows(A[n][0]) for n in ("rwkv_a0_2", "rwkv_k_k_2", "rwkv_k_a_2")]
                        + [A["rwkv_r_k_2"][0].rearrange("(k a) d -> k (a d)", a=2)]
                        + [rows(A[n][0]) for n in ("rwkv_ln_g_2", "rwkv_ln_b_2")] + [rows(A["kv_norm_2"])]):
                load(vec_rows[r:r + KT, P:2 * P], src)
                r += KT
            head_gains = [A["k_norm_2"], A["diff_q_norm_2"][0]]
            for src in head_gains:
                act.dma_start(vec_rows[r:r + 1, P:P + DH], src.rearrange("(a d) -> a d", a=1)).then_inc(S("params"), 16)
                act.dma_start(vec_rows[r:r + 1, P + DH:2 * P], src.rearrange("(a d) -> a d", a=1))\
                   .then_inc(S("params"), 16)
                r += 1
            load(vec_rows[r:r + 1, P:2 * P], A["diff_subln_2"])
            load(w_f[:, :, :], A["w_in"][0].rearrange("(k p) c -> p k c", p=P)[:, :, 3584:3600])
            load(b_f, A["b_f"].rearrange("a h -> h a"))
            load(w_pool, A["w_pool"][0].rearrange("g c d -> c g d"))
            act.wait_ge(S("cT"), 1)
            act.activation(hh[:, :, 0:P], cT.unsqueeze(2).to_broadcast([P, KT, P]), ACT.Copy).then_inc(S("c_hi"), 1)

        N_PARAMS = 16 * (3 + 7 + 7 + 4 + 1 + 3)

        pool_order = []

        def setup_pool(pool):
            o = Order(pool, S("pool_order"))
            pool_order.append(o)
            o(pool.memset(ident[:, :], 0.0))
            o(pool.memset(stat[:, 6:8], -0.5))
            pool.memset(ones[:, :], 1.0).then_inc(S("ones"), 1)
            o.wait()
            pool.affine_select(out=ident[:, :], in_=ident[:, :], compare_op=ALU.not_equal, fill=1.0, base=0,
                               pattern=[[-1, P]], channel_multiplier=1).then_inc(S("ident"), 1)
            o(pool.memset(amask[:, :], 0.0))
            o.wait()
            for c0 in (0, 256):
                pool.affine_select(out=amask[:, c0:c0 + P], in_=amask[:, c0:c0 + P], compare_op=ALU.is_ge, fill=NEG,
                                   base=0, pattern=[[-1, P]], channel_multiplier=1).then_inc(S("causal"), 1)
            pool.iota(small[:, 80:96], pattern=[[1, 16]], base=1, channel_multiplier=0,
                      allow_small_or_imprecise_dtypes=True).then_inc(S("token_count"), 1)

        def setup_pe(pe):
            pe.wait_ge(S("ident"), 1)
            pe.wait_ge(S("ones"), 1)
            pe.wait_ge(S("params"), N_PARAMS)
            pe.transpose(bank[4][:, 0:KT], c_rows, ident[0:KT, 0:KT]).then_inc(S("setup_tr"), 1)
            pe.transpose(bank[5][:, 0:P], vec_rows[:, 0:P], ident[:, :])
            pe.transpose(bank[5][:, P:NVEC], vec_rows[0:NVEC_B, P:2 * P], ident[0:NVEC_B, 0:NVEC_B])\
              .then_inc(S("setup_tr"), 1)
            pe.wait_ge(S("act_split_c"), 1)
            for n in range(24):
                project(pe, n, hh, hl, "M")
                if n == 2:
                    norm_pe(pe, 0)
            for b in range(2):
                pe.wait_ge(S(f"proj_free{b}"), 10)
            for j in range(4 * KT):
                mm = pe.matmul(bank[2][:, j:j + 1], mod_tmp[0:1, j * P:(j + 1) * P], ones[0:1, 0:1],
                               start=True, stop=True)
            mm.then_inc(S("mod_tr"), 1)

        def setup_dve(dve, lo):
            o = Order(dve, S("dve_order"))
            dve.wait_ge(S("setup_tr"), 1)
            dve.tensor_copy(cT, bank[4][:, 0:KT]).then_inc(S("cT"), 1)
            dve.wait_ge(S("setup_tr"), 2)
            dve.tensor_copy(vec[:, :], bank[5][:, 0:NVEC]).then_inc(S("vec"), 1)
            dve.wait_ge(S("c_hi"), 1)
            dve.tensor_tensor(hl[:, :, 0:P], cT.unsqueeze(2).to_broadcast([P, KT, P]), hh[:, :, 0:P].bitcast(F32),
                              ALU.subtract).then_inc(S("act_split_c"), 1)
            dve.wait_ge(S("token_count"), 1)
            for g, w in enumerate(POOL_WINDOWS):
                o(dve.tensor_scalar(inv_count[:, g, :], small[:, 80:96], float(w), None, ALU.min))
            o.wait()
            o(dve.reciprocal(inv_count, inv_count))
            for n in range(24):
                lo.upto(n + 2)
                b, free = evac_ready(dve, n)
                dve.tensor_copy(mod_place(n), b[:, 0:CW]).then_inc(free, 1)
                if n == 5:
                    norm_dve(dve, 0, None)
            dve.wait_ge(S("mod_tr"), 1)
            dve.tensor_copy(modc[:, 0:32], bank[2][:, 0:32]).then_inc(S("modc"), 1)
            dve.wait_ge(S("modc"), 1)
            dve.wait_ge(S("vec"), 1)
            for i, g in enumerate(("norm1_g", "norm2_g")):
                o(dve.scalar_tensor_tensor(out=modc[:, 32 + KT * i:32 + KT * (i + 1)],
                                           in0=modc[:, 16 * i + KT:16 * i + 2 * KT], scalar=1.0,
                                           in1=vec[:, COL[g]:COL[g] + KT], op0=ALU.add, op1=ALU.mult))
            o.wait()
            dve.sem_inc(S("modc"), 1)
            return o

        WIN = BASE["w_in"]
        Q0, K0, V0, U0, GA0, GB0 = WIN, WIN + 4, WIN + 8, WIN + 12, WIN + 14, WIN + 18

        def block1_pe(pe):
            pe.wait_ge(S("modc"), 1)
            keep_warm(pe, 10)
            pe.wait_ge(S("act_split"), SPLITS["norm0"])
            for n in range(WIN, WIN + 22):
                project(pe, n, hh, hl, "T" if V0 <= n < U0 else "F")
                if n == WIN + 1:
                    for k in range(KT):
                        mm = pe.matmul(bank[2][0:HEADS, 0:T], w_f[:, k, :], hf[:, k, :], start=(k == 0),
                                       stop=(k == KT - 1))
                    mm.then_inc(S("forget_logits"), 1)
            pe.wait_ge(S("pooled"), 4)
            for g in range(4):
                for half in range(2):
                    mm = pe.matmul(bank[4 + g][:, half * T:(half + 1) * T], w_pool[:, g, half * P:(half + 1) * P],
                                   pooled[:, g, :], start=True, stop=True)
                mm.then_inc(S("pool_out"), 1)
            pe.wait_ge(S("pool_mixed"), 4)
            pe.wait_ge(S("att_consts"), 4)
            for b in range(2):
                pe.wait_ge(S(f"proj_free{b}"), projection_number(U0) // 2)

            def scores(h):
                po, k = DH * (h % 2), h // 2
                if h >= 2:
                    pe.wait_ge(S("att_exp"), h - 1)
                for qt in range(TT):
                    n_keys = P * (qt + 1)
                    o_ = bank[2 + h % 2][:, P * qt:P * qt + n_keys]
                    pick = ident_r[0:HEADS, h:h + 1].to_broadcast([HEADS, P])
                    pe.matmul(o_, qT[po:po + DH, k, qt * P:(qt + 1) * P], kT[po:po + DH, k, 0:n_keys],
                              start=True, stop=False)
                    for part in (negf_hi, negf_lo):
                        pe.matmul(o_, pick, part[:, 0:n_keys], start=False, stop=False)
                    mm = pe.matmul(o_, ident_r, mask_r[:, P * qt:P * qt + n_keys], start=False, stop=True)
                mm.then_inc(S("att_scores"), 1)

            def turn(h):
                pe.wait_ge(S("att_p"), h + 1)
                if h >= 2:
                    pe.wait_ge(S("att_pT"), h - 1)
                for j in range(3):
                    mm = pe.transpose(bank[4 + h % 2][:, j * P:(j + 1) * P], att_s[:, h % 4, j * P:(j + 1) * P],
                                      ident[:, :])
                mm.then_inc(S("att_turned"), 1)

            def values(h):
                po = DH * (h % 2)
                pe.wait_ge(S("att_pT"), h + 1)
                if h % 2 == 0 and h >= 4:
                    pe.wait_ge(S("att_out"), h // 2 - 1)
                o_ = bank[6 + (h // 2) % 2][po:po + DH, :]
                for qt, j, kt in ((0, 0, 0), (1, 1, 0), (1, 2, 1)):
                    mm = pe.matmul(o_[:, qt * P:(qt + 1) * P], vtok[:, kt, h * DH:(h + 1) * DH],
                                   att_pT[:, h % 2, j * P:(j + 1) * P], start=(kt == 0), stop=(kt == qt))
                mm.then_inc(S("att_pv"), 1)
            for h in range(HEADS + 4):
                if h < HEADS:
                    scores(h)
                if h < 3:
                    keep_warm(pe, 3, 7)
                if 3 <= h <= HEADS + 2:
                    turn(h - 3)
                if h >= 4:
                    values(h - 4)
            keep_warm(pe, 13)
            pe.wait_ge(S("act_split"), SPLITS["y1"])
            for n in range(BASE["w_out"], BASE["w_out"] + 4):
                project(pe, n, hh, hl, "T")
                if n == BASE["w_out"] + 1:
                    keys_pe(pe)

        def forget_softplus(act):
            o = Order(act, S("act_order"))
            act.wait_ge(S("forget_z"), 1)
            o(act.activation(ftmp, logf, ACT.Abs))
            o.wait()
            o(act.activation(ftmp, ftmp, ACT.Exp, scale=-1.0))
            o.wait()
            act.activation(ftmp, ftmp, ACT.Ln, bias=1.0).then_inc(S("softplus"), 1)
            act.wait_ge(S("causal"), 2)
            act.activation(mask_r, amask[:, :], ACT.Copy).then_inc(S("att_consts"), 1)
            act.wait_ge(S("ident"), 1)
            act.activation(ident_r, ident[:, :], ACT.Copy).then_inc(S("att_consts"), 1)
            act.wait_ge(S("cumf"), 2)
            act.activation(negf_hi, negf, ACT.Copy).then_inc(S("att_consts"), 1)

        def block1_gate_out(act, n):
            j = n - WIN
            if Q0 <= n < K0:
                b, free = evac_ready(act, n)
                act.activation(qT[:, 2 * j:2 * j + 2, :], b[:, :], ACT.Copy, scale=DH ** -0.5).then_inc(free, 1)
            if GA0 <= n:
                b, free = evac_ready(act, n)
                g, j = (ga, n - GA0) if n < GB0 else (gb, n - GB0)
                act.activation(g[:, 2 * j:2 * j + 2, :], b[:, :], ACT.Sigmoid).then_inc(free, 1)

        def block1_act(act, hi):
            act.wait_ge(S("params"), N_PARAMS)
            norm_act(act, 0, hi)
            for n in range(WIN, WIN + 22):
                hi.upto(n + 2)
                if n == WIN + 3:
                    forget_softplus(act)
                block1_gate_out(act, n)
            def exps(h):
                act.wait_ge(S("att_max"), h + 1)
                if h >= 4:
                    act.wait_ge(S("att_turned"), h - 3)
                for qt in range(TT):
                    keys = slice(P * qt, P * qt + P * (qt + 1))
                    a = act.activation(att_s[:, h % 4, keys], bank[2 + h % 2][:, keys], ACT.Exp,
                                       bias=att_stat[:, h % 4, qt:qt + 1], accum_out=att_stat[:, h % 4, 2 + qt:3 + qt])
                a.then_inc(S("att_exp"), 1)

            def copy_out(h):
                act.wait_ge(S("att_turned"), h + 1)
                if h >= 2:
                    act.wait_ge(S("att_pv"), h - 1)
                act.activation(att_pT[:, h % 2, :], bank[4 + h % 2][:, 0:384], ACT.Copy).then_inc(S("att_pT"), 1)
            for h in range(HEADS + 3):
                if h < HEADS:
                    exps(h)
                if h >= 3:
                    copy_out(h - 3)
            act.wait_ge(S("att_out"), HEADS // 2)
            act.dma_start(keys_rows, A["peer_sub_keys"][0].rearrange("h i n c -> n (h i) c")).then_inc(S("keys"), 16)
            act.activation(hh[:, :, :], hf[:, :, :], ACT.Copy).then_inc(S("y1_hi"), 1)
            hi.upto(BASE["w_out"] + 4)
            keys_act(act)
            hi.upto(BASE["w_out"] + 5)

        def forget_sums(dve, o):
            dve.wait_ge(S("forget_logits"), 1)
            dve.tensor_scalar(logf, bank[2][0:HEADS, 0:T], b_f, None, ALU.add).then_inc(S("forget_z"), 1)
            dve.wait_ge(S("softplus"), 1)
            o(dve.tensor_scalar(logf, logf, 0.0, None, ALU.min))
            o.wait()
            o(dve.tensor_tensor(logf, logf, ftmp, ALU.subtract))
            o.wait()
            dve.tensor_tensor_scan(cumf, ones[0:HEADS, :], logf, 0.0, ALU.mult, ALU.add).then_inc(S("cumf"), 1)
            dve.wait_ge(S("cumf"), 1)
            dve.tensor_scalar(negf, cumf, -1.0, None, ALU.mult).then_inc(S("cumf"), 1)
            dve.wait_ge(S("att_consts"), 3)
            dve.tensor_tensor(negf_lo, negf, negf_hi.bitcast(F32), ALU.subtract).then_inc(S("att_consts"), 1)

        def block1_out(dve, n):
            if K0 <= n < GA0:
                b, free = evac_ready(dve, n)
                two = b[:, :].rearrange("p (a t) -> p a t", a=2)
                if n < V0:
                    v = dve.tensor_copy(kT[:, 2 * (n - K0):2 * (n - K0) + 2, :], two)
                elif n < U0:
                    v = dve.tensor_copy(vtok[:, :, CW * (n - V0):CW * (n - V0 + 1)], two)
                else:
                    v = dve.tensor_copy(upool[:, 2 * (n - U0):2 * (n - U0) + 2, :], two)
                v.then_inc(free, 1)

        def pooled_gate(dve):
            dve.wait_ge(S(f"proj_free{projection_number(GB0 - 1) % 2}"), projection_number(GB0 - 1) // 2 + 1)
            dve.wait_ge(S(f"proj_free{projection_number(GB0 - 2) % 2}"), projection_number(GB0 - 2) // 2 + 1)
            for g in range(4):
                dve.wait_ge(S("pool_out"), g + 1)
                for half in range(2):
                    k = 2 * g + half
                    v = dve.scalar_tensor_tensor(out=ga[:, k, :], in0=bank[4 + g][:, half * T:(half + 1) * T],
                                                 scalar=col("pool_scale", k), in1=ga[:, k, :],
                                                 op0=ALU.mult, op1=ALU.mult)
                v.then_inc(S("pool_mixed"), 1)

        def block1_dve(dve, lo, o):
            norm_rest(dve, 0)
            for n in range(WIN, WIN + 22):
                lo.upto(n + 2)
                if n == WIN + 3:
                    forget_sums(dve, o)
                block1_out(dve, n)
                if n == GA0:
                    pool_windows(dve, o)
            pooled_gate(dve)
            def row_max(h):
                dve.wait_ge(S("att_scores"), h + 1)
                if h >= 4:
                    dve.wait_ge(S("att_p"), h - 3)
                for qt in range(TT):
                    v = dve.tensor_reduce(att_stat[:, h % 4, qt:qt + 1], bank[2 + h % 2][:, P * qt:P * qt + P * (qt + 1)],
                                          AXX, ALU.max, negate=True)
                v.then_inc(S("att_max"), 1)

            def normalise(h):
                dve.wait_ge(S("att_exp"), h + 1)
                o(dve.reciprocal(att_stat[:, h % 4, 4:6], att_stat[:, h % 4, 2:4]))
                o.wait()
                for qt in range(TT):
                    s = att_s[:, h % 4, P * qt:P * qt + P * (qt + 1)]
                    v = dve.tensor_scalar(s, s, att_stat[:, h % 4, 4 + qt:5 + qt], None, ALU.mult)
                v.then_inc(S("att_p"), 1)

            def gate(k):
                dve.wait_ge(S("att_pv"), 2 * k + 2)
                dve.tensor_tensor(hf[:, k, :], bank[6 + k % 2][:, 0:T], gb[:, k, :], ALU.mult).then_inc(S("att_gated"), 1)
                dve.wait_ge(S("att_gated"), k + 1)
                dve.tensor_tensor(hf[:, k, :], hf[:, k, :], ga[:, k, :], ALU.add).then_inc(S("att_out"), 1)
            for h in range(HEADS + 6):
                if h < HEADS:
                    row_max(h)
                if 1 <= h <= HEADS:
                    normalise(h - 1)
                if h >= 7 and h % 2 == 1:
                    gate((h - 7) // 2)
            dve.wait_ge(S("y1_hi"), 1)
            dve.tensor_tensor(hl[:, :, :], hf[:, :, :], hh[:, :, :].bitcast(F32), ALU.subtract)\
               .then_inc(S("act_split"), 1)
            residual(dve, lo, BASE["w_out"], gt1)

        def pool_windows(dve, o):
            win = big[:, 7 * SLOTW:8 * SLOTW].rearrange("p (b g t) -> p b g t", b=2, g=4)
            src = upool
            for b, free in ((projection_number(U0) % 2, projection_number(U0) // 2 + 1),
                            (projection_number(U0 + 1) % 2, projection_number(U0 + 1) // 2 + 1)):
                dve.wait_ge(S(f"proj_free{b}"), free)
            for level in range(4):
                shift, dst = 1 << level, win[:, level % 2, :, :]
                o(dve.tensor_tensor(dst[:, level:4, shift:T], src[:, level:4, shift:T], src[:, level:4, 0:T - shift],
                                    ALU.add))
                o(dve.tensor_copy(dst[:, level:4, 0:shift], src[:, level:4, 0:shift]))
                o.wait()
                src = dst
            for g, w in enumerate(POOL_WINDOWS):
                s = win[:, g % 2, g, :]
                dve.scalar_tensor_tensor(out=pooled[:, g, 16:T], in0=s[:, 16:T], scalar=1.0 / w, in1=upool[:, g, 16:T],
                                         op0=ALU.mult, op1=ALU.subtract)
                o(dve.tensor_tensor(s[:, 0:16], s[:, 0:16], inv_count[:, g, :], ALU.mult))
            o.wait()
            for g in range(4):
                dve.tensor_tensor(pooled[:, g, 0:16], win[:, g % 2, g, 0:16], upool[:, g, 0:16], ALU.subtract)\
                   .then_inc(S("pooled"), 1)

        res_count = [0]

        def residual(dve, lo, base, gate_bc=None):
            tmp = big[:, 0:2 * 512].rearrange("p (b a c) -> p b a c", b=2, a=TT)
            for j in range(4):
                lo.upto(base + j + 2)
                b, free = evac_ready(dve, base + j)
                two = b[:, :].rearrange("p (a t) -> p a t", a=TT)
                part = x[:, :, j * CW:(j + 1) * CW]
                if gate_bc is not None:
                    dve.tensor_tensor(tmp[:, j % 2], two, gate_bc[:, j * CW:(j + 1) * CW].unsqueeze(1)
                                      .to_broadcast([P, TT, CW]), ALU.mult).then_inc(free, 1)
                    dve.wait_ge(free, projection_number(base + j) // 2 + 1)
                    dve.tensor_tensor(part, part, tmp[:, j % 2], ALU.add).then_inc(S("x_ready"), 1)
                else:
                    dve.tensor_tensor(part, part, two, ALU.add).then_inc(free, 1)
                    dve.wait_ge(free, projection_number(base + j) // 2 + 1)
                    dve.sem_inc(S("x_ready"), 1)
        QRY = BASE["query"]
        NPICK = PEER_HEADS * TOPK
        ring_rows = [big[:, s * D:(s + 1) * D] for s in range(RROWS)]
        keys_rows = big[:, 4 * SLOTW:5 * SLOTW].rearrange("p (j c) -> p j c", c=P)
        keysT = big[:, 6 * SLOTW:7 * SLOTW].rearrange("p (j n) -> p j n", n=NKEYS)
        scores_tok = big[:, 4 * SLOTW:6 * SLOTW].rearrange("p (a n) -> p a n", a=TT)
        query = big[:, 7 * SLOTW:7 * SLOTW + 1024].rearrange("p (b i t) -> p b i t", b=2, i=2)
        one_hot = [big[:, 7 * SLOTW + c:7 * SLOTW + c + 1024].rearrange("p (h k i) -> p h k i", h=4, k=TOPK)
                   for c in (1024, 0)]
        diag = big[:, 7 * SLOTW + 1024:8 * SLOTW].rearrange("p (s n) -> p s n", n=P)
        v_acc = big[:, 6 * SLOTW:7 * SLOTW].rearrange("p (a d) -> p a d", a=TT)
        final_gain = big[:, 5 * SLOTW:5 * SLOTW + D]
        cand = hf[:, :, :].rearrange("p k t -> p (k t)").rearrange("p (h n) -> p h n", h=PEER_HEADS)
        half_s = aux[:, 4096:4608].rearrange("p (a h i k) -> p a h i k", a=TT, h=PEER_HEADS, i=2)
        half_i = aux[:, 4608:5120].bitcast(U32).rearrange("p (a h i k) -> p a h i k", a=TT, h=PEER_HEADS, i=2)
        half_if = aux[:, 5120:5632].rearrange("p (a h i k) -> p a h i k", a=TT, h=PEER_HEADS, i=2)
        sel = aux[:, 5632:5888].bitcast(U32).rearrange("p (a n) -> p a n", a=TT)
        top_s = aux[:, 5888:6144].rearrange("p (a n) -> p a n", a=TT)
        expert = aux[:, 6144:6400].bitcast(I32)
        sel_part = [aux[:, P * i:P * (i + 1)] for i in range(2)]
        sel_key = [aux[:, 256 + P * i:256 + P * (i + 1)] for i in range(2)]
        gates = aux[:, 512:768].rearrange("p (a n) -> p a n", a=TT)
        dots = aux[:, 768:1024]
        gate_sum = small[:, 112:128].rearrange("p (a h) -> p a h", a=TT)
        stage = ctx.enter_context(nc.sbuf_tensor("stage", [P, 2 * RROWS], I32))
        PER = NPICK // RROWS
        V_SHARES = {0: [(0, 5, ()), (5, PER, (0, 4))], 1: [(0, PER, (0, 4))]}

        def diag_before(tt, step0):
            total = 0
            for a in range(TT):
                for s0, s1, mine in V_SHARES[a]:
                    if (a, s0) < (tt, step0):
                        total += (s1 - s0) * (RROWS - len(mine))
            return total

        def keys_pe(pe):
            pe.wait_ge(S("keys"), 16)
            for g in range(4):
                for j in range(4):
                    mm = pe.transpose(bank[4 + g][:, j * P:(j + 1) * P], keys_rows[:, 4 * g + j, :], ident[:, :])
                mm.then_inc(S("keys_tr"), 1)

        def peer_pe(pe):
            pe.wait_ge(S("keysT"), 4)
            norm_pe(pe, 1)
            pe.wait_ge(S("norm_hf"), 8)
            for tt in range(TT):
                for half in range(2):
                    for j in range(4):
                        k = 4 * half + j
                        mm = pe.transpose(bank[4 + 2 * tt + half][:, j * P:(j + 1) * P],
                                          hf[:, k, tt * P:(tt + 1) * P], ident[:, :])
                    mm.then_inc(S("h2tok_tr"), 1)
            pe.wait_ge(S("act_split"), SPLITS["norm1"])

            def key_scores(h):
                pe.wait_ge(S("query"), h + 1)
                if h >= 2:
                    pe.wait_ge(S("key_scores_read"), h - 1)
                for tt in range(TT):
                    for i in range(2):
                        c = (tt * 2 + i) * P
                        mm = pe.matmul(bank[2 + h % 2][:, c:c + P], query[:, h % 2, i, tt * P:(tt + 1) * P],
                                       keysT[:, 2 * h + i, :], start=True, stop=True)
                mm.then_inc(S("key_scores"), 1)
            for h in range(PEER_HEADS + 1):
                if h < PEER_HEADS:
                    project(pe, QRY + h, hh, hl, "F")
                if h >= 1:
                    key_scores(h - 1)
            for tt in range(TT):
                pe.wait_ge(S("v_zero"), TT)
                if tt == 0:
                    pe.wait_ge(S("h2tok"), 4)
                for half in range(2):
                    mm = pe.matmul(bank[4 + 2 * tt + half][:, :], v_acc[:, tt, 0:P],
                                   h2tok[:, tt, half * 512:(half + 1) * 512], start=True, stop=True)
            mm.then_inc(S("v_open"), 1)
            for tt in range(TT):
                for s0, s1, mine in V_SHARES[tt]:
                    own = [s for s in range(RROWS) if s not in mine]
                    with pe.Fori(s0, s1) as it:
                        use = it + PER * (2 * tt + 1)
                        for i, s in enumerate(own):
                            pe.wait_ge(S(f"row{s}"), use * 16 + 16)
                            pe.wait_ge(S("diag"), (it - s0) * len(own) + (diag_before(tt, s0) + i + 1))
                            for half in range(2):
                                mm = pe.matmul(bank[4 + 2 * tt + half][:, :], diag[:, s, :],
                                               ring_rows[s][:, half * 512:(half + 1) * 512],
                                               start=False, stop=True, skip_group_check=True)
                            mm.then_inc(S(f"row_used{s}"), 1)

        def keys_act(act):
            for g in range(4):
                act.wait_ge(S("keys_tr"), g + 1)
                act.activation(keysT[:, 4 * g:4 * g + 4, :], bank[4 + g][:, :], ACT.Copy).then_inc(S("keysT"), 1)

        def peer_act(act, hi):
            norm_act(act, 1, hi)
            for tt in range(TT):
                for half in range(2):
                    act.wait_ge(S("h2tok_tr"), 2 * tt + half + 1)
                    act.activation(h2tok[:, tt, half * 512:(half + 1) * 512], bank[4 + 2 * tt + half][:, :], ACT.Copy)\
                       .then_inc(S("h2tok"), 1)

            def key_scores_out(h):
                act.wait_ge(S("key_scores"), h + 1)
                act.activation(scores_tok[:, :, h * 256:(h + 1) * 256], bank[2 + h % 2][:, :], ACT.Copy)\
                   .then_inc(S("key_scores_read"), 1)
            for h in range(PEER_HEADS + 1):
                if h < PEER_HEADS:
                    hi.upto(QRY + h + 2)
                    b, free = evac_ready(act, QRY + h)
                    if h >= 2:
                        act.wait_ge(S("key_scores"), h - 1)
                    act.activation(query[:, h % 2], b[:, :], ACT.Copy).then_inc(S("query"), 1)
                    act.wait_ge(S("query"), h + 1)
                    act.sem_inc(free, 1)
                if h >= 1:
                    key_scores_out(h - 1)
            hi.upto(QRY + 9)
            for tt in range(TT):
                if tt == 0:
                    gate_exp(act, 0)
                act.wait_ge(S(f"row_used{RROWS - 1}"), PER * (2 * tt + 1))
                act.activation(dots[:, tt * P:(tt + 1) * P], dots[:, tt * P:(tt + 1) * P], ACT.Gelu)\
                   .then_inc(S("gelu"), 1)
                act.wait_ge(S("v_coef"), tt + 1)
                for s0, s1, mine in V_SHARES[tt]:
                    own = [s for s in range(RROWS) if s not in mine]
                    with act.Fori(s0, s1) as it:
                        use = it + PER * (2 * tt + 1)
                        for s in own:
                            act.wait_ge(S(f"row_used{s}"), use)
                            act.activation(diag[:, s, :], ident[:, :], ACT.Copy,
                                           scale=dots[:, bass.ds(it * RROWS + (tt * P + s), 1)]).then_inc(S("diag"), 1)
                    if tt == 0 and s0 == 0:
                        gate_exp(act, 1)
            act.wait_ge(S("experts"), PEER_HEADS // 2 + 2)
            act.dma_start(final_gain, A["final_g"].partition_broadcast(P)).then_inc(S("final_gain"), 16)
            for tt in range(TT):
                act.wait_ge(S("peer_x"), tt + 1)
                act.activation(v_acc[:, tt, :], x[:, tt, :], ACT.Square, accum_out=stat[:, 8 + tt:9 + tt])\
                   .then_inc(S("final_ss"), 1)

        def gate_exp(act, tt):
            act.wait_ge(S("gate_shifted"), tt + 1)
            act.activation(gates[:, tt, :], gates[:, tt, :], ACT.Exp).then_inc(S("gate_exp"), 1)

        def peer_pool(pool):
            norm_pool(pool, 1)
            ring = [s for s in range(RROWS)]

            def gather(table, tt, ph, it, half, picks):
                use = it * 2 + (PER * ph + half)
                if not (isinstance(use, int) and use < 2):
                    for s in ring:
                        pool.wait_ge(S(f"row{s}"), use * 16 - 16)
                staged = stage[:, half * RROWS:(half + 1) * RROWS]
                pool.tensor_copy(staged, expert[:, bass.ds(it * 2 * RROWS + (tt * P + half * RROWS), RROWS)])\
                    .then_inc(S("staged"), 1)
                copies = pool.to_reg(use + 1)
                for s in ring:
                    pool.wait_ge(S("experts"), picks)
                    if s == 0:
                        pool.wait_ge(S("staged"), copies)
                    if not (isinstance(use, int) and use < 1):
                        pool.wait_ge(S(f"row_used{s}"), use)
                    pool.indirect_dma_start(ring_rows[s], None, table,
                                            bass.IndirectOffsetOnAxis(ap=staged[:, s:s + 1], axis=0))\
                        .then_inc(S(f"row{s}"), 16)
            for tt in range(TT):
                for q, table in enumerate((A["peer_u"][0], A["peer_v"][0])):
                    ph = 2 * tt + q
                    if ph == 0:
                        pool.wait_ge(S("experts"), 1)
                        for it in range(2):
                            for half in range(2):
                                gather(table, tt, ph, it, half, 1)
                        with pool.Fori(1, PEER_HEADS // 2) as pair:
                            pool.wait_ge(S("experts"), pair + 1)
                            for j in range(2):
                                for half in range(2):
                                    gather(table, tt, ph, pair * 2 + j, half, 1)
                        continue
                    picks = PEER_HEADS // 2 + 2 * tt
                    pool.wait_ge(S("experts"), picks)
                    with pool.Fori(0, PER // 2) as it:
                        for half in range(2):
                            gather(table, tt, ph, it, half, picks)
            pool.wait_ge(S("final_ss"), TT)
            pool.tensor_scalar(stat[:, 10:12], stat[:, 8:10], 1.0 / D, EPS, ALU.mult, ALU.add).then_inc(S("final_ms"), 1)
            pool.wait_ge(S("final_ms"), 1)
            pool.tensor_tensor(stat[:, 12:14], stat[:, 10:12], stat[:, 6:8], ALU.pow).then_inc(S("final_rstd"), 1)

        def top16(dve, o, values, tops, indices):
            n = range(len(values))
            for b in range(2):
                part = slice(8 * b, 8 * b + 8)
                for i in n:
                    o(dve.max(tops[i][:, part], values[i]))
                o.wait()
                for i in n:
                    o(dve.max_index(indices[i][:, part], tops[i][:, part], values[i]))
                o.wait()
                if b == 0:
                    for i in n:
                        o(dve.match_replace(values[i], tops[i][:, part], values[i], -3e38))
                    o.wait()

        def top_keys(dve, o, tt, heads):
            pairs = [(h, i) for h in heads for i in range(2)]
            top16(dve, o, [scores_tok[:, tt, (2 * h + i) * NKEYS:(2 * h + i + 1) * NKEYS] for h, i in pairs],
                  [half_s[:, tt, h, i, :] for h, i in pairs], [half_i[:, tt, h, i, :] for h, i in pairs])

        def top_experts(dve, o, tt, h0, h1):
            hs, cols, n = slice(h0, h1), slice(h0 * TOPK, h1 * TOPK), h1 - h0
            hot = one_hot[tt][:, 0:n]
            o(dve.tensor_copy(half_if[:, tt, hs], half_i[:, tt, hs]))
            o(dve.tensor_tensor(cand[:, hs, :].rearrange("p h (i j) -> p h i j", j=TOPK),
                                half_s[:, tt, hs, 0, :].unsqueeze(3).to_broadcast([P, n, TOPK, TOPK]),
                                half_s[:, tt, hs, 1, :].unsqueeze(2).to_broadcast([P, n, TOPK, TOPK]), ALU.add))
            o.wait()
            heads = range(h0, h1)
            top16(dve, o, [cand[:, h, :] for h in heads], [top_s[:, tt, h * TOPK:(h + 1) * TOPK] for h in heads],
                  [sel[:, tt, h * TOPK:(h + 1) * TOPK] for h in heads])
            su = [p.bitcast(U32)[:, cols] for p in sel_part]
            o(dve.tensor_scalar(su[0], sel[:, tt, cols], 4, None, ALU.logical_shift_right))
            o(dve.tensor_scalar(su[1], sel[:, tt, cols], 15, None, ALU.bitwise_and))
            o.wait()
            for i in range(2):
                o(dve.tensor_scalar(sel_key[i][:, cols], su[i], 1.0, None, ALU.add))
            o.wait()
            for i in range(2):
                o(dve.tensor_copy(sel_part[i][:, cols], sel_key[i][:, cols]))
            o.wait()
            rank = small[:, 80:96].unsqueeze(1).unsqueeze(1).to_broadcast([P, n, TOPK, TOPK])
            for i in range(2):
                picked = sel_part[i][:, cols].rearrange("p (h k) -> p h k", k=TOPK)
                o(dve.tensor_tensor(hot, picked.unsqueeze(3).to_broadcast([P, n, TOPK, TOPK]), rank, ALU.is_equal))
                o.wait()
                o(dve.tensor_tensor(hot, hot, half_if[:, tt, hs, i, :].unsqueeze(2).to_broadcast([P, n, TOPK, TOPK]),
                                    ALU.mult))
                o.wait()
                o(dve.tensor_reduce(sel_key[i][:, cols].rearrange("p (h k) -> p h k", k=TOPK), hot, AXX, ALU.add))
                o.wait()
            dve.scalar_tensor_tensor(out=expert[:, tt * P:(tt + 1) * P][:, cols], in0=sel_key[0][:, cols],
                                     scalar=float(NKEYS), in1=sel_key[1][:, cols], op0=ALU.mult, op1=ALU.add)\
               .then_inc(S("experts"), 1)

        def softmax_gates(dve, o, tt):
            best = top_s[:, tt, :].rearrange("p (h k) -> p h k", k=TOPK)
            dve.tensor_tensor(gates[:, tt, :].rearrange("p (h k) -> p h k", k=TOPK), best,
                              best[:, :, 0:1].to_broadcast([P, PEER_HEADS, TOPK]), ALU.subtract)\
               .then_inc(S("gate_shifted"), 1)
            dve.wait_ge(S("gate_exp"), tt + 1)
            g3 = gates[:, tt, :].rearrange("p (h k) -> p h k", k=TOPK)
            o(dve.tensor_reduce(gate_sum[:, tt, :], g3, AXX, ALU.add))
            o.wait()
            o(dve.reciprocal(gate_sum[:, tt, :], gate_sum[:, tt, :]))
            o.wait()
            o(dve.tensor_tensor(g3, g3, gate_sum[:, tt, :].unsqueeze(2).to_broadcast([P, PEER_HEADS, TOPK]), ALU.mult))
            o.wait()

        def dot_products(dve, tt, first, last):
            with dve.Fori(first, last) as it:
                use = it + PER * 2 * tt
                for s in range(RROWS):
                    dve.wait_ge(S(f"row{s}"), use * 16 + 16)
                    dve.scalar_tensor_tensor(out=ring_rows[s], in0=ring_rows[s], scalar=1.0, in1=h2tok[:, tt, :],
                                             op0=ALU.mult, op1=ALU.mult,
                                             accum_out=dots[:, bass.ds(it * RROWS + (tt * P + s), 1)])\
                       .then_inc(S(f"row_used{s}"), 1)

        def peer_dve(dve, lo, o):
            norm_dve(dve, 1, None)

            def rank_keys(h):
                lo.upto(min(QRY + h + 4, QRY + 9))
                dve.wait_ge(S("key_scores_read"), h + 1)
                top_keys(dve, o, 0, [h])
            lo.upto(QRY + 3)
            dve.wait_ge(S("h2tok"), 4)
            for pair in range(PEER_HEADS // 2):
                for h in (2 * pair, 2 * pair + 1):
                    rank_keys(h)
                if pair == PEER_HEADS // 2 - 1:
                    for tt in range(TT):
                        dve.memset(v_acc[:, tt, :], 0.0).then_inc(S("v_zero"), 1)
                for first, last in {1: [(0, 1)], 2: [(2, 4)], 3: [(6, 8)]}.get(pair, []):
                    dot_products(dve, 0, first, last)
                top_experts(dve, o, 0, 2 * pair, 2 * pair + 2)
                for first, last in {1: [(1, 2)], 2: [(4, 6)]}.get(pair, []):
                    dot_products(dve, 0, first, last)
            softmax_gates(dve, o, 0)
            for tt in range(TT):
                if tt == 0:
                    dot_products(dve, 0, 8, PER)
                else:
                    dot_products(dve, tt, 0, PER)
                dve.wait_ge(S("gelu"), tt + 1)
                dve.tensor_tensor(dots[:, tt * P:(tt + 1) * P], dots[:, tt * P:(tt + 1) * P], gates[:, tt, :], ALU.mult)\
                   .then_inc(S("v_coef"), 1)
                if tt == 0:
                    top_keys(dve, o, 1, range(PEER_HEADS))
                    for quad in range(2):
                        top_experts(dve, o, 1, 4 * quad, 4 * quad + 4)
                    softmax_gates(dve, o, 1)
                dve.wait_ge(S("v_coef"), tt + 1)
                for s0, s1, mine in V_SHARES[tt]:
                    if not mine:
                        continue
                    with dve.Fori(s0, s1) as it:
                        use = it + PER * (2 * tt + 1)
                        for i, s in enumerate(mine):
                            dve.wait_ge(S(f"row{s}"), use * 16 + 16)
                            dve.wait_ge(S(f"row_used{mine[i - 1]}"), use + min(i, 1))
                            dve.scalar_tensor_tensor(out=v_acc[:, tt, :], in0=ring_rows[s],
                                                     scalar=dots[:, bass.ds(it * RROWS + (tt * P + s), 1)],
                                                     in1=v_acc[:, tt, :], op0=ALU.mult, op1=ALU.add)\
                               .then_inc(S(f"row_used{s}"), 1)
            for tt in range(TT):
                for s in (RROWS - 1, V_SHARES[tt][-1][2][-1]):
                    dve.wait_ge(S(f"row_used{s}"), PER * (2 * tt + 2))
                for half in range(2):
                    part = slice(half * 512, (half + 1) * 512)
                    o(dve.tensor_tensor(v_acc[:, tt, part], v_acc[:, tt, part], bank[4 + 2 * tt + half][:, :], ALU.add))
                o.wait()
                o(dve.tensor_tensor(v_acc[:, tt, :], v_acc[:, tt, :], gt2, ALU.mult))
                o.wait()
                dve.tensor_tensor(x[:, tt, :], x[:, tt, :], v_acc[:, tt, :], ALU.add).then_inc(S("peer_x"), 1)
            dve.wait_ge(S("final_rstd"), 1)
            dve.wait_ge(S("final_gain"), 16)
            for tt in range(TT):
                dve.scalar_tensor_tensor(out=x[:, tt, :], in0=x[:, tt, :], scalar=stat[:, 12 + tt:13 + tt], in1=final_gain,
                                         op0=ALU.mult, op1=ALU.mult).then_inc(S("x_ready"), 1)

        RKV = BASE["rkv"]
        dx, gate_fm = fm(bigs(0)), fm(bigs(0))
        mixed = [fm(bigs(1)), fm(bigs(2))]
        rT, kkT, keyT, vrw, sig, aT = fm(bigs(3)), fm(bigs(1)), fm(bigs(4)), tm(bigs(5)), fm(bigs(6)), fm(bigs(7))
        scratch, kk_squares, growth = fm(bigs(2)), fm(aux[:, 0:SLOTW]), fm(aux[:, 2 * SLOTW:3 * SLOTW])
        lw1 = aux[:, 0:512].rearrange("p (k c) -> p k c", k=KT)
        la1 = aux[:, 512:1024].rearrange("p (k c) -> p k c", k=KT)
        lg1 = aux[:, 1024:2304].rearrange("p (k c) -> p k c", k=KT)
        lw2, la2 = aux[0:LORA, 2304:3328], aux[LORA:2 * LORA, 2304:3328]
        lg2 = [aux[:, 3328:4352], aux[0:LORA_G - P, 4352:5376]]
        mid_w, mid_a = amask[0:LORA, 0:T], amask[LORA:2 * LORA, 0:T]
        mid_g = [big[:, 5 * SLOTW:5 * SLOTW + T], big[0:LORA_G - P, 5 * SLOTW + T:5 * SLOTW + 2 * T]]
        tile_mid = small[:, 128:144]
        y_stat, y_mean, bonus = small[:, 144:176], small[:, 176:208], small[:, 208:240]
        carry = small[:, 240:248]
        one_minus_ka = small[:, 248:256]
        flat = "p k t -> p (k t)"
        tok_bk = bigs(6)
        y_tok = hf[:, :, :].rearrange(flat)

        def head_groups(tile2048):
            return tile2048.rearrange("p (g c) -> p g c", c=DH)

        mats = [[aux[:, 512 * i:512 * (i + 1)] for i in range(7)],
                [aux[:, 3584 + 512 * i:3584 + 512 * (i + 1)] for i in range(5)]
                + [big[:, 2 * SLOTW + 512 * i:2 * SLOTW + 512 * (i + 1)] for i in range(2)]]
        vecs = [[big[:, 2 * SLOTW + 1024 + 256 * (2 * g + i):2 * SLOTW + 1024 + 256 * (2 * g + i + 1)] for i in range(2)]
                for g in range(2)]
        state = [aux[:, 6144:6400].rearrange("p (k c) -> p k c", c=DH), amask[:, 0:256].rearrange("p (k c) -> p k c", c=DH)]
        PAIRS = [(tt, qq) for tt in range(TT) for qq in range(2)]
        STAGES = 11
        ACT_STAGES = [1, 2, 3, 5, 6, 7, 10]

        def event(pr, st, g):
            return (pr * STAGES + st) * 2 + g + 1

        def dve_event(pr, st, g):
            return event(pr, st, g) - 2 * max(0, pr - 2)

        def act_event(pr, st, g):
            return (pr * len(ACT_STAGES) + ACT_STAGES.index(st)) * 2 + g + 1

        def masks_pool(pool):
            o = pool_order[0]
            for m in (low16, low_far, up16, up_strict, up_incl, head_pick[:, :, :], half_ones[:, :],
                      head_rows[:, :]):
                o(pool.memset(m, 1.0))
            o.wait()

            def keep(m, pattern, base, mult, op):
                o(pool.affine_select(out=m, in_=m, compare_op=op, fill=0.0, base=base, pattern=pattern,
                                     channel_multiplier=mult))
                o.wait()
            start, end = [[-16, 8], [0, 16]], [[16, 8], [0, 16]]
            keep(low16, start, 0, 1, ALU.is_ge)
            keep(low16, end, 15, -1, ALU.is_ge)
            keep(low16, [[-1, P]], 0, 1, ALU.is_gt)
            keep(low_far, start, -16, 1, ALU.is_ge)
            keep(up16, start, 0, 1, ALU.is_ge)
            keep(up16, end, 15, -1, ALU.is_ge)
            keep(up16, [[1, P]], 0, -1, ALU.is_gt)
            keep(up_strict, [[1, P]], 0, -1, ALU.is_gt)
            keep(up_incl, [[1, P]], 0, -1, ALU.is_ge)
            keep(head_pick[:, :, :], [[P, KT // 2], [-DH, HEADS // 2]], 0, 1, ALU.is_ge)
            keep(head_pick[:, :, :], [[-P, KT // 2], [DH, HEADS // 2]], DH - 1, -1, ALU.is_ge)
            keep(head_rows[:, :], [[1, D // 2]], 0, -DH, ALU.is_ge)
            keep(head_rows[:, :], [[-1, D // 2]], DH - 1, DH, ALU.is_ge)
            keep(half_ones[:, :], [[-DH, 2]], 0, 1, ALU.is_ge)
            pool.affine_select(out=half_ones[:, :], in_=half_ones[:, :], compare_op=ALU.is_ge, fill=0.0, base=DH - 1,
                               pattern=[[DH, 2]], channel_multiplier=-1).then_inc(S("masks"), 1)

        def lora_loads(act):
            act.wait_ge(S("x_ready"), XREADY[2])
            for dst, src in ((lw1, A["rwkv_w1_2"][0].rearrange("(k p) c -> p k c", p=P)),
                             (la1, A["rwkv_a1_2"][0].rearrange("(k p) c -> p k c", p=P)),
                             (lg1, A["rwkv_g1_2"][0].rearrange("(k p) c -> p k c", p=P)),
                             (lw2, A["rwkv_w2_2"][0]), (la2, A["rwkv_a2_2"][0]),
                             (lg2[0], A["rwkv_g2_2"][0, 0:P]), (lg2[1], A["rwkv_g2_2"][0, P:LORA_G])):
                act.dma_start(dst, src).then_inc(S("lora_w"), 16)

        head_rstd = aux[0:HEADS // 2, SLOTW:SLOTW + 2 * T]

        def head_sums_pe(pe, i, squares):
            pe.wait_ge(S("head_squares"), 4 * (i + 1))
            for k in range(KT):
                half, i = k // 4, k % 4
                mm = pe.matmul(bank[4][0:HEADS // 2, half * T:(half + 1) * T], head_pick[:, i, :], squares[:, k, :],
                               start=(i == 0), stop=(i == 3))
            mm.then_inc(S("head_sums"), 1)

        def head_spread_pe(pe, i):
            pe.wait_ge(S("head_rstd"), i + 1)
            for kp in range(4):
                for k in (2 * kp, 2 * kp + 1):
                    mm = pe.matmul(bank[4 + kp][:, (k % 2) * T:(k % 2 + 1) * T], head_rows[:, (k % 4) * P:(k % 4 + 1) * P],
                                   head_rstd[:, (k // 4) * T:(k // 4 + 1) * T], start=True, stop=True)
                mm.then_inc(S("head_spread"), 1)

        def head_root_act(act, i):
            act.wait_ge(S("head_ms"), i + 1)
            act.activation(head_rstd, head_rstd, ACT.Sqrt).then_inc(S("head_root"), 1)

        def head_inverse_dve(dve, i):
            dve.wait_ge(S("head_root"), i + 1)
            dve.reciprocal(head_rstd, head_rstd).then_inc(S("head_rstd"), 1)

        def head_guard_dve(dve, i, scale, guard, op0, op1):
            dve.wait_ge(S("head_sums"), i + 1)
            dve.tensor_scalar(head_rstd, bank[4][0:HEADS // 2, :], scale, guard, op0, op1).then_inc(S("head_ms"), 1)

        def head_scale_dve(dve, i, values, gain):
            for kp in range(4):
                dve.wait_ge(S("head_spread"), 4 * i + kp + 1)
                part = values[:, 2 * kp:2 * kp + 2, :]
                dve.scalar_tensor_tensor(out=part, in0=part, scalar=gain, in1=bank[4 + kp][:, :]
                                         .rearrange("p (a t) -> p a t", a=2), op0=ALU.mult, op1=ALU.mult)\
                   .then_inc(S("head_normed"), 1)

        def rwkv_pe(pe):
            norm_pe(pe, 3)
            keep_warm(pe, 16)
            pe.wait_ge(S("act_split"), SPLITS["mix_r"])
            for n in range(RKV, RKV + 4):
                project(pe, n, hh, hl, "F")
            pe.wait_ge(S("lora_w"), 16 * 7)
            for m, (w, o_) in enumerate(((lw1, bank[2][0:LORA, 0:T]), (la1, bank[3][LORA:2 * LORA, 0:T]))):
                pe.wait_ge(S("mixed"), 2 + m)
                for k in range(KT):
                    mm = pe.matmul(o_, w[:, k, :], mixed[(1 + m) % 2][:, k, :], start=(k == 0), stop=(k == KT - 1))
                mm.then_inc(S("lora_mid"), 1)
            pe.wait_ge(S("mixed"), 4)
            for b, c0, c1 in ((6, 0, P), (7, P, LORA_G)):
                for k in range(KT):
                    mm = pe.matmul(bank[b][0:c1 - c0, 0:T], lg1[:, k, c0:c1], mixed[1][:, k, :],
                                   start=(k == 0), stop=(k == KT - 1))
            mm.then_inc(S("lora_mid"), 1)
            for m in range(3):
                pe.wait_ge(S("lora_act"), m + 1)
                for kp in range(4):
                    q = 4 * m + kp
                    if q >= 2:
                        pe.wait_ge(S("lora_out_read"), q - 1)
                    for k in (2 * kp, 2 * kp + 1):
                        o_ = bank[4 + q % 2][:, (k % 2) * T:(k % 2 + 1) * T]
                        cols = slice(k * P, (k + 1) * P)
                        if m < 2:
                            mm = pe.matmul(o_, (lw2, la2)[m][:, cols], (mid_w, mid_a)[m], start=True, stop=True)
                        else:
                            pe.matmul(o_, lg2[0][:, cols], mid_g[0], start=True, stop=False)
                            mm = pe.matmul(o_, lg2[1][:, cols], mid_g[1], start=False, stop=True)
                    mm.then_inc(S("lora_out"), 1)
            pe.wait_ge(S("act_split"), SPLITS["mix_k"])
            for n in range(RKV + 4, RKV + 8):
                project(pe, n, hh, hl, "F")
            pe.wait_ge(S("act_split"), SPLITS["mix_v"])
            for j in range(4):
                project(pe, RKV + 8 + j, hh, hl, "T")
                if j == 0:
                    pe.wait_ge(S("masks"), 1)
                    pe.wait_ge(S("lora_out_read"), 12)
                    head_sums_pe(pe, 0, kk_squares)
                if j == 1:
                    head_spread_pe(pe, 0)
                if j == 2:
                    pe.wait_ge(S("bonus_rk"), 1)
                    for tt in range(TT):
                        for k in range(KT):
                            mm = pe.matmul(bank[2][:, tt * HEADS + 2 * k:tt * HEADS + 2 * k + 2],
                                           scratch[:, k, tt * P:(tt + 1) * P], half_ones[:, :], start=True, stop=True)
                    mm.then_inc(S("bonus_sum"), 1)
            pe.wait_ge(S("wkv_in"), 2)
            for w, src in enumerate((aT, keyT)):
                for half in range(2):
                    for j in range(4):
                        mm = pe.transpose(bank[4 + 2 * w + half][:, j * P:(j + 1) * P], src[:, 4 * half + j, 0:P],
                                          ident[:, :])
                    mm.then_inc(S("bk_turned"), 1)
            pe.wait_ge(S("bk_tok"), 4)
            pe.wait_ge(S("bonus_read"), 1)
            for b in range(2):
                pe.wait_ge(S(f"proj_free{b}"), (projection_number(RKV + 12) + 1 - b) // 2)
            for pr, (tt, qq) in enumerate(PAIRS):
                for st in range(STAGES):
                    for g in range(2):
                        wkv_stage(pe, pr, tt, qq, st, g)
            pe.wait_ge(S("wkv_act"), act_event(len(PAIRS) - 1, STAGES - 1, 1))
            keep_warm(pe, 26)
            pe.wait_ge(S("mix_normed"), 1)
            pe.wait_ge(S("bonus_v"), 1)
            for kp in range(4):
                for b, src in ((4 + kp, y_tok), (kp, bigs(5))):
                    for k in (2 * kp, 2 * kp + 1):
                        for tt in range(TT):
                            mm = pe.transpose(bank[b][:, (k % 2) * T + tt * P:(k % 2) * T + (tt + 1) * P],
                                              src[:, tt * D + k * P:tt * D + (k + 1) * P], ident[:, :])
                mm.then_inc(S("mix_turned"), 1)
            pe.wait_ge(S("mix_scaled"), 4)
            keep_warm(pe, 8)
            pe.wait_ge(S("act_split"), SPLITS["rwkv_y"])
            for n in range(BASE["rwkv_o"], BASE["rwkv_o"] + 4):
                project(pe, n, hh, hl, "T")

        def wkv_stage(pe, pr, tt, qq, st, g):
            b = bank[4 * g:4 * g + 4]
            mD, mDt, mD2, mD2t, mT, mE, mK = mats[g]
            xin, u = vecs[g]
            if st > 0 or pr > 0:
                prev = (pr, st - 1) if st else (pr - 1, STAGES - 1)
                if not (prev[1] == STAGES - 1 and prev[0] >= 2):
                    pe.wait_ge(S("wkv_dve"), dve_event(*prev, g))
                if prev[1] in ACT_STAGES:
                    pe.wait_ge(S("wkv_act"), act_event(*prev, g))
            tok = slice(tt * P, (tt + 1) * P)
            for i in range(4):
                h, k = 8 * qq + 2 * i + g, 4 * qq + i
                ch = slice(g * DH, (g + 1) * DH)
                al, be, ka, rh = (t[ch, k, tok] for t in (kkT, aT, keyT, rT))
                v = vrw[:, tt, h * DH:(h + 1) * DH]
                s_in = state[qq][ch, i, :]
                c = slice(i * P, (i + 1) * P)
                d = slice(i * DH, (i + 1) * DH)

                def mul(bk, cols, lhsT, rhs, start=True, stop=True):
                    return pe.matmul(b[bk][:, cols], lhsT, rhs, start=start, stop=stop)
                if st == 0:
                    mul(0, c, al, be)
                    mul(1, c, be, al)
                    mm = mul(2, c, ka, al)
                elif st == 1:
                    mul(0, c, mDt[:, c], mD[:, c])
                    mm = mul(1, c, mD[:, c], mDt[:, c])
                elif st == 2:
                    mul(0, c, mD2t[:, c], mD2[:, c])
                    mul(1, c, mD2[:, c], mD2t[:, c])
                    mm = mul(2, c, mD2[:, c], mT[:, c])
                elif st == 3:
                    mul(0, c, mDt[:, c], mD[:, c])
                    mm = mul(1, c, mD[:, c], mT[:, c])
                elif st == 4:
                    mm = mul(0, c, mD2[:, c], mT[:, c])
                elif st == 5:
                    mul(0, c, mT[:, c], mE[:, c])
                    mul(1, c, mE[:, c], mT[:, c])
                    mm = mul(2, d, mK[:, c], v, stop=(tt == 0))
                    if tt:
                        mm = mul(2, d, al, s_in, start=False)
                elif st == 6:
                    mul(0, c, mD[:, c], mD2t[:, c])
                    mul(1, c, mD2t[:, c], mD[:, c])
                    mul(2, d, mT[:, c], xin[:, d])
                    mm = mul(3, c, be, rh)
                elif st == 7:
                    mul(0, c, mE[:, c], mDt[:, c])
                    mul(1, d, mD[:, c], u[:, d])
                    mm = mul(3, c, ka, rh)
                elif st == 8:
                    mm = mul(0, d, mDt[:, c], u[:, d])
                elif st == 9:
                    mm = mul(0, d, mD2[:, c], u[:, d])
                else:
                    mul(0, d, mK[:, c], u[:, d], stop=False)
                    mm = mul(0, d, mD2t[:, c], v, start=False, stop=(tt == 0))
                    if tt:
                        mm = mul(0, d, rh, s_in, start=False)
                    else:
                        o_ = b[1][ch, d]
                        pe.matmul(o_, tok_bk[:, h * DH:(h + 1) * DH], u[:, d], start=True, stop=False)
                        mm = pe.matmul(o_, tok_bk[:, D + h * DH:D + (h + 1) * DH], v, start=False, stop=True)
            mm.then_inc(S("wkv_mm"), 1)

        def wkv_act(act):
            for pr, (tt, qq) in enumerate(PAIRS):
                for st in ACT_STAGES:
                    for g in range(2):
                        b = bank[4 * g:4 * g + 4]
                        mD, mDt, mD2, mD2t, mT, mE, mK = mats[g]
                        xin, u = vecs[g]
                        act.wait_ge(S("wkv_mm"), event(pr, st, g))
                        y_group = y_tok[:, tt * D + qq * 512:tt * D + (qq + 1) * 512]\
                            .rearrange("p (i g c) -> p i g c", g=2, c=DH)[:, :, g, :]
                        y_bank = b[0][:, 0:T].rearrange("p (i c) -> p i c", c=DH)
                        moves = {1: [(mD2, b[0][:, :])], 2: [(mD, b[0][:, :])], 3: [(mD2, b[0][:, :])],
                                 5: [(mD2t, b[0][:, :]), (xin, b[2][:, 0:T])], 6: [(mE, b[0][:, :]), (u, b[2][:, 0:T])],
                                 7: [(mD2, b[0][:, :])],
                                 10: [(y_group, y_bank)]}[st]
                        for dst, src in moves:
                            a = act.activation(dst, src, ACT.Copy)
                        a.then_inc(S("wkv_act"), 1)

        def wkv_dve(dve):
            def heads(m):
                return m.rearrange("p (h n) -> p h n", h=4)

            def each(mask):
                return mask.unsqueeze(1).to_broadcast([P, 4, P])
            for pr, (tt, qq) in enumerate(PAIRS):
                for st in range(STAGES):
                    for g in range(2):
                        b = [x_[:, :] for x_ in bank[4 * g:4 * g + 4]]
                        mD, mDt, mD2, mD2t, mT, mE, mK = mats[g]
                        xin, u = vecs[g]
                        ch = slice(g * DH, (g + 1) * DH)
                        if st == STAGES - 1 and tt == TT - 1:
                            continue
                        dve.wait_ge(S("wkv_mm"), event(pr, st, g))
                        if st == 0:
                            dve.tensor_tensor(heads(mDt), heads(b[1]), each(up16), ALU.mult).then_inc(S("wkv_dt"), 1)
                            dve.tensor_tensor(heads(mD), heads(b[0]), each(low16), ALU.mult)
                            dve.tensor_tensor(heads(mE), heads(b[0]), each(low_far), ALU.mult)
                            dve.tensor_tensor(heads(mK), heads(b[2]), each(up_strict), ALU.mult)
                            dve.wait_ge(S("wkv_dt"), 2 * pr + g + 1)
                            v = dve.tensor_tensor(heads(mT), heads(mDt), each(ident[:, :]), ALU.add)
                        elif st == 1:
                            v = dve.tensor_copy(mD2t, b[1])
                        elif st == 2:
                            dve.tensor_copy(mDt, b[1])
                            v = dve.tensor_tensor(mT, mT, b[2], ALU.add)
                        elif st == 3:
                            v = dve.tensor_tensor(mT, mT, b[1], ALU.add)
                        elif st == 4:
                            v = dve.tensor_tensor(mT, mT, b[0], ALU.add)
                        elif st == 5:
                            v = dve.tensor_copy(mD, b[1])
                        elif st == 6:
                            dve.tensor_copy(mDt, b[1])
                            v = dve.tensor_tensor(heads(mK), heads(b[3]), each(up_incl), ALU.mult)
                        elif st == 7:
                            dve.tensor_tensor(heads(mD2t), heads(b[3]), each(up_incl), ALU.mult)
                            v = dve.tensor_tensor(u, u, b[1][:, 0:T], ALU.add)
                        elif st in (8, 9):
                            v = dve.tensor_tensor(u, u, b[0][:, 0:T], ALU.add)
                        else:
                            carried = carry[ch, 4 * qq:4 * qq + 4].unsqueeze(2).to_broadcast([DH, 4, DH])
                            v = dve.tensor_tensor(state[qq][ch, :, :], b[1][ch, 0:T].rearrange("p (i c) -> p i c", c=DH),
                                                  carried, ALU.mult)
                        v.then_inc(S("wkv_dve"), 1)

        def rwkv_act(act, hi):
            norm_act(act, 3, hi)
            def mix_hi(i, position):
                act.wait_ge(S("mixed"), position)
                act.wait_ge(S("slot_done"), RKV + 4 * i)
                act.activation(hh[:, :, :], mixed[(position - 1) % 2], ACT.Copy).then_inc(S("mix_hi"), 1)
            mix_hi(0, 1)
            for j in range(4):
                hi.upto(RKV + j + 2)
                b, free = evac_ready(act, RKV + j)
                act.activation(rT[:, 2 * j:2 * j + 2, :], b[:, :], ACT.Copy).then_inc(free, 1)
            act.wait_ge(S("lora_mid"), 1)
            act.activation(mid_w, bank[2][0:LORA, 0:T], ACT.Tanh).then_inc(S("lora_act"), 1)
            act.wait_ge(S("lora_mid"), 2)
            act.activation(mid_a, bank[3][LORA:2 * LORA, 0:T], ACT.Copy).then_inc(S("lora_act"), 1)
            mix_hi(1, 5)
            act.wait_ge(S("lora_mid"), 3)
            act.activation(mid_g[0], bank[6][:, 0:T], ACT.Sigmoid)
            act.activation(mid_g[1], bank[7][0:LORA_G - P, 0:T], ACT.Sigmoid).then_inc(S("lora_act"), 1)
            for q in range(12):
                m, kp = q // 4, q % 4
                act.wait_ge(S("lora_out"), q + 1)
                if q == 8:
                    act.wait_ge(S("mixed"), 6)
                for k in (2 * kp, 2 * kp + 1):
                    src = bank[4 + q % 2][:, (k % 2) * T:(k % 2 + 1) * T]
                    if m == 2:
                        a = act.activation(gate_fm[:, k, :], src, ACT.Copy)
                    else:
                        a = act.activation((sig, aT)[m][:, k, :], src, ACT.Sigmoid, bias=col(("w0", "a0")[m], k))
                a.then_inc(S("lora_out_read"), 1)
                if q == 3:
                    hi.upto(RKV + 6)
            act.wait_ge(S("act_split"), SPLITS["mix_k"])
            for j in range(4):
                hi.upto(RKV + 4 + j + 2)
                b, free = evac_ready(act, RKV + 4 + j)
                act.activation(keyT[:, 2 * j:2 * j + 2, :], b[:, :], ACT.Copy)
                for k in (2 * j, 2 * j + 1):
                    src = b[:, (k % 2) * T:(k % 2 + 1) * T]
                    act.activation(kkT[:, k, :], src, ACT.Copy, scale=col("k_k", k))
                    a = act.activation(kk_squares[:, k, :], src, ACT.Square, scale=col("k_k", k))
                a.then_inc(S("head_squares"), 1)
                act.wait_ge(S("head_squares"), j + 1)
                act.sem_inc(free, 1)
            mix_hi(2, 6)
            hi.upto(RKV + 10)
            act.wait_ge(S("one_minus_ka"), 1)
            act.wait_ge(S("act_split"), SPLITS["mix_v"])
            for k in range(KT):
                a = act.activation(scratch[:, k, :], aT[:, k, :], ACT.Identity, scale=col("k_a", k),
                                   bias=one_minus_ka[:, k:k + 1])
            a.then_inc(S("key_factor"), 1)
            act.wait_ge(S("decay_sums"), 1)
            act.activation(growth, hf[:, :, :], ACT.Exp, scale=DECAY).then_inc(S("decays"), 1)
            act.wait_ge(S("decays"), 1)
            act.activation(carry, carry, ACT.Exp, scale=-DECAY)
            act.activation(hf[:, :, :], hf[:, :, :], ACT.Exp, scale=-DECAY).then_inc(S("decays"), 1)
            act.activation(sig, sig, ACT.Exp, scale=-DECAY).then_inc(S("decays"), 1)
            hi.upto(RKV + 11)
            head_root_act(act, 0)
            hi.upto(RKV + 13)
            act.wait_ge(S("wkv_in"), 4)
            for j in range(4):
                act.wait_ge(S("bk_turned"), j + 1)
                act.activation(tok_bk[:, j * 512:(j + 1) * 512], bank[4 + j][:, :], ACT.Copy).then_inc(S("bk_tok"), 1)
            wkv_act(act)
            act.wait_ge(S("y_centred"), 1)
            act.activation(bigs(2), y_tok, ACT.Square).then_inc(S("y_square"), 1)
            act.wait_ge(S("y_ms"), 1)
            act.activation(y_stat, y_stat, ACT.Sqrt).then_inc(S("y_root"), 1)
            act.wait_ge(S("mix_normed"), 1)
            for kp in range(4):
                act.wait_ge(S("mix_turned"), kp + 1)
                for k in (2 * kp, 2 * kp + 1):
                    a = act.activation(scratch[:, k, :], bank[4 + kp][:, (k % 2) * T:(k % 2 + 1) * T], ACT.Identity,
                                       scale=col("ln_g", k), bias=col("ln_b", k))
                a.then_inc(S("y_affine"), 1)
            act.wait_ge(S("mix_scaled"), 4)
            act.activation(hh[:, :, :], scratch, ACT.Copy).then_inc(S("mix_out_hi"), 1)
            hi.upto(BASE["rwkv_o"] + 5)

        def rwkv_dve(dve, lo, o):
            norm_dve(dve, 3, lambda k: col("mix0", k))
            dve.wait_ge(S("norm_hf"), 16)
            o(dve.tensor_scalar(dx[:, :, 0:1], hf[:, :, 0:1], -1.0, None, ALU.mult))
            o(dve.tensor_tensor(dx[:, :, 1:T], hf[:, :, 0:T - 1], hf[:, :, 1:T], ALU.subtract))
            o.wait()

            def mix(position, m):
                for k in range(KT):
                    v = dve.scalar_tensor_tensor(out=mixed[(position - 1) % 2][:, k, :], in0=dx[:, k, :],
                                                 scalar=col(f"mu{m}", k), in1=hf[:, k, :], op0=ALU.mult, op1=ALU.add)
                v.then_inc(S("mixed"), 1)

            def rest(i, position):
                dve.wait_ge(S("mix_hi"), i + 1)
                dve.tensor_tensor(hl[:, :, :], mixed[(position - 1) % 2], hh[:, :, :].bitcast(F32), ALU.subtract)\
                   .then_inc(S("act_split"), 1)
            mix(1, 0)
            rest(0, 1)
            mix(2, 3)
            lo.upto(RKV + 2)
            dve.wait_ge(S("act_split"), SPLITS["mix_r"])
            mix(3, 4)
            dve.tensor_scalar(one_minus_ka, vec[:, COL["k_a"]:COL["k_a"] + KT], -1.0, 1.0, ALU.mult, ALU.add)\
               .then_inc(S("one_minus_ka"), 1)
            lo.upto(RKV + 5)
            dve.wait_ge(S("lora_mid"), 1)
            mix(4, 5)
            dve.wait_ge(S("lora_mid"), 2)
            mix(5, 1)
            rest(1, 5)
            dve.wait_ge(S("lora_mid"), 3)
            mix(6, 2)
            sums = hf[:, :, :].rearrange(flat)
            sig_flat = bigs(6)
            dve.wait_ge(S("mixed"), 6)
            dve.wait_ge(S("lora_out_read"), 4)
            for j in range(KT * TT):
                o(dve.tensor_tensor_scan(sums[:, j * P:(j + 1) * P], ones[:, 0:P], sig_flat[:, j * P:(j + 1) * P], 0.0,
                                         ALU.mult, ALU.add))
            lo.upto(RKV + 6)
            o.wait()
            tiles = sums.rearrange("p (j t) -> p j t", t=P)
            o(dve.tensor_copy(tile_mid.unsqueeze(2), tiles[:, :, P // 2 - 1:P // 2]))
            o.wait()
            o(dve.tensor_tensor(tiles, tiles, tile_mid.unsqueeze(2).to_broadcast([P, KT * TT, P]), ALU.subtract))
            o.wait()
            lo.upto(RKV + 7)
            o(dve.tensor_tensor(sig_flat, sums, sig_flat, ALU.subtract))
            o(dve.tensor_tensor(carry.unsqueeze(2), tiles.rearrange("p (k a) t -> p k a t", a=TT)[:, :, 0, P - 1:P],
                                tile_mid.rearrange("p (k a) -> p k a", a=TT)[:, :, 1:2], ALU.add))
            o.wait()
            dve.sem_inc(S("decay_sums"), 1)
            lo.upto(RKV + 9)
            rest(2, 6)
            lo.upto(RKV + 10)

            def values_out(j):
                b, free = evac_ready(dve, RKV + 8 + j)
                dve.tensor_copy(vrw[:, :, j * CW:(j + 1) * CW], b[:, :].rearrange("p (a c) -> p a c", a=TT))\
                   .then_inc(free, 1)
            dve.wait_ge(S("key_factor"), 1)
            o(dve.tensor_tensor(keyT, keyT, scratch, ALU.mult))
            head_guard_dve(dve, 0, 1e-24, None, ALU.max, ALU.bypass)
            o.wait()
            values_out(0)
            head_inverse_dve(dve, 0)
            for k in range(KT):
                v = dve.scalar_tensor_tensor(out=scratch[:, k, :], in0=rT[:, k, :], scalar=col("r_k", k),
                                             in1=keyT[:, k, :], op0=ALU.mult, op1=ALU.mult)
            v.then_inc(S("bonus_rk"), 1)
            lo.upto(RKV + 11)
            head_scale_dve(dve, 0, kkT, 1.0)
            values_out(1)
            lo.upto(RKV + 12)
            dve.wait_ge(S("head_normed"), 4)
            o(dve.tensor_tensor(aT, aT, kkT, ALU.mult))
            dve.wait_ge(S("decays"), 1)
            dve.tensor_tensor(keyT, keyT, growth, ALU.mult).then_inc(S("wkv_in"), 1)
            o.wait()
            dve.tensor_tensor(aT, aT, growth, ALU.mult).then_inc(S("wkv_in"), 1)
            values_out(2)
            lo.upto(RKV + 13)
            dve.wait_ge(S("decays"), 2)
            dve.wait_ge(S("bonus_rk"), 1)
            dve.tensor_tensor(rT, rT, hf[:, :, :], ALU.mult).then_inc(S("wkv_in"), 1)
            dve.wait_ge(S("decays"), 3)
            dve.scalar_tensor_tensor(out=kkT, in0=kkT, scalar=-1.0, in1=sig, op0=ALU.mult, op1=ALU.mult)\
               .then_inc(S("wkv_in"), 1)
            values_out(3)
            dve.wait_ge(S("bonus_sum"), 1)
            dve.tensor_copy(bonus, bank[2][:, 0:2 * HEADS]).then_inc(S("bonus_read"), 1)
            wkv_dve(dve)
            dve.wait_ge(S("wkv_act"), act_event(len(PAIRS) - 1, STAGES - 1, 1))
            v3 = head_groups(bigs(5))
            dve.tensor_tensor(v3, v3, bonus.unsqueeze(2).to_broadcast([P, 2 * HEADS, DH]), ALU.mult)\
               .then_inc(S("bonus_v"), 1)
            y3 = head_groups(y_tok)
            o(dve.tensor_reduce(y_stat, y3, AXX, ALU.add))
            o.wait()
            o(dve.tensor_scalar(y_mean, y_stat, 1.0 / DH, None, ALU.mult))
            o.wait()
            dve.tensor_tensor(y3, y3, y_mean.unsqueeze(2).to_broadcast([P, 2 * HEADS, DH]), ALU.subtract)\
               .then_inc(S("y_centred"), 1)
            dve.wait_ge(S("y_square"), 1)
            o(dve.tensor_reduce(y_stat, head_groups(bigs(2)), AXX, ALU.add))
            o.wait()
            dve.tensor_scalar(y_stat, y_stat, 1.0 / DH, RWKV_EPS, ALU.mult, ALU.add).then_inc(S("y_ms"), 1)
            dve.wait_ge(S("y_root"), 1)
            o(dve.reciprocal(y_stat, y_stat))
            o.wait()
            dve.tensor_tensor(y3, y3, y_stat.unsqueeze(2).to_broadcast([P, 2 * HEADS, DH]), ALU.mult)\
               .then_inc(S("mix_normed"), 1)
            for kp in range(4):
                dve.wait_ge(S("y_affine"), kp + 1)
                part = scratch[:, 2 * kp:2 * kp + 2, :]
                o(dve.tensor_tensor(part, part, bank[kp][:, :].rearrange("p (a t) -> p a t", a=2), ALU.add))
                o.wait()
                dve.tensor_tensor(part, part, gate_fm[:, 2 * kp:2 * kp + 2, :], ALU.mult).then_inc(S("mix_scaled"), 1)
            dve.wait_ge(S("mix_out_hi"), 1)
            dve.tensor_tensor(hl[:, :, :], scratch, hh[:, :, :].bitcast(F32), ALU.subtract).then_inc(S("act_split"), 1)
            residual(dve, lo, BASE["rwkv_o"])

        def rwkv_pool(pool):
            norm_pool(pool, 3)

        KV, DQ = BASE["kv"], BASE["diff_q"]
        k_sh, v_sh, q_df = fm(bigs(0)), tm(bigs(1)), fm(bigs(2))
        k_squares, q_squares = fm(bigs(2)), fm(bigs(3))

        def head_out(act, n, values, squares, j):
            b, free = evac_ready(act, n)
            act.activation(values[:, 2 * j:2 * j + 2, :], b[:, :], ACT.Copy)
            act.activation(squares[:, 2 * j:2 * j + 2, :], b[:, :], ACT.Square).then_inc(S("head_squares"), 1)
            act.wait_ge(S("head_squares"), (4 if values is k_sh else 8) + j + 1)
            act.sem_inc(free, 1)

        def kv_pe(pe):
            norm_pe(pe, 5)
            pe.wait_ge(S("act_split"), SPLITS["norm5"])
            for j in range(8):
                project(pe, KV + j, hh, hl, "F" if j < 4 else "T")
                if j == 4:
                    head_sums_pe(pe, 1, k_squares)
                if j == 5:
                    head_spread_pe(pe, 1)
            pe.wait_ge(S("head_normed"), 8)

        def kv_act(act, hi):
            norm_act(act, 5, hi)
            for j in range(8):
                hi.upto(KV + j + 2)
                if j < 4:
                    head_out(act, KV + j, k_sh, k_squares, j)
                if j == 4:
                    head_root_act(act, 1)

        def kv_dve(dve, lo, o):
            norm_dve(dve, 5, lambda k: col("kv_norm", k))
            for j in range(8):
                lo.upto(KV + j + 2)
                if j >= 4:
                    b, free = evac_ready(dve, KV + j)
                    dve.tensor_copy(v_sh[:, :, (j - 4) * CW:(j - 3) * CW], b[:, :].rearrange("p (a c) -> p a c", a=TT))\
                       .then_inc(free, 1)
                if j == 4:
                    head_guard_dve(dve, 1, 1.0 / DH, EPS, ALU.mult, ALU.add)
                    head_inverse_dve(dve, 1)
                if j == 5:
                    head_scale_dve(dve, 1, k_sh, col("k_norm", 0))

        df_s = big[:, 4 * SLOTW:4 * SLOTW + 6 * 384].rearrange("p (b c n) -> p b c n", b=3, c=2)
        df_pT = big[:, 6 * SLOTW:6 * SLOTW + 2 * 384].rearrange("p (b n) -> p b n", b=2)
        df_junk = big[:, 5 * SLOTW + 512:5 * SLOTW + 512 + 2 * 2 * P].rearrange("p (b a n) -> p b a n", b=2, a=TT)
        o_tok = tm(bigs(7))
        q_gain, neg_lambda, subln_gain = small[:, 128:129], small[:, 129:130], small[:, 130:131]
        df_max, df_sum, df_inv = (small[:, 144 + 12 * i:156 + 12 * i].rearrange("p (b c a) -> p b c a", b=3, c=2)
                                  for i in range(3))
        df_coef = small[:, 180:186].rearrange("p (b a) -> p b a", b=3)
        o_ss = small[:, 192:208]
        lam_rows = aux[0:1, 0:4 * DH].rearrange("p (a b c) -> p a b c", a=2, b=2)
        lam_products = aux[0:1, 256:256 + 2 * DH].rearrange("p (a c) -> p a c", a=2)
        lam_exp, lam_row = aux[0:1, 384:386], aux[0:1, 386:387]
        distances = amask[:, :]

        def key_span(qt):
            return slice(P * qt, P * qt + P * (qt + 1))

        def distance_pool(pool):
            pool.wait_ge(S("x_ready"), XREADY[4])
            o = pool_order[0]
            for qt in range(TT):
                o(pool.iota(distances[:, key_span(qt)], pattern=[[1, P * (qt + 1)]], base=-P * qt, channel_multiplier=-1,
                            allow_small_or_imprecise_dtypes=True))
            o.wait()
            for c0 in (0, 2 * P):
                pool.affine_select(out=distances[:, c0:c0 + P], in_=distances[:, c0:c0 + P], compare_op=ALU.is_ge,
                                   fill=NEG, base=0, pattern=[[-1, P]], channel_multiplier=1)\
                    .then_inc(S("distances"), 1)

        def diff_pool(pool):
            norm_pool(pool, 7)

        def diff_pe(pe):
            norm_pe(pe, 7)
            pe.wait_ge(S("act_split"), SPLITS["norm7"])
            for n in range(DQ, DQ + 4):
                project(pe, n, hh, hl, "F")
            pe.wait_ge(S("lam_row"), 1)
            pe.matmul(bank[2][:, 0:1], ones[0:1, 0:P], lam_row, start=True, stop=True).then_inc(S("lam_column"), 1)
            head_sums_pe(pe, 2, q_squares)
            head_spread_pe(pe, 2)
            pe.wait_ge(S("lam_read"), 1)
            pe.wait_ge(S("head_normed"), 12)

            def scores(h):
                for c in range(2):
                    if h >= 1:
                        pe.wait_ge(S("df_masked"), 2 * h - 1 + c)
                    ch = slice(DH * c, DH * (c + 1))
                    for qt in range(TT):
                        mm = pe.matmul(bank[2 + c][:, key_span(qt)], q_df[ch, h, qt * P:(qt + 1) * P],
                                       k_sh[ch, h, 0:P * (qt + 1)], start=True, stop=True)
                    mm.then_inc(S("df_scores"), 1)

            def turn(h):
                pe.wait_ge(S("df_attn"), h + 1)
                if h >= 2:
                    pe.wait_ge(S("df_pT"), h - 1)
                for j in range(3):
                    mm = pe.transpose(bank[4 + h % 2][:, j * P:(j + 1) * P], df_s[:, h % 3, 0, j * P:(j + 1) * P],
                                      ident[:, :])
                mm.then_inc(S("df_turned"), 1)

            def values(h):
                pe.wait_ge(S("df_pT"), h + 1)
                if h >= 2:
                    pe.wait_ge(S("df_out"), h - 1)
                for qt, j, kt in ((0, 0, 0), (1, 1, 0), (1, 2, 1)):
                    mm = pe.matmul(bank[6 + h % 2][:, qt * P:(qt + 1) * P], df_pT[:, h % 2, j * P:(j + 1) * P],
                                   v_sh[:, kt, h * P:(h + 1) * P], start=(kt == 0), stop=(kt == qt))
                mm.then_inc(S("df_pv"), 1)
            for h in range(DIFF_HEADS + 3):
                if h < DIFF_HEADS:
                    scores(h)
                if 2 <= h <= DIFF_HEADS + 1:
                    turn(h - 2)
                if h >= 3:
                    values(h - 3)
            pe.wait_ge(S("mix_normed"), 2)
            for kp in range(4):
                for k in (2 * kp, 2 * kp + 1):
                    for tt in range(TT):
                        mm = pe.transpose(bank[4 + kp][:, (k % 2) * T + tt * P:(k % 2) * T + (tt + 1) * P],
                                          o_tok[:, tt, k * P:(k + 1) * P], ident[:, :])
                mm.then_inc(S("mix_turned"), 1)
            pe.wait_ge(S("act_split"), SPLITS["diff_y"])
            for n in range(BASE["diff_o"], BASE["diff_o"] + 4):
                project(pe, n, hh, hl, "T")

        def diff_act(act, hi):
            act.wait_ge(S("x_ready"), XREADY[4])
            act.dma_start(lam_rows, A["diff_lambda_2"].rearrange("o (a b) c -> o a b c", a=2)).then_inc(S("lam_loaded"), 16)
            norm_act(act, 7, hi)
            act.wait_ge(S("lam_sums"), 1)
            act.activation(lam_exp, lam_exp, ACT.Exp).then_inc(S("lam_exp"), 1)
            for j in range(4):
                hi.upto(DQ + j + 2)
                head_out(act, DQ + j, q_df, q_squares, j)
            head_root_act(act, 2)
            hi.upto(DQ + 6)

            def exps(h):
                for c in range(2):
                    act.wait_ge(S("df_max"), 2 * h + c + 1)
                    for qt in range(TT):
                        s = df_s[:, h % 3, c, key_span(qt)]
                        a = act.activation(s, s, ACT.Exp, bias=df_max[:, h % 3, c, qt:qt + 1],
                                           accum_out=df_sum[:, h % 3, c, qt:qt + 1])
                    a.then_inc(S("df_exp"), 1)

            def copy_out(h):
                act.wait_ge(S("df_turned"), h + 1)
                if h >= 2:
                    act.wait_ge(S("df_pv"), h - 1)
                act.activation(df_pT[:, h % 2, :], bank[4 + h % 2][:, 0:384], ACT.Copy).then_inc(S("df_pT"), 1)

            def outputs(h):
                act.wait_ge(S("df_pv"), h + 1)
                if h >= 2:
                    act.wait_ge(S("df_out"), h - 1)
                for qt in range(TT):
                    src, inv = bank[6 + h % 2][:, qt * P:(qt + 1) * P], df_inv[:, h % 3, 0, qt:qt + 1]
                    act.activation(o_tok[:, qt, h * P:(h + 1) * P], src, ACT.Copy, scale=inv)
                    a = act.activation(df_junk[:, h % 2, qt, :], src, ACT.Square, scale=inv,
                                       accum_out=o_ss[:, qt * DIFF_HEADS + h:qt * DIFF_HEADS + h + 1])
                a.then_inc(S("df_out"), 1)
            for h in range(DIFF_HEADS + 3):
                if h < DIFF_HEADS:
                    exps(h)
                if 2 <= h <= DIFF_HEADS + 1:
                    copy_out(h - 2)
                if h >= 3:
                    outputs(h - 3)
            act.wait_ge(S("o_ms"), 1)
            act.activation(o_ss, o_ss, ACT.Sqrt).then_inc(S("o_root"), 1)
            for kp in range(4):
                act.wait_ge(S("mix_scaled"), kp + 5)
                act.activation(hh[:, 2 * kp:2 * kp + 2, :], hf[:, 2 * kp:2 * kp + 2, :], ACT.Copy).then_inc(S("mix_out_hi"), 1)
            hi.upto(BASE["diff_o"] + 5)

        def diff_dve(dve, lo, o):
            o(dve.tensor_scalar(q_gain, col("q_norm", 0), DH ** -0.5, None, ALU.mult))
            o(dve.tensor_scalar(subln_gain, col("subln", 0), 1.0 - LAM_INIT, None, ALU.mult))
            dve.wait_ge(S("lam_loaded"), 16)
            o(dve.tensor_tensor(lam_products, lam_rows[:, :, 0, :], lam_rows[:, :, 1, :], ALU.mult))
            o.wait()
            dve.tensor_reduce(lam_exp, lam_products, AXX, ALU.add).then_inc(S("lam_sums"), 1)
            norm_dve(dve, 7, lambda k: col("mix1", k))
            dve.wait_ge(S("lam_exp"), 1)
            dve.scalar_tensor_tensor(out=lam_row, in0=lam_exp[:, 1:2], scalar=-LAM_INIT, in1=lam_exp[:, 0:1],
                                     op0=ALU.add, op1=ALU.subtract).then_inc(S("lam_row"), 1)
            for j in range(4):
                lo.upto(DQ + j + 2)
            dve.wait_ge(S("lam_column"), 1)
            dve.tensor_copy(neg_lambda, bank[2][:, 0:1]).then_inc(S("lam_read"), 1)
            head_guard_dve(dve, 2, 1.0 / DH, EPS, ALU.mult, ALU.add)
            head_inverse_dve(dve, 2)
            head_scale_dve(dve, 2, q_df, q_gain)
            lo.upto(DQ + 6)
            dve.wait_ge(S("distances"), 2)

            def mask_max(h):
                for c in range(2):
                    dve.wait_ge(S("df_scores"), 2 * h + c + 1)
                    if h >= 3:
                        dve.wait_ge(S("df_turned"), h - 2)
                    dve.scalar_tensor_tensor(out=df_s[:, h % 3, c, :], in0=distances, scalar=2.0 ** -(h + 1),
                                             in1=bank[2 + c][:, 0:384], op0=ALU.mult, op1=ALU.add)\
                       .then_inc(S("df_masked"), 1)
                for c in range(2):
                    dve.wait_ge(S("df_masked"), 2 * h + c + 1)
                    for qt in range(TT):
                        v = dve.tensor_reduce(df_max[:, h % 3, c, qt:qt + 1], df_s[:, h % 3, c, key_span(qt)], AXX,
                                              ALU.max, negate=True)
                    v.then_inc(S("df_max"), 1)

            def combine(h):
                dve.wait_ge(S("df_exp"), 2 * h + 2)
                if h >= 3:
                    dve.wait_ge(S("df_out"), h - 2)
                o(dve.reciprocal(df_inv[:, h % 3, :, :], df_sum[:, h % 3, :, :]))
                o.wait()
                o(dve.scalar_tensor_tensor(out=df_coef[:, h % 3, :], in0=df_sum[:, h % 3, 0, :], scalar=neg_lambda,
                                           in1=df_inv[:, h % 3, 1, :], op0=ALU.mult, op1=ALU.mult))
                o.wait()
                for qt in range(TT):
                    s0, s1 = (df_s[:, h % 3, c, key_span(qt)] for c in range(2))
                    v = dve.scalar_tensor_tensor(out=s0, in0=s1, scalar=df_coef[:, h % 3, qt:qt + 1], in1=s0,
                                                 op0=ALU.mult, op1=ALU.add)
                v.then_inc(S("df_attn"), 1)
            for h in range(DIFF_HEADS + 1):
                if h < DIFF_HEADS:
                    mask_max(h)
                if h >= 1:
                    combine(h - 1)
            dve.wait_ge(S("df_out"), DIFF_HEADS)
            dve.tensor_scalar(o_ss, o_ss, 1.0 / (2 * DH), SUBLN_EPS, ALU.mult, ALU.add).then_inc(S("o_ms"), 1)
            dve.wait_ge(S("o_root"), 1)
            o(dve.reciprocal(o_ss, o_ss))
            o.wait()
            o3 = bigs(7).rearrange("p (g c) -> p g c", c=2 * DH)
            dve.tensor_tensor(o3, o3, o_ss.unsqueeze(2).to_broadcast([P, TT * DIFF_HEADS, 2 * DH]), ALU.mult)\
               .then_inc(S("mix_normed"), 1)
            for kp in range(4):
                dve.wait_ge(S("mix_turned"), kp + 5)
                dve.tensor_scalar(hf[:, 2 * kp:2 * kp + 2, :], bank[4 + kp][:, :].rearrange("p (a t) -> p a t", a=2),
                                  subln_gain, None, ALU.mult).then_inc(S("mix_scaled"), 1)
            dve.wait_ge(S("mix_out_hi"), 5)
            dve.tensor_tensor(hl[:, :, :], hf[:, :, :], hh[:, :, :].bitcast(F32), ALU.subtract)\
               .then_inc(S("act_split"), 1)
            residual(dve, lo, BASE["diff_o"])

        block = ctx.enter_context(nc.Block())

        @block.sync
        def _(sp):
            for name, count in PHASES:
                if name.startswith("ffn"):
                    ffn_sp(sp, int(name[3]))
                else:
                    for n in range(BASE[name], BASE[name] + count):
                        load_slot(sp, n, n % WRING, slot_source(n))
            sp.wait_ge(S("x_ready"), 30)
            sp.dma_start(out[0].rearrange("(a p) d -> p a d", p=P), x[:, :, :]).then_inc(S("stored"), 16)
            sp.wait_ge(S("stored"), 16)

        @block.gpsimd
        def _(pool):
            setup_pool(pool)
            norm_pool(pool, 0)
            masks_pool(pool)
            peer_pool(pool)
            norm_pool(pool, 2)
            rwkv_pool(pool)
            norm_pool(pool, 4)
            norm_pool(pool, 5)
            distance_pool(pool)
            norm_pool(pool, 6)
            diff_pool(pool)
            norm_pool(pool, 8)

        @block.scalar
        def _(act):
            hi = HiStream(act)
            setup_act(act)
            hi.upto(1)
            for n in range(24):
                hi.upto(n + 2)
                if n == 0:
                    act.wait_ge(S("params"), N_PARAMS)
                    norm_squares(act, 0)
            block1_act(act, hi)
            peer_act(act, hi)
            lora_loads(act)
            ffn_act(act, 0, hi)
            rwkv_act(act, hi)
            ffn_act(act, 1, hi)
            kv_act(act, hi)
            ffn_act(act, 2, hi)
            diff_act(act, hi)
            ffn_act(act, 3, hi)

        @block.vector
        def _(dve):
            lo = LoStream(dve)
            o = setup_dve(dve, lo)
            block1_dve(dve, lo, o)
            peer_dve(dve, lo, o)
            ffn_dve(dve, 0, lo)
            rwkv_dve(dve, lo, o)
            ffn_dve(dve, 1, lo)
            kv_dve(dve, lo, o)
            ffn_dve(dve, 2, lo)
            diff_dve(dve, lo, o)
            ffn_dve(dve, 3, lo)

        @block.tensor
        def _(pe):
            setup_pe(pe)
            block1_pe(pe)
            peer_pe(pe)
            ffn_pe(pe, 0)
            rwkv_pe(pe)
            ffn_pe(pe, 1)
            kv_pe(pe)
            ffn_pe(pe, 2)
            diff_pe(pe)
            ffn_pe(pe, 3)


_INS = ["x", "c", "w_mod", "b_mod", "norm1_g", "w_in", "b_f", "w_pool", "pool_scale", "w_out", "norm2_g", "peer_w_query",
        "peer_sub_keys", "peer_u", "peer_v", "final_g", "ffn_norm_2", "ffn_w_in_2", "ffn_w_out_2", "mix_norm_2",
        "rwkv_mu_2", "rwkv_w_rkv_2", "rwkv_w0_2", "rwkv_w1_2", "rwkv_w2_2", "rwkv_a0_2", "rwkv_a1_2", "rwkv_a2_2",
        "rwkv_g1_2", "rwkv_g2_2", "rwkv_k_k_2", "rwkv_k_a_2", "rwkv_r_k_2", "rwkv_ln_g_2", "rwkv_ln_b_2",
        "rwkv_w_o_2", "kv_norm_2", "w_kv_2", "k_norm_2", "diff_w_q_2", "diff_q_norm_2", "diff_lambda_2",
        "diff_subln_2", "diff_w_o_2"]


def kernel(**inputs):
    import numpy as np
    import concourse.bacc as bacc
    from concourse.bass_utils import run_bass_kernel_spmd

    nc = bacc.Bacc("TRN2", target_bir_lowering=False, num_devices=1)
    arrays, aps = {}, {}
    for name in _INS:
        a = np.ascontiguousarray(inputs[name])
        arrays[f"in_{name}"] = a
        aps[name] = nc.dram_tensor(f"in_{name}", a.shape, mybir.dt.from_np(a.dtype), kind="ExternalInput").ap()
    out = nc.dram_tensor("out", (1, T, D), F32, kind="ExternalOutput").ap()
    build_program(nc, aps, out)
    return run_bass_kernel_spmd(nc, [arrays], core_ids=[0]).results[0]["out"]
```
